# Optimizing a Trainium2 kernel written in Bass

```python
import math
import jax, jax.numpy as jnp
from jax import lax
import numpy as np

D_MODEL = 1024
BATCH = 1
SEQ = 512
DEPTH = 1

N_HEADS = 8
HEAD_DIM = 64
V_DIM = 2 * HEAD_DIM
QK_WIDTH = N_HEADS * 2 * HEAD_DIM
ATTN_WIDTH = N_HEADS * V_DIM
Q_BLOCK = 128
SSM_WIDTH = D_MODEL // 2
SSM_GROUP = 16
SSM_GROUPS = SSM_WIDTH // SSM_GROUP
SSM_STATE = 64
DT_MIN = 1e-3
DT_MAX = 1e-1
D_FF = 4 * D_MODEL
N_BUCKETS = 32
MAX_DISTANCE = 128
EPS = 1e-6
IN_WIDTH = 2 * QK_WIDTH + ATTN_WIDTH + SSM_WIDTH + 2 * D_MODEL
SPLITS = [QK_WIDTH, 2 * QK_WIDTH, 2 * QK_WIDTH + ATTN_WIDTH,
          2 * QK_WIDTH + ATTN_WIDTH + SSM_WIDTH,
          2 * QK_WIDTH + ATTN_WIDTH + SSM_WIDTH + D_MODEL]

kernel_name = 'hybrid_diffattn_s5_gated_block'

def rmsnorm(x, g):
    xf = x.astype(jnp.float32)
    y = xf * lax.rsqrt(jnp.mean(xf * xf, axis=-1, keepdims=True) + EPS)
    return (y * g.astype(jnp.float32)).astype(x.dtype)

def lambda_init_fn(layer):
    return 0.8 - 0.6 * math.exp(-0.3 * layer)

def t5_bucket(rel):
    n = jnp.maximum(rel, 0)
    max_exact = N_BUCKETS // 2
    is_small = n < max_exact
    large = max_exact + (jnp.log(jnp.maximum(n, 1).astype(jnp.float32) / max_exact)
                         / math.log(MAX_DISTANCE / max_exact)
                         * (N_BUCKETS - max_exact)).astype(jnp.int32)
    large = jnp.minimum(large, N_BUCKETS - 1)
    return jnp.where(is_small, n, large)

def diff_attention(q, k, v, rel_bias, lam, subln_g, lam_init):
    b, l = q.shape[0], q.shape[1]
    nb = l // Q_BLOCK
    q = q.reshape(b, l, N_HEADS, 2, HEAD_DIM).transpose(0, 2, 3, 1, 4)
    k = k.reshape(b, l, N_HEADS, 2, HEAD_DIM).transpose(0, 2, 3, 1, 4)
    v = v.reshape(b, l, N_HEADS, V_DIM).transpose(0, 2, 1, 3)
    q_blocks = q.reshape(b, N_HEADS, 2, nb, Q_BLOCK, HEAD_DIM).transpose(3, 0, 1, 2, 4, 5)
    k_pos = jnp.arange(l)
    scale = HEAD_DIM ** -0.5

    def one_block(args):
        q_blk, i = args
        q_pos = i * Q_BLOCK + jnp.arange(Q_BLOCK)
        rel = q_pos[:, None] - k_pos[None, :]
        bias = rel_bias[t5_bucket(rel)].astype(jnp.float32).transpose(2, 0, 1)
        s = jnp.einsum('bhmqd,bhmkd->bhmqk', q_blk, k).astype(jnp.float32) * scale
        s = s + bias[None, :, None]
        s = jnp.where((rel >= 0)[None, None, None], s, -jnp.inf)
        p = jax.nn.softmax(s, axis=-1)
        w = p[:, :, 0] - lam * p[:, :, 1]
        return jnp.einsum('bhqk,bhkv->bhqv', w.astype(v.dtype), v)

    o = lax.map(one_block, (q_blocks, jnp.arange(nb)))
    o = o.transpose(1, 0, 3, 2, 4).reshape(b, l, N_HEADS, V_DIM)
    o = rmsnorm(o, subln_g) * (1.0 - lam_init)
    return o.reshape(b, l, ATTN_WIDTH)

def _complex_affine_combine(e1, e2):
    a1r, a1i, b1r, b1i = e1
    a2r, a2i, b2r, b2i = e2
    ar = a2r * a1r - a2i * a1i
    ai = a2r * a1i + a2i * a1r
    br = a2r * b1r - a2i * b1i + b2r
    bi = a2r * b1i + a2i * b1r + b2i
    return (ar, ai, br, bi)

def s5_ssm(u, a_re, a_im, log_dt, b_re, b_im, c_re, c_im, d_skip):
    bsz, l = u.shape[0], u.shape[1]
    uf = u.astype(jnp.float32).reshape(bsz, l, SSM_GROUPS, SSM_GROUP)
    dt = jnp.exp(log_dt.astype(jnp.float32))[:, None]
    ar = a_re.astype(jnp.float32)
    ai = a_im.astype(jnp.float32)
    mag = jnp.exp(ar * dt)
    lb_re = mag * jnp.cos(ai * dt)
    lb_im = mag * jnp.sin(ai * dt)
    nr = lb_re - 1.0
    ni = lb_im
    den = ar * ar + ai * ai
    cr = ((nr * ar + ni * ai) / den)[..., None]
    ci = ((ni * ar - nr * ai) / den)[..., None]
    br = b_re.astype(jnp.float32)
    bi = b_im.astype(jnp.float32)
    bb_re = cr * br - ci * bi
    bb_im = cr * bi + ci * br
    bu_re = jnp.einsum('blgh,gph->blgp', uf, bb_re)
    bu_im = jnp.einsum('blgh,gph->blgp', uf, bb_im)
    lam_re = jnp.broadcast_to(lb_re, bu_re.shape)
    lam_im = jnp.broadcast_to(lb_im, bu_im.shape)
    _, _, s_re, s_im = lax.associative_scan(
        _complex_affine_combine, (lam_re, lam_im, bu_re, bu_im), axis=1)
    y = (jnp.einsum('blgp,ghp->blgh', s_re, c_re.astype(jnp.float32))
         - jnp.einsum('blgp,ghp->blgh', s_im, c_im.astype(jnp.float32))
         + d_skip.astype(jnp.float32).reshape(SSM_GROUPS, SSM_GROUP) * uf)
    return y.reshape(bsz, l, SSM_WIDTH).astype(u.dtype)

def setup_inputs(seed: int = 0) -> dict:
    key = jax.random.key(seed)
    ks = jax.random.split(key, 24)
    f32 = jnp.float32
    nrm = lambda k, shape, s: jax.random.normal(k, shape, f32) * s
    n_idx = jnp.arange(SSM_STATE, dtype=f32)
    a_re = -0.5 + nrm(ks[9], (DEPTH, SSM_GROUPS, SSM_STATE), 0.01)
    a_im = math.pi * n_idx[None, None, :] + nrm(ks[10], (DEPTH, SSM_GROUPS, SSM_STATE), 0.01)
    log_dt = jax.random.uniform(ks[11], (DEPTH, SSM_GROUPS), f32,
                                math.log(DT_MIN), math.log(DT_MAX))
    b_scale = (0.5 / SSM_GROUP) ** 0.5
    c_scale = (0.5 / SSM_STATE) ** 0.5
    return {
        'x': jax.random.normal(ks[0], (BATCH, SEQ, D_MODEL), f32),
        'g_mix': 1.0 + nrm(ks[1], (DEPTH, D_MODEL), 0.02),
        'w_in': nrm(ks[2], (DEPTH, D_MODEL, IN_WIDTH), D_MODEL ** -0.5),
        'lambda_q1': nrm(ks[3], (DEPTH, HEAD_DIM), 0.1),
        'lambda_k1': nrm(ks[4], (DEPTH, HEAD_DIM), 0.1),
        'lambda_q2': nrm(ks[5], (DEPTH, HEAD_DIM), 0.1),
        'lambda_k2': nrm(ks[6], (DEPTH, HEAD_DIM), 0.1),
        'subln_g': 1.0 + nrm(ks[7], (DEPTH, V_DIM), 0.02),
        'rel_bias': nrm(ks[8], (N_BUCKETS, N_HEADS), 0.5),
        'ssm_a_re': a_re,
        'ssm_a_im': a_im,
        'ssm_log_dt': log_dt,
        'ssm_b_re': nrm(ks[12], (DEPTH, SSM_GROUPS, SSM_STATE, SSM_GROUP), b_scale),
        'ssm_b_im': nrm(ks[13], (DEPTH, SSM_GROUPS, SSM_STATE, SSM_GROUP), b_scale),
        'ssm_c_re': nrm(ks[14], (DEPTH, SSM_GROUPS, SSM_GROUP, SSM_STATE), c_scale),
        'ssm_c_im': nrm(ks[15], (DEPTH, SSM_GROUPS, SSM_GROUP, SSM_STATE), c_scale),
        'ssm_d': nrm(ks[16], (DEPTH, SSM_WIDTH), 1.0),
        'w_glu': nrm(ks[17], (DEPTH, SSM_WIDTH, 2 * D_MODEL), SSM_WIDTH ** -0.5),
        'w_out': nrm(ks[18], (DEPTH, D_MODEL, D_MODEL), D_MODEL ** -0.5),
        'g_mlp': 1.0 + nrm(ks[19], (DEPTH, D_MODEL), 0.02),
        'w1': nrm(ks[20], (DEPTH, D_MODEL, D_FF), D_MODEL ** -0.5),
        'w2': nrm(ks[21], (DEPTH, D_FF, D_MODEL), D_FF ** -0.5),
        'g_final': 1.0 + nrm(ks[22], (D_MODEL,), 0.02),
    }

def reference(x, g_mix, w_in, lambda_q1, lambda_k1, lambda_q2, lambda_k2, subln_g,
              rel_bias, ssm_a_re, ssm_a_im, ssm_log_dt, ssm_b_re, ssm_b_im,
              ssm_c_re, ssm_c_im, ssm_d, w_glu, w_out, g_mlp, w1, w2, g_final):
    for layer in range(DEPTH):
        h = rmsnorm(x, g_mix[layer])
        proj = h @ w_in[layer]
        q, k, v, u, gate_a, gate_s = jnp.split(proj, SPLITS, axis=-1)
        lam_init = lambda_init_fn(layer)
        lam = (jnp.exp(jnp.sum(lambda_q1[layer].astype(jnp.float32) * lambda_k1[layer].astype(jnp.float32)))
               - jnp.exp(jnp.sum(lambda_q2[layer].astype(jnp.float32) * lambda_k2[layer].astype(jnp.float32)))
               + lam_init)
        attn = diff_attention(q, k, v, rel_bias, lam, subln_g[layer], lam_init)
        y = s5_ssm(u, ssm_a_re[layer], ssm_a_im[layer], ssm_log_dt[layer],
                   ssm_b_re[layer], ssm_b_im[layer], ssm_c_re[layer], ssm_c_im[layer],
                   ssm_d[layer])
        z = jax.nn.gelu(y) @ w_glu[layer]
        z_val, z_gate = jnp.split(z, 2, axis=-1)
        ssm = z_val * jax.nn.sigmoid(z_gate)
        mixed = jax.nn.sigmoid(gate_a) * attn + jax.nn.sigmoid(gate_s) * ssm
        x = x + mixed @ w_out[layer]
        h = rmsnorm(x, g_mlp[layer])
        x = x + jnp.square(jax.nn.relu(h @ w1[layer])) @ w2[layer]
    return rmsnorm(x, g_final)


_drawn_inputs = setup_inputs


def setup_inputs(seed=0):
    import zlib

    import numpy as np

    out = dict(_drawn_inputs(seed))
    spreads = {}
    factors = {'g_mix': 3.236,
     'lambda_q1': 4.753,
     'lambda_k1': 3.451,
     'lambda_q2': 64.0,
     'subln_g': 6.199,
     'ssm_a_re': 64.0,
     'ssm_a_im': 41.16,
     'ssm_log_dt': 42.32,
     'ssm_b_re': 58.2,
     'ssm_b_im': 59.416,
     'ssm_c_re': 58.232,
     'ssm_c_im': 57.76,
     'g_mlp': 3.324,
     'g_final': 7.929}
    for name, (base, spread) in spreads.items():
        noise = np.random.default_rng([zlib.crc32(name.encode()), seed]).standard_normal(out[name].shape)
        drawn = base * np.exp(spread * noise) if base else spread * noise
        out[name] = __import__('jax').numpy.asarray(drawn.astype(out[name].dtype))
    for name, factor in factors.items():
        out[name] = (out[name] * factor).astype(out[name].dtype)
    return out
```

```python
import math
from contextlib import ExitStack

import numpy as np

import concourse.bass as bass
from concourse import mybir
from concourse.alu_op_type import AluOpType as ALU

ACT = mybir.ActivationFunctionType
F32 = mybir.dt.float32
F32R = mybir.dt.float32r

P = 128
SEQ, D_MODEL = 512, 1024
N_HEADS, HEAD_DIM, V_DIM = 8, 64, 128
SSM_WIDTH, SSM_GROUP, SSM_GROUPS, SSM_STATE = 512, 16, 32, 64
D_FF = 4096
N_BUCKETS, MAX_DISTANCE = 32, 128
EPS = 1e-6
LAM_INIT = 0.8 - 0.6 * math.exp(-0.3 * 0)
MASKED = -1e30

TOK = SEQ // P
KT = D_MODEL // P
UT = SSM_WIDTH // P
PAIRS = SSM_GROUPS // 2
HALF = SEQ // 2
BIAS_W = 640
BLOCKS = N_HEADS * TOK

RING = 4
U_SSM, U_V, U_GA, U_QK, U_GS, U_GLU, U_OUT, U_MLP = 0, 4, 12, 20, 36, 44, 52, 60
N_UNITS = U_MLP + 64
COL_Q, COL_K, COL_V, COL_U, COL_GA, COL_GS = 0, 1024, 2048, 3072, 3584, 4608

B_SCORE, B_WT, B_O, B_QK, B_Y, B_BU, B_T = 0, 2, 3, 4, 5, 6, 4


def bucket_onehot():
    rel = SEQ - 1 - np.arange(BIAS_W)
    n = np.maximum(rel, 0)
    exact = N_BUCKETS // 2
    large = exact + (np.log(np.maximum(n, 1).astype(np.float32) / np.float32(exact)).astype(np.float32)
                     / np.float32(math.log(MAX_DISTANCE / exact)) * np.float32(N_BUCKETS - exact)).astype(np.int32)
    bucket = np.where(n < exact, n, np.minimum(large, N_BUCKETS - 1))
    return ((bucket[None, :] == np.arange(N_BUCKETS)[:, None]) & (rel >= 0)[None, :]).astype(np.float32)


def build(nc, x, g_mix, w_in, lambda_q1, lambda_k1, lambda_q2, lambda_k2, subln_g, rel_bias,
          ssm_a_re, ssm_a_im, ssm_log_dt, ssm_b_re, ssm_b_im, ssm_c_re, ssm_c_im, ssm_d,
          w_glu, w_out, g_mlp, w1, w2, g_final, onehot, out):
    ctx = ExitStack()
    base = (nc.sbuf_base + 63) // 64 * 64
    at = {"next": base}

    def sb(name, shape, dt=F32, offset=None):
        size = 4 * int(np.prod(shape[1:]))
        if offset is None:
            offset = at["next"]
            at["next"] += (size + 31) // 32 * 32
        at[name] = offset
        return nc.alloc_sbuf_tensor_at(name, list(shape), dt, offset=offset)

    def sem(name):
        return ctx.enter_context(nc.semaphore(name))

    ident = sb("ident", [P, P])
    hT_hi = sb("hT_hi", [P, KT, SEQ], F32R)
    hT_lo = sb("hT_lo", [P, KT, SEQ], F32R)
    raw = sb("raw", [P, RING, 1024])
    w_hi = sb("w_hi", [P, RING, 1024], F32R)
    w_lo = sb("w_lo", [P, RING, 1024], F32R)
    mixA = sb("mixA", [P, TOK, D_MODEL])
    V = sb("V", [P, TOK, D_MODEL])
    uT = sb("uT", [P, UT, SEQ])
    E_re = sb("E_re", [P, PAIRS, HALF])
    BT = sb("BT", [P, 2, 2, UT, P])
    CT = sb("CT", [P, PAIRS, 2, 2, 32])
    E_im = sb("E_im", [P, PAIRS, HALF])
    rt = sb("rt", [P, 4, SEQ])
    st = sb("st", [P, 2, SEQ])
    qT = sb("qT", [P, 2, SEQ])
    kT = sb("kT", [P, 2, SEQ])
    bias = sb("bias", [P, 2, SEQ])
    Pm = sb("Pm", [P, 2, 2, SEQ])
    wT = sb("wT", [P, 2, SEQ])
    mag = sb("mag", [P, 5, PAIRS])
    coef = sb("coef", [P, 2, 2, PAIRS])
    pw = sb("pw", [P, 2, 2, PAIRS])
    pwt = sb("pwt", [P, 4, PAIRS])
    cols = sb("cols", [P, 2 * KT + UT])
    gsub = sb("gsub", [P, V_DIM])
    ssq = sb("ssq", [P, TOK, N_HEADS])
    rsub = sb("rsub", [P, TOK, N_HEADS])
    ms = sb("ms", [P, 3, TOK])
    rstd = sb("rstd", [P, 3, TOK])
    mx = sb("mx", [P, 2, 2])
    nmx = sb("nmx", [P, 2, 2])
    sums = sb("sums", [P, 2, 2])
    rinv = sb("rinv", [P, 8, 2])
    cfac = sb("cfac", [P, 2, 1])
    nlam = sb("nlam", [P, 4])
    osq = sb("osq", [P, V_DIM])
    eps_t = sb("eps_t", [P, 1])
    halfpi = sb("halfpi", [P, 1])
    assert at["next"] <= nc.sbuf_usable_end, (at["next"], nc.sbuf_usable_end)
    pt = at["qT"]
    prm = sb("prm", [PAIRS, 20, P], offset=pt)
    b_nat = sb("b_nat", [P, 2, PAIRS, SSM_GROUP], offset=pt + 10240)
    c_nat = sb("c_nat", [P, 2, UT, 2, SSM_STATE], offset=pt + 12288)
    c_pk = sb("c_pk", [P, 2, PAIRS, SSM_GROUP], offset=pt + 16384)
    oneh = sb("oneh", [N_BUCKETS, BIAS_W], offset=pt + 18432)
    frow = sb("frow", [N_HEADS, BIAS_W], offset=pt + 20992)
    lamv = sb("lamv", [P, 2, 2, HEAD_DIM], offset=at["rt"] + 11264)
    cols_nat = sb("cols_nat", [2 * KT + UT, P], offset=pt + 23552)
    bb = sb("bb", [P, 2, PAIRS, 32], offset=at["rt"])
    bt = sb("bt", [P, 4, PAIRS, SSM_GROUP], offset=at["rt"] + 4096)
    rb = sb("rb", [N_BUCKETS, N_HEADS], offset=at["rt"] + 8192)
    dtt = sb("dtt", [PAIRS, 2, 2], offset=at["rt"] + 8256)
    em = sb("em", [P, 2, PAIRS, HALF // 2], offset=at["mixA"])
    mixS = sb("mixS", [P, TOK, D_MODEL], offset=at["V"])
    gT_hi = sb("gT_hi", [P, UT, SEQ], F32R, offset=at["E_re"])
    gT_lo = sb("gT_lo", [P, UT, SEQ], F32R, offset=at["E_re"] + 8192)
    zt = sb("zt", [P, 2, SEQ], offset=at["qT"])
    junk = sb("junk", [P, D_MODEL], offset=at["Pm"])
    x2 = sb("x2", [P, TOK, D_MODEL], offset=at["E_im"])
    xn2 = sb("xn2", [P, TOK, D_MODEL], offset=at["mixA"])
    fT_hi = sb("fT_hi", [P, 2, KT, SEQ], F32R, offset=at["mixA"])
    fT_lo = sb("fT_lo", [P, 2, KT, SEQ], F32R, offset=at["mixA"] + 32768)
    fr = sb("fr", [P, 2, SEQ], offset=at["rt"])
    fs = sb("fs", [P, 2, SEQ], offset=at["rt"] + 4096)
    gfin = sb("gfin", [P, D_MODEL], offset=at["kT"])
    assert at["fT_lo"] + 32768 <= at["E_im"]
    ps = ctx.enter_context(nc.psum_tensor("ps", [P, 8, 512], F32))
    g1_col, g2_col, d_col = cols[:, 0:KT], cols[:, KT:2 * KT], cols[:, 2 * KT:2 * KT + UT]
    frow_dram = nc.dram_tensor("frow_dram", [N_HEADS, P, BIAS_W], F32, kind="Internal").ap()

    x_in = sem("x_in"); x_again = sem("x_again"); out_stored = sem("out_stored")
    consts_in = sem("consts_in"); prm_in = sem("prm_in"); gfin_in = sem("gfin_in")
    frow_out = sem("frow_out"); frow_done = sem("frow_done"); frow_mm = sem("frow_mm")
    bias_in = [sem(f"bias_in{i}") for i in range(2)]
    raw_in = [sem(f"raw_in{i}") for i in range(RING)]
    w_hi_done = sem("w_hi_done"); w_lo_done = sem("w_lo_done"); unit_used = sem("unit_used")
    ident_set = sem("ident_set"); tiles_set = sem("tiles_set")
    x_sq = sem("x_sq"); x_rt = sem("x_rt"); x_rstd = sem("x_rstd"); x_scaled = sem("x_scaled")
    turned = sem("turned"); hT_hi_done = sem("hT_hi_done"); hT_lo_done = sem("hT_lo_done")
    u_copied = sem("u_copied")
    nat_ready = sem("nat_ready"); nat_copied = sem("nat_copied"); nat_added = sem("nat_added")
    gates_done = sem("gates_done"); zt_used = sem("zt_used")
    cols_turned = sem("cols_turned"); cols_copied = sem("cols_copied")
    prep = sem("prep"); lam_dots = sem("lam_dots"); args_ready = sem("args_ready"); prm_ready = sem("prm_ready"); prm_copied = sem("prm_copied"); prep_act = sem("prep_act"); prm_turned = sem("prm_turned")
    table = sem("table"); bb_ready = sem("bb_ready"); bb_turned = sem("bb_turned")
    BT_ready = sem("BT_ready"); c_turned = sem("c_turned"); c_packed = sem("c_packed")
    bu_ready = sem("bu_ready"); bu_read = sem("bu_read"); ssm_step = sem("ssm_step")
    y_ready = sem("y_ready"); y_done = sem("y_done"); gelu_done = sem("gelu_done")
    gT_hi_done = sem("gT_hi_done"); gT_lo_done = sem("gT_lo_done")
    qk_copied = sem("qk_copied")
    score_ready = sem("score_ready"); score_read = sem("score_read"); nmax_ready = sem("nmax_ready")
    exp_done = sem("exp_done"); att_step = sem("att_step"); wT_ready = sem("wT_ready")
    wT_copied = sem("wT_copied"); pv_done = sem("pv_done"); o_squared = sem("o_squared")
    o_gated = sem("o_gated"); rsub_step = sem("rsub_step"); mixed_done = sem("mixed_done")
    f_relu = sem("f_relu"); f_hi_done = sem("f_hi_done")
    f_sq = sem("f_sq"); f_lo_done = sem("f_lo_done"); out_ready = sem("out_ready")

    NAT_OUT, NAT_END = 2 * TOK, 12 * TOK

    block = ctx.enter_context(nc.Block())

    def col_unit(w, c0):
        return w[:, c0:c0 + P].rearrange("(k p) n -> p k n", p=P)

    def row_unit(w, r0, c0):
        return w[r0:r0 + 2 * P, c0:c0 + 512].rearrange("(k p) n -> p k n", p=P)

    def unit_source(u):
        if u < U_V:
            return col_unit(w_in, COL_U + P * u)
        if u < U_GA:
            return row_unit(w_in, 256 * ((u - U_V) % 4), COL_V + 512 * ((u - U_V) // 4))
        if u < U_QK:
            return row_unit(w_in, 256 * ((u - U_GA) % 4), COL_GA + 512 * ((u - U_GA) // 4))
        if u < U_GS:
            return col_unit(w_in, ((u - U_QK) % 2) * COL_K + P * ((u - U_QK) // 2))
        if u < U_GLU:
            return row_unit(w_in, 256 * ((u - U_GS) % 4), COL_GS + 512 * ((u - U_GS) // 4))
        if u < U_OUT:
            c = (u - U_GLU) // 2
            return row_unit(w_glu, 256 * ((u - U_GLU) % 2), (1 - c % 2) * D_MODEL + 512 * (c // 2))
        if u < U_MLP:
            return row_unit(w_out, 256 * ((u - U_OUT) % 4), 512 * ((u - U_OUT) // 4))
        kind, quarter = MLP_ORDER[(u - U_MLP) // 8]
        n = (u - U_MLP) % 8
        if kind == "up":
            return col_unit(w1, 1024 * quarter + P * n)
        return row_unit(w2, 1024 * quarter + 256 * (n % 4), 512 * (n // 4))

    MLP_ORDER = [("up", 0), ("up", 1), ("down", 0), ("up", 2), ("down", 1), ("up", 3), ("down", 2), ("down", 3)]

    def last_unit(c):
        if c < 2:
            return U_V + 4 * c + 3
        if c < 4:
            return U_GA + 4 * (c - 2) + 3
        if c < 6:
            return U_GS + 4 * (c - 4) + 3
        if c < 10:
            return U_GLU + 2 * (c - 6) + 1
        if c < 12:
            return U_OUT + 4 * (c - 10) + 3
        step = MLP_ORDER.index(("down", (c - 12) // 2))
        return U_MLP + 8 * step + 4 * ((c - 12) % 2) + 3

    def wait_rows(eng, c, t):
        if t < TOK - 1:
            eng.wait_ge(nat_ready, (TOK - 1) * c + t + 1)
        else:
            eng.wait_ge(unit_used, last_unit(c) + 1)

    @block.sync
    def _(sp):
        for t in range(TOK):
            sp.dma_start(mixA[:, t, :], x[0, P * t:P * t + P, :]).then_inc(x_in, 16)

        def load_raw(u):
            if u >= RING:
                sp.wait_ge(w_lo_done, u - RING + 1)
            dst = raw[:, u % RING, :]
            src = unit_source(u)
            sp.dma_start(dst.rearrange("p (k n) -> p k n", k=src.shape[1]), src).then_inc(raw_in[u % RING], 16)

        def load_bias(h):
            if h >= 2:
                sp.wait_ge(score_read, 2 * TOK * (h - 1))
            else:
                sp.wait_ge(BT_ready, 4)
                sp.wait_ge(c_packed, 4)
                sp.wait_ge(table, 1)
                sp.wait_ge(frow_done, 16)
            src = bass.AP(frow_dram.tensor, h * P * BIAS_W + P - 1, [[BIAS_W - 1, P], [1, SEQ]])
            sp.dma_start(bias[:, h % 2, :], src).then_inc(bias_in[h % 2], 16)

        for u in range(N_UNITS):
            load_raw(u)
            if u == U_GA + 4:
                load_bias(0)
                load_bias(1)
            if U_QK + 6 <= u < U_QK + 6 + 2 * (N_HEADS - 2) and u % 2 == 0:
                load_bias((u - U_QK - 6) // 2 + 2)
            if u == U_OUT:
                sp.wait_ge(y_done, UT)
                for t in range(TOK):
                    sp.dma_start(x2[:, t, :], x[0, P * t:P * t + P, :]).then_inc(x_again, 16)
                sp.wait_ge(score_read, 2 * BLOCKS)
                sp.dma_start(gfin[:, :], bass.AP(g_final.tensor, 0, [[0, P], [1, D_MODEL]])).then_inc(gfin_in, 16)
        for t in range(TOK):
            sp.wait_ge(out_ready, t + 1)
            sp.dma_start(out[0, P * t:P * t + P, :], x2[:, t, :]).then_inc(out_stored, 16)
        sp.wait_ge(out_stored, 16 * TOK)

    N_PRM, N_CONST = 3, 16

    @block.gpsimd
    def _(pool):
        nc.gpsimd.memset(ident[:, :], 0.0).then_inc(ident_set, 1)
        nc.gpsimd.memset(eps_t[:, :], EPS).then_inc(tiles_set, 1)
        nc.gpsimd.memset(halfpi[:, :], math.pi / 2).then_inc(tiles_set, 1)
        pool.wait_ge(ident_set, 1)
        nc.gpsimd.affine_select(out=ident[:, :], in_=ident[:, :], compare_op=ALU.not_equal, fill=1.0,
                                base=0, pattern=[[-1, P]], channel_multiplier=1).then_inc(ident_set, 1)
        nc.gpsimd.memset(bb[:, :, :, :], 0.0).then_inc(tiles_set, 1)
        nc.gpsimd.memset(CT[:, :, :, :, :], 0.0).then_inc(tiles_set, 1)
        nc.gpsimd.memset(E_re[:, :, 0:1], 1.0).then_inc(tiles_set, 1)
        nc.gpsimd.memset(E_im[:, :, 0:1], 0.0).then_inc(tiles_set, 1)
        for u in range(N_UNITS):
            pool.wait_ge(w_hi_done, u + 1)
            nc.gpsimd.tensor_tensor(w_lo[:, u % RING, :], raw[:, u % RING, :],
                                    w_hi[:, u % RING, :].bitcast(F32), ALU.subtract).then_inc(w_lo_done, 1)

    @block.scalar
    def _(act):
        def col(src):
            return src.rearrange("(k p) -> k p", p=P)

        for src, dst in ((ssm_log_dt[0].rearrange("(i two) -> i two", two=2), dtt[:, 0, :]),
                         (ssm_a_re[0].rearrange("(i two) s -> i (two s)", two=2), prm[:, 0, :]),
                         (ssm_a_im[0].rearrange("(i two) s -> i (two s)", two=2), prm[:, 1, :])):
            act.dma_start(dst, src).then_inc(prm_in, 16)
        for src, dst in ((col(g_mix[0]), cols_nat[0:KT, :]), (col(g_mlp[0]), cols_nat[KT:2 * KT, :]),
                         (col(ssm_d[0]), cols_nat[2 * KT:, :]),
                         (bass.AP(subln_g.tensor, 0, [[0, P], [1, V_DIM]]), gsub[:, :]),
                         (bass.AP(lambda_q1.tensor, 0, [[0, P], [1, HEAD_DIM]]), lamv[:, 0, 0, :]),
                         (bass.AP(lambda_k1.tensor, 0, [[0, P], [1, HEAD_DIM]]), lamv[:, 0, 1, :]),
                         (bass.AP(lambda_q2.tensor, 0, [[0, P], [1, HEAD_DIM]]), lamv[:, 1, 0, :]),
                         (bass.AP(lambda_k2.tensor, 0, [[0, P], [1, HEAD_DIM]]), lamv[:, 1, 1, :]),
                         (rel_bias, rb[:, :]), (onehot, oneh[:, :]),
                         (ssm_b_re[0].rearrange("(i two) s h -> (two s) i h", two=2), b_nat[:, 0, :, :]),
                         (ssm_b_im[0].rearrange("(i two) s h -> (two s) i h", two=2), b_nat[:, 1, :, :]),
                         (ssm_c_re[0].rearrange("(t g) h s -> (g h) t s", g=8), c_nat[:, 0, :, 0, :]),
                         (ssm_c_re[0].rearrange("(t g) h s -> (g h) t s", g=8), c_nat[:, 0, :, 1, :]),
                         (ssm_c_im[0].rearrange("(t g) h s -> (g h) t s", g=8), c_nat[:, 1, :, 0, :]),
                         (ssm_c_im[0].rearrange("(t g) h s -> (g h) t s", g=8), c_nat[:, 1, :, 1, :])):
            act.dma_start(dst, src).then_inc(consts_in, 16)

        def split_hi(u):
            if u >= N_UNITS:
                return
            act.wait_ge(raw_in[u % RING], 16 * (u // RING + 1))
            if u >= RING:
                act.wait_ge(unit_used, u - RING + 1)
            nc.scalar.activation(w_hi[:, u % RING, :], raw[:, u % RING, :], ACT.Identity).then_inc(w_hi_done, 1)

        def row_stats(g, t, src):
            nc.scalar.activation(junk[:, :], src, ACT.Square, accum_out=ms[:, g, t:t + 1]).then_inc(x_sq, 1)

        def row_root(g):
            act.wait_ge(x_sq, TOK * (g + 1))
            act.wait_ge(tiles_set, 2)
            nc.scalar.activation(ms[:, g, :], ms[:, g, :], ACT.Sqrt, bias=eps_t[:, :],
                                 scale=1.0 / D_MODEL).then_inc(x_rt, 1)

        def turn_hi(g, k, gain):
            act.wait_ge(turned, KT * g + k + 1)
            kw = {} if gain is None else {"scale": gain[:, k:k + 1]}
            nc.scalar.activation(hT_hi[:, k, :], ps[:, B_T + k % 4, :], ACT.Identity, **kw).then_inc(hT_hi_done, 1)

        for t in range(TOK):
            if t == 0:
                act.wait_ge(x_in, 16 * TOK)
            else:
                act.wait_ge(x_sq, t)
            nc.scalar.activation(V[:, 0, :], mixA[:, t, :], ACT.Square,
                                 accum_out=ms[:, 0, t:t + 1]).then_inc(x_sq, 1)
        row_root(0)
        split_hi(0)
        split_hi(1)
        act.wait_ge(prm_in, 16 * N_PRM)
        nc.scalar.activation(dtt[:, 1, :], dtt[:, 0, :], ACT.Exp).then_inc(prep_act, 1)
        act.wait_ge(lam_dots, 2)
        nc.scalar.activation(nlam[:, 2:4], nlam[:, 0:2], ACT.Exp).then_inc(prep_act, 1)
        act.wait_ge(cols_turned, 1)
        nc.scalar.activation(cols[:, :], ps[:, 0, 0:2 * KT + UT], ACT.Identity).then_inc(cols_copied, 1)
        act.wait_ge(cols_copied, 1)
        for k in range(KT):
            turn_hi(0, k, g1_col)
        act.wait_ge(args_ready, 1)
        nc.scalar.activation(prm[:, 4, :], prm[:, 2, :], ACT.Exp).then_inc(prep_act, 1)
        act.wait_ge(args_ready, 3)
        nc.scalar.activation(prm[:, 6, :], prm[:, 8, :], ACT.Sin).then_inc(prep_act, 1)
        nc.scalar.activation(prm[:, 5, :], prm[:, 9, :], ACT.Sin, bias=halfpi[0:PAIRS, :],
                             scale=-1.0).then_inc(prep_act, 1)

        act.wait_ge(frow_out, 1)
        act.dma_start(frow_dram, frow[:, :].unsqueeze(1).to_broadcast([N_HEADS, P, BIAS_W])).then_inc(frow_done, 16)

        for u in range(U_SSM, U_V):
            split_hi(u + 2)
            act.wait_ge(unit_used, U_SSM + u + 1)
            nc.scalar.activation(uT[:, u, :], ps[:, u, :], ACT.Identity).then_inc(u_copied, 1)

        def copy_c():
            for ri in range(2):
                act.wait_ge(c_turned, ri + 1)
                for g2 in range(2):
                    rows = slice(64 * g2, 64 * g2 + 64)
                    src = ps[rows, 4 + ri, :].rearrange("p (t j g h) -> p (t j) g h", t=UT, g=2, h=SSM_GROUP)
                    nc.scalar.activation(c_pk[rows, ri, :, :], src[:, :, g2, :], ACT.Identity).then_inc(c_packed, 1)

        def copy_bb(half):
            for n in (2 * half, 2 * half + 1):
                act.wait_ge(bb_turned, n + 1)
                nc.scalar.activation(BT[:, n // 2, n % 2, :, :].rearrange("p t s -> p (t s)"),
                                     ps[:, 6 + n % 2, :], ACT.Identity).then_inc(BT_ready, 1)

        for u in range(U_V, U_QK):
            split_hi(u + 2)
            c, last = (u - U_V) // 4, (u - U_V) % 4 == 3
            if u == U_V + 4:
                copy_c()
                copy_bb(0)
            if u == U_GA:
                copy_bb(1)
            if last:
                for t in range(TOK):
                    wait_rows(act, c, t)
                    if c < 2:
                        nc.scalar.activation(V[:, t, 512 * c:512 * c + 512], ps[:, t, :],
                                             ACT.Identity).then_inc(nat_copied, 1)
                    else:
                        if c == 2:
                            act.wait_ge(table, 1)
                        nc.scalar.activation(mixA[:, t, 512 * (c - 2):512 * (c - 1)], ps[:, t, :], ACT.Tanh,
                                             scale=0.5).then_inc(nat_copied, 1)

        def copy_qk(v):
            act.wait_ge(unit_used, U_QK + v + 1)
            h = v // 2
            if h >= 2:
                act.wait_ge(score_ready, TOK * (h - 1))
            if v == 0:
                act.wait_ge(table, 1)
                act.wait_ge(frow_done, 16)
            dst = (qT, kT)[v % 2][:, h % 2, :]
            nc.scalar.activation(dst, ps[:, B_QK, :], ACT.Identity,
                                 scale=(HEAD_DIM ** -0.5 if v % 2 == 0 else 1.0)).then_inc(qk_copied, 1)

        def exps(n):
            L = P * (n % TOK + 1)
            act.wait_ge(nmax_ready, n + 1)
            for m in range(2):
                nc.scalar.activation(Pm[:, n % 2, m, 0:L], Pm[:, n % 2, m, 0:L], ACT.Exp,
                                     bias=nmx[:, n % 2, m:m + 1],
                                     accum_out=sums[:, n % 2, m:m + 1]).then_inc(exp_done, 1)

        def copy_wT(n):
            L = P * (n % TOK + 1)
            act.wait_ge(wT_ready, n + 1)
            if n >= 2:
                act.wait_ge(pv_done, n - 1)
            nc.scalar.activation(wT[:, n % 2, 0:L], ps[:, B_WT, 0:L], ACT.Identity).then_inc(wT_copied, 1)

        def square_o(h):
            act.wait_ge(pv_done, TOK * (h + 1))
            for i in range(TOK):
                n = TOK * h + i
                if n >= 1:
                    act.wait_ge(o_squared, n)
                nc.scalar.activation(osq[:, :], ps[:, B_O, P * i:P * i + P], ACT.Square,
                                     scale=rinv[:, n % 8, 0:1],
                                     accum_out=ssq[:, i, h:h + 1]).then_inc(o_squared, 1)

        for v in range(2):
            split_hi(U_QK + v + 2)
            copy_qk(v)
        for n in range(BLOCKS + 2):
            h, i = n // TOK, n % TOK
            if n < BLOCKS:
                exps(n)
                if i % 2 == 0 and h < N_HEADS - 1:
                    split_hi(U_QK + 2 * (h + 1) + i // 2 + 2)
            if 1 <= n <= BLOCKS:
                copy_wT(n - 1)
            if i % 2 == 1 and h < N_HEADS - 1:
                copy_qk(2 * (h + 1) + i // 2)
            if i == 1 and h >= 1:
                square_o(h - 1)

        for u in range(U_GS, U_GLU):
            split_hi(u + 2)
            c = 4 + (u - U_GS) // 4
            if (u - U_GS) % 4 == 3:
                for t in range(TOK):
                    wait_rows(act, c, t)
                    nc.scalar.activation(mixS[:, t, 512 * (c - 4):512 * (c - 3)], ps[:, t, :], ACT.Tanh,
                                         scale=0.5).then_inc(nat_copied, 1)
        act.wait_ge(o_squared, BLOCKS)
        nc.scalar.activation(ssq[:, :, :], ssq[:, :, :], ACT.Sqrt, bias=eps_t[:, :],
                             scale=1.0 / V_DIM).then_inc(rsub_step, 1)
        for k in range(UT):
            act.wait_ge(y_done, k + 1)
            nc.scalar.activation(uT[:, k, :], uT[:, k, :], ACT.Gelu_apprx_tanh).then_inc(gelu_done, 1)
        for k in range(UT):
            act.wait_ge(gelu_done, k + 1)
            nc.scalar.activation(gT_hi[:, k, :], uT[:, k, :], ACT.Identity).then_inc(gT_hi_done, 1)
        for u in range(U_GLU, U_OUT):
            split_hi(u + 2)
            c = 6 + (u - U_GLU) // 2
            if (u - U_GLU) % 4 == 1:
                for t in range(TOK):
                    n = TOK * ((c - 6) // 2) + t
                    wait_rows(act, c, t)
                    if n >= 2:
                        act.wait_ge(zt_used, n - 1)
                    nc.scalar.activation(zt[:, n % 2, :], ps[:, t, :], ACT.Tanh, scale=0.5).then_inc(nat_copied, 1)

        for k in range(KT):
            turn_hi(1, k, None)
        for u in range(U_OUT, U_MLP):
            split_hi(u + 2)
        for t in range(TOK):
            act.wait_ge(nat_added, NAT_OUT + TOK + t + 1)
            if t:
                act.wait_ge(x_sq, TOK + t)
            row_stats(1, t, x2[:, t, :])
        row_root(1)
        for k in range(KT):
            turn_hi(2, k, g2_col)

        f = 0
        for step, (kind, quarter) in enumerate(MLP_ORDER):
            for n in range(8):
                u = U_MLP + 8 * step + n
                split_hi(u + 2)
                if kind == "up":
                    act.wait_ge(unit_used, u + 1)
                    if f >= 2:
                        act.wait_ge(f_sq, f - 1)
                        act.wait_ge(f_hi_done, f - 1)
                    nc.scalar.activation(fr[:, f % 2, :], ps[:, B_T + f % 4, :], ACT.Relu).then_inc(f_relu, 1)
                    act.wait_ge(f_relu, f + 1)
                    if quarter >= 2 and n == 0:
                        act.wait_ge(unit_used, U_MLP + 8 * (MLP_ORDER.index(("down", quarter - 2)) + 1))
                    nc.scalar.activation(fT_hi[:, quarter % 2, n, :], fr[:, f % 2, :],
                                         ACT.Square).then_inc(f_hi_done, 1)
                    f += 1
        for t in range(TOK):
            act.wait_ge(nat_added, NAT_END - TOK + t + 1)
            if t:
                act.wait_ge(x_sq, 2 * TOK + t)
            row_stats(2, t, x2[:, t, :])
        row_root(2)

    @block.vector
    def _(dve):
        steps = [0]

        def link(ins):
            steps[0] += 1
            ins.then_inc(prep, 1)

        def settle():
            dve.wait_ge(prep, steps[0])

        TT, TS, STT = nc.vector.tensor_tensor, nc.vector.tensor_scalar, nc.vector.scalar_tensor_tensor

        def turn_lo(g, k, gain):
            dve.wait_ge(hT_hi_done, KT * g + k + 1)
            src, hi = ps[:, B_T + k % 4, :], hT_hi[:, k, :].bitcast(F32)
            if gain is None:
                ins = TT(hT_lo[:, k, :], src, hi, ALU.subtract)
            else:
                ins = STT(out=hT_lo[:, k, :], in0=src, scalar=gain[:, k:k + 1], in1=hi,
                          op0=ALU.mult, op1=ALU.subtract)
            ins.then_inc(hT_lo_done, 1)

        def scale_rows(g, src, dst):
            dve.wait_ge(x_rt, g + 1)
            nc.vector.reciprocal(rstd[:, g, :], ms[:, g, :]).then_inc(x_rstd, 1)
            dve.wait_ge(x_rstd, g + 1)
            for t in range(TOK):
                TS(dst[:, t, :], src[:, t, :], rstd[:, g, t:t + 1], None, ALU.mult).then_inc(x_scaled, 1)

        dve.wait_ge(consts_in, 16 * N_CONST)
        for j in range(2):
            TT(lamv[:, j, 0, :], lamv[:, j, 0, :], lamv[:, j, 1, :], ALU.mult).then_inc(prep, 1)
        steps[0] = 2
        settle()
        for j in range(2):
            nc.vector.tensor_reduce(nlam[:, j:j + 1], lamv[:, j, 0, :], mybir.AxisListType.X,
                                    ALU.add).then_inc(lam_dots, 1)
        link(TS(gsub[:, :], gsub[:, :], (1.0 - LAM_INIT) * 0.5, None, ALU.mult))
        scale_rows(0, mixA, mixA)
        dve.wait_ge(cols_copied, 1)
        for k in range(KT):
            turn_lo(0, k, g1_col)

        dve.wait_ge(frow_mm, 1)
        link(TS(frow[:, 0:512], ps[0:N_HEADS, 4, :], 1.0, None, ALU.mult))
        link(TS(frow[:, 512:BIAS_W], ps[0:N_HEADS, 5, 0:BIAS_W - 512], 0.0, MASKED, ALU.mult, ALU.add))
        settle()
        nc.vector.sem_inc(frow_out, 1)

        dve.wait_ge(prep_act, 2)
        link(TT(nlam[:, 0:1], nlam[:, 3:4], nlam[:, 2:3], ALU.subtract))
        settle()
        link(TS(nlam[:, 0:1], nlam[:, 0:1], -LAM_INIT, None, ALU.add))

        def prow(i):
            return prm[:, i, :]

        A_RE, A_IM, A_DT, TH, MAG, COS, SIN, TURNS, RED, ABS, LR, LI, DEN, T0, T1, CR, CI = range(17)
        dt_b = dtt[:, 1, :].unsqueeze(2).to_broadcast([PAIRS, 2, SSM_STATE])

        def by_group(i):
            return prow(i).rearrange("i (two s) -> i two s", two=2)

        TT(by_group(A_DT), by_group(A_RE), dt_b, ALU.mult).then_inc(args_ready, 1)
        link(TT(by_group(TH), by_group(A_IM), dt_b, ALU.mult))
        settle()
        BIG = 1.5 * 2.0 ** 23
        C1 = 6.28125
        C2 = float(np.float32(np.round((2 * math.pi - C1) * 2.0 ** 20) / 2.0 ** 20))
        C3 = float(np.float32(2 * math.pi - C1 - C2))
        link(TS(prow(TURNS), prow(TH), 1.0 / (2 * math.pi), BIG, ALU.mult, ALU.add))
        settle()
        link(TS(prow(TURNS), prow(TURNS), -BIG, None, ALU.add))
        settle()
        link(STT(out=prow(RED), in0=prow(TURNS), scalar=-C1, in1=prow(TH), op0=ALU.mult, op1=ALU.add))
        settle()
        link(STT(out=prow(RED), in0=prow(TURNS), scalar=-C2, in1=prow(RED), op0=ALU.mult, op1=ALU.add))
        settle()
        link(STT(out=prow(RED), in0=prow(TURNS), scalar=-C3, in1=prow(RED), op0=ALU.mult, op1=ALU.add))
        settle()
        TS(prow(RED), prow(RED), 3.1415925, -3.1415925, ALU.min, ALU.max).then_inc(args_ready, 1)
        dve.wait_ge(args_ready, 2)
        STT(out=prow(ABS), in0=prow(RED), scalar=-1.0, in1=prow(RED), op0=ALU.mult,
            op1=ALU.max).then_inc(args_ready, 1)
        link(TT(prow(T0), prow(A_RE), prow(A_RE), ALU.mult))
        link(TT(prow(T1), prow(A_IM), prow(A_IM), ALU.mult))
        settle()
        link(TT(prow(DEN), prow(T0), prow(T1), ALU.add))
        settle()
        link(nc.vector.reciprocal(prow(DEN), prow(DEN)))
        dve.wait_ge(prep_act, 5)
        link(TT(prow(LR), prow(MAG), prow(COS), ALU.mult))
        link(TT(prow(LI), prow(MAG), prow(SIN), ALU.mult))
        settle()
        link(TS(prow(LR), prow(LR), -1.0, None, ALU.add))
        settle()
        link(TT(prow(T0), prow(LR), prow(A_RE), ALU.mult))
        link(TT(prow(T1), prow(LI), prow(A_IM), ALU.mult))
        settle()
        link(TT(prow(CR), prow(T0), prow(T1), ALU.add))
        settle()
        link(TT(prow(T0), prow(LI), prow(A_RE), ALU.mult))
        link(TT(prow(T1), prow(LR), prow(A_IM), ALU.mult))
        settle()
        link(TT(prow(CI), prow(T0), prow(T1), ALU.subtract))
        link(TT(prow(CR), prow(CR), prow(DEN), ALU.mult))
        settle()
        link(TT(prow(CI), prow(CI), prow(DEN), ALU.mult))
        settle()
        nc.vector.sem_inc(prm_ready, 1)
        dve.wait_ge(prm_turned, 1)
        nc.vector.tensor_copy(mag[:, :, :].rearrange("p a i -> p (a i)"), ps[:, 7, 0:5 * PAIRS]).then_inc(prm_copied, 1)
        dve.wait_ge(prm_copied, 1)

        def coef_b(half):
            cr = coef[:, half, 0, :].unsqueeze(2).to_broadcast([P, PAIRS, SSM_GROUP])
            ci = coef[:, half, 1, :].unsqueeze(2).to_broadcast([P, PAIRS, SSM_GROUP])
            if half:
                dve.wait_ge(bb_turned, 2)
            else:
                dve.wait_ge(tiles_set, 3)
            link(TT(bt[:, 0, :, :], b_nat[:, 0, :, :], cr, ALU.mult))
            link(TT(bt[:, 1, :, :], b_nat[:, 1, :, :], ci, ALU.mult))
            link(TT(bt[:, 2, :, :], b_nat[:, 1, :, :], cr, ALU.mult))
            link(TT(bt[:, 3, :, :], b_nat[:, 0, :, :], ci, ALU.mult))
            settle()
            for ri in range(2):
                for g2 in range(2):
                    rows, cols = slice(64 * g2, 64 * g2 + 64), slice(16 * g2, 16 * g2 + 16)
                    TT(bb[rows, ri, :, cols], bt[rows, 2 * ri, :, :], bt[rows, 2 * ri + 1, :, :],
                       (ALU.subtract, ALU.add)[ri]).then_inc(bb_ready, 1)

        link(nc.vector.tensor_copy(coef[:, 0, :, :], mag[:, 3:5, :]))
        link(nc.vector.tensor_copy(pw[:, 0, :, :], mag[:, 1:3, :]))
        settle()
        coef_b(0)

        dve.wait_ge(tiles_set, 6)
        dve.wait_ge(turned, KT)
        levels = HALF.bit_length() - 1
        for lv in range(levels):
            n = 1 << lv
            p_re, p_im = pw[:, lv % 2, 0, :], pw[:, lv % 2, 1, :]
            q_re, q_im = pw[:, (lv + 1) % 2, 0, :], pw[:, (lv + 1) % 2, 1, :]
            pr = p_re.unsqueeze(2).to_broadcast([P, PAIRS, n])
            pi = p_im.unsqueeze(2).to_broadcast([P, PAIRS, n])
            a, b = em[:, 0, :, 0:n], em[:, 1, :, 0:n]
            link(TT(a, E_re[:, :, 0:n], pr, ALU.mult))
            link(TT(b, E_im[:, :, 0:n], pi, ALU.mult))
            link(TT(pwt[:, 0, :], p_re, p_re, ALU.mult))
            link(TT(pwt[:, 1, :], p_im, p_im, ALU.mult))
            link(STT(out=q_im, in0=p_re, scalar=2.0, in1=p_im, op0=ALU.mult, op1=ALU.mult))
            settle()
            link(TT(E_re[:, :, n:2 * n], a, b, ALU.subtract))
            link(TT(q_re, pwt[:, 0, :], pwt[:, 1, :], ALU.subtract))
            settle()
            link(TT(a, E_re[:, :, 0:n], pi, ALU.mult))
            link(TT(b, E_im[:, :, 0:n], pr, ALU.mult))
            settle()
            link(TT(E_im[:, :, n:2 * n], a, b, ALU.add))
            settle()
        p_re, p_im = pw[:, levels % 2, 0, :], pw[:, levels % 2, 1, :]
        c_re, c_im = coef[:, 0, 0, :], coef[:, 0, 1, :]
        link(TT(pwt[:, 0, :], c_re, p_re, ALU.mult))
        link(TT(pwt[:, 1, :], c_im, p_im, ALU.mult))
        link(TT(pwt[:, 2, :], c_im, p_re, ALU.mult))
        link(TT(pwt[:, 3, :], c_re, p_im, ALU.mult))
        settle()
        link(TT(coef[:, 1, 0, :], pwt[:, 0, :], pwt[:, 1, :], ALU.add))
        link(TT(coef[:, 1, 1, :], pwt[:, 2, :], pwt[:, 3, :], ALU.subtract))
        settle()
        coef_b(1)
        dve.wait_ge(c_packed, 4)
        pr = p_re.unsqueeze(2).to_broadcast([P, PAIRS, SSM_GROUP])
        pi = p_im.unsqueeze(2).to_broadcast([P, PAIRS, SSM_GROUP])
        dve.wait_ge(bb_ready, 8)
        settle()
        link(TT(bt[:, 0, :, :], c_pk[:, 0, :, :], pr, ALU.mult))
        link(TT(bt[:, 1, :, :], c_pk[:, 1, :, :], pi, ALU.mult))
        link(TT(bt[:, 2, :, :], c_pk[:, 0, :, :], pi, ALU.mult))
        link(TT(bt[:, 3, :, :], c_pk[:, 1, :, :], pr, ALU.mult))
        settle()
        for g2 in range(2):
            rows, cols = slice(64 * g2, 64 * g2 + 64), slice(16 * g2, 16 * g2 + 16)
            link(TS(CT[rows, :, 0, 0, cols], c_pk[rows, 0, :, :], 1.0, None, ALU.mult))
            link(TS(CT[rows, :, 0, 1, cols], c_pk[rows, 1, :, :], -1.0, None, ALU.mult))
            link(TT(CT[rows, :, 1, 0, cols], bt[rows, 0, :, :], bt[rows, 1, :, :], ALU.subtract))
            link(STT(out=CT[rows, :, 1, 1, cols], in0=bt[rows, 2, :, :], scalar=-1.0, in1=bt[rows, 3, :, :],
                     op0=ALU.mult, op1=ALU.subtract))
        settle()
        nc.vector.sem_inc(table, 1)

        STEPS = 14

        def halves(ap):
            return ap.rearrange("p (c j) -> p c j", c=2)

        def ssm_part(i, part):
            def done(k):
                dve.wait_ge(ssm_step, STEPS * i + k)

            er = E_re[:, i:i + 1, :].to_broadcast([P, 2, HALF])
            ei = E_im[:, i:i + 1, :].to_broadcast([P, 2, HALF])
            t = [halves(rt[:, k, :]) for k in range(4)]
            s = [halves(st[:, k, :]) for k in range(2)]
            if part == 0:
                dve.wait_ge(bu_ready, i + 1)
                done(0)
                b_re, b_im = halves(ps[:, B_BU, :]), halves(ps[:, B_BU + 1, :])
                TT(t[0], b_re, er, ALU.mult).then_inc(ssm_step, 1)
                TT(t[1], b_im, ei, ALU.mult).then_inc(ssm_step, 1)
                TT(t[2], b_im, er, ALU.mult).then_inc(ssm_step, 1)
                TT(t[3], b_re, ei, ALU.mult).then_inc(ssm_step, 1)
            elif part == 1:
                done(2)
                TT(t[0], t[0], t[1], ALU.add).then_inc(ssm_step, 1)
                done(4)
                TT(t[2], t[2], t[3], ALU.subtract).then_inc(ssm_step, 1)
                decay = mag[:, 0, i:i + 1].to_broadcast([P, SEQ])
                for k in range(2):
                    done(5 + k)
                    nc.vector.tensor_tensor_scan(rt[:, 2 * k + 1, :], decay, rt[:, 2 * k, :], 0.0,
                                                 ALU.mult, ALU.add).then_inc(ssm_step, 1)
            elif part == 2:
                if i:
                    dve.wait_ge(y_ready, i)
                done(7)
                TT(t[0], t[1], er, ALU.mult).then_inc(ssm_step, 1)
                TT(s[1], t[1], ei, ALU.mult).then_inc(ssm_step, 1)
                done(8)
                TT(t[2], t[3], ei, ALU.mult).then_inc(ssm_step, 1)
                TT(t[3], t[3], er, ALU.mult).then_inc(ssm_step, 1)
            else:
                done(11)
                TT(s[0], t[0], t[2], ALU.subtract).then_inc(ssm_step, 1)
                done(12)
                TT(s[1], s[1], t[3], ALU.add).then_inc(ssm_step, 1)

        def y_skip(ut):
            dve.wait_ge(y_ready, 4 * ut + 4)
            STT(out=uT[:, ut, :], in0=uT[:, ut, :], scalar=d_col[:, ut:ut + 1], in1=ps[:, B_Y, :],
                op0=ALU.mult, op1=ALU.add).then_inc(y_done, 1)

        def ssm_tile(i):
            for part in range(4):
                ssm_part(i, part)
                if part == 1 and i % 4 == 0 and i:
                    y_skip(i // 4 - 1)

        def gate_a(c):
            for t in range(TOK):
                dve.wait_ge(nat_copied, TOK * (2 + c) + t + 1)
                g = mixA[:, t, 512 * c:512 * c + 512].rearrange("p (h v) -> p h v", v=V_DIM)
                STT(out=g, in0=g, scalar=1.0, in1=gsub[:, :].unsqueeze(1).to_broadcast([P, 4, V_DIM]),
                    op0=ALU.add, op1=ALU.mult).then_inc(gates_done, 1)

        for i in range(4):
            ssm_tile(i)
            if i % 2:
                gate_a(i // 2)

        def pre(n):
            h, i = n // TOK, n % TOK
            L = P * (i + 1)
            dve.wait_ge(score_ready, n + 1)
            dve.wait_ge(bias_in[h % 2], 16 * (h // 2 + 1))
            if n >= 2:
                dve.wait_ge(wT_ready, n - 1)
            for m in range(2):
                nc.vector.tensor_tensor_reduce(
                    out=Pm[:, n % 2, m, 0:L], in0=ps[:, B_SCORE + m, 0:L],
                    in1=bias[:, h % 2, SEQ - L:SEQ], scale=1.0, scalar=-3e38,
                    op0=ALU.add, op1=ALU.max, accum_out=mx[:, n % 2, m:m + 1]).then_inc(score_read, 1)
            dve.wait_ge(score_read, 2 * n + 2)
            TS(nmx[:, n % 2, :], mx[:, n % 2, :], -1.0, None, ALU.mult).then_inc(nmax_ready, 1)

        def post(n):
            L = P * (n % TOK + 1)
            dve.wait_ge(exp_done, 2 * n + 2)
            nc.vector.reciprocal(rinv[:, n % 8, :], sums[:, n % 2, :]).then_inc(att_step, 1)
            dve.wait_ge(att_step, 3 * n + 1)
            STT(out=cfac[:, n % 2, :], in0=rinv[:, n % 8, 1:2], scalar=sums[:, n % 2, 0:1], in1=nlam[:, 0:1],
                op0=ALU.mult, op1=ALU.mult).then_inc(att_step, 1)
            dve.wait_ge(att_step, 3 * n + 2)
            STT(out=Pm[:, n % 2, 0, 0:L], in0=Pm[:, n % 2, 1, 0:L], scalar=cfac[:, n % 2, :],
                in1=Pm[:, n % 2, 0, 0:L], op0=ALU.mult, op1=ALU.add).then_inc(att_step, 1)

        def gate_o(h):
            dve.wait_ge(o_squared, TOK * (h + 1))
            for i in range(TOK):
                n = TOK * h + i
                g = mixA[:, i, V_DIM * h:V_DIM * h + V_DIM]
                STT(out=g, in0=ps[:, B_O, P * i:P * i + P], scalar=rinv[:, n % 8, 0:1], in1=g,
                    op0=ALU.mult, op1=ALU.mult).then_inc(o_gated, 1)

        dve.wait_ge(gates_done, 2 * TOK)
        for n in range(BLOCKS + 2):
            h, i = n // TOK, n % TOK
            if n < BLOCKS:
                pre(n)
                ssm_part(4 + h, i)
                if i == 1 and h % 4 == 0:
                    y_skip(h // 4)
                post(n)
            if i == 1 and h >= 1:
                gate_o(h - 1)

        def gate_s(c):
            for t in range(TOK):
                dve.wait_ge(nat_copied, TOK * (4 + c) + t + 1)
                g = mixS[:, t, 512 * c:512 * c + 512]
                TS(g, g, 0.25, 0.25, ALU.mult, ALU.add).then_inc(gates_done, 1)

        for i in range(4):
            ssm_tile(12 + i)
            if i % 2:
                gate_s(i // 2)
        y_skip(3)
        for k in range(UT):
            dve.wait_ge(gT_hi_done, k + 1)
            TT(gT_lo[:, k, :], uT[:, k, :], gT_hi[:, k, :].bitcast(F32), ALU.subtract).then_inc(gT_lo_done, 1)

        for half in range(2):
            cols = slice(512 * half, 512 * half + 512)
            for t in range(TOK):
                n = TOK * half + t
                dve.wait_ge(nat_copied, TOK * (6 + half) + t + 1)
                dve.wait_ge(gates_done, 4 * TOK)
                STT(out=mixS[:, t, cols], in0=zt[:, n % 2, :], scalar=1.0, in1=mixS[:, t, cols],
                    op0=ALU.add, op1=ALU.mult).then_inc(zt_used, 1)
            if half == 0:
                dve.wait_ge(rsub_step, 1)
                nc.vector.reciprocal(rsub[:, :, :], ssq[:, :, :]).then_inc(rsub_step, 1)
            for t in range(TOK):
                wait_rows(dve, (7 + 2 * half), t)
                dve.wait_ge(zt_used, TOK * half + t + 1)
                TT(mixS[:, t, cols], ps[:, t, :], mixS[:, t, cols], ALU.mult).then_inc(nat_added, 1)
            dve.wait_ge(rsub_step, 2)
            dve.wait_ge(o_gated, BLOCKS)
            for t in range(TOK):
                dve.wait_ge(nat_added, TOK * half + t + 1)
                for h in range(4 * half, 4 * half + 4):
                    hc = slice(V_DIM * h, V_DIM * h + V_DIM)
                    STT(out=mixA[:, t, hc], in0=mixA[:, t, hc], scalar=rsub[:, t, h:h + 1], in1=mixS[:, t, hc],
                        op0=ALU.mult, op1=ALU.add).then_inc(mixed_done, 1)
        for k in range(KT):
            turn_lo(1, k, None)

        dve.wait_ge(x_again, 16 * TOK)

        def add_chunk(c, index):
            for t in range(TOK):
                wait_rows(dve, c, t)
                if index > 3:
                    dve.wait_ge(nat_added, TOK * (index - 2) + t + 1)
                cols = slice(512 * (c % 2), 512 * (c % 2) + 512)
                TT(x2[:, t, cols], x2[:, t, cols], ps[:, t, :], ALU.add).then_inc(nat_added, 1)

        add_chunk(10, 2)
        add_chunk(11, 3)
        scale_rows(1, x2, xn2)
        for k in range(KT):
            turn_lo(2, k, g2_col)

        f = 0
        for kind, quarter in MLP_ORDER:
            if kind == "up":
                for n in range(8):
                    dve.wait_ge(f_relu, f + 1)
                    if f >= 2:
                        dve.wait_ge(f_lo_done, f - 1)
                    TT(fs[:, f % 2, :], fr[:, f % 2, :], fr[:, f % 2, :], ALU.mult).then_inc(f_sq, 1)
                    dve.wait_ge(f_sq, f + 1)
                    dve.wait_ge(f_hi_done, f + 1)
                    TT(fT_lo[:, quarter % 2, n, :], fs[:, f % 2, :], fT_hi[:, quarter % 2, n, :].bitcast(F32),
                       ALU.subtract).then_inc(f_lo_done, 1)
                    f += 1
            else:
                for half in range(2):
                    add_chunk(12 + 2 * quarter + half, 4 + 2 * quarter + half)
        dve.wait_ge(x_rt, 3)
        nc.vector.reciprocal(rstd[:, 2, :], ms[:, 2, :]).then_inc(x_rstd, 1)
        dve.wait_ge(x_rstd, 3)
        dve.wait_ge(gfin_in, 16)
        for t in range(TOK):
            STT(out=x2[:, t, :], in0=x2[:, t, :], scalar=rstd[:, 2, t:t + 1], in1=gfin[:, :],
                op0=ALU.mult, op1=ALU.mult).then_inc(out_ready, 1)

    @block.tensor
    def _(pe):
        def mm3(dst, a_hi, a_lo, b_hi, b_lo, start, stop):
            nc.tensor.matmul(dst, a_hi, b_hi, start=start, stop=False)
            nc.tensor.matmul(dst, a_hi, b_lo, start=False, stop=False)
            return nc.tensor.matmul(dst, a_lo, b_hi, start=False, stop=stop)

        def col_mm(u, bank, ks):
            for k in ks:
                c = slice(P * k, P * k + P)
                mm = mm3(ps[:, bank, :], w_hi[:, u % RING, c], w_lo[:, u % RING, c],
                         hT_hi[:, k, :], hT_lo[:, k, :], k == 0, k == KT - 1)
            return mm

        def row_unit_mm(u, c, r, n_rows, hi, lo, ready, per_row):
            pe.wait_ge(w_lo_done, u + 1)
            for t in range(TOK):
                if r == 0:
                    nat_free(c, t)
                for k2 in range(2):
                    k = 2 * r + k2
                    if t == 0 and ready is not None:
                        pe.wait_ge(ready, per_row + k + 1)
                    wc = slice(512 * k2, 512 * k2 + 512)
                    tc_ = slice(P * t, P * t + P)
                    mm = mm3(ps[:, t, :], hi[:, k, tc_], lo[:, k, tc_], w_hi[:, u % RING, wc],
                             w_lo[:, u % RING, wc], r == 0 and k2 == 0, r == n_rows - 1 and k2 == 1)
                if r == n_rows - 1 and t < TOK - 1:
                    mm.then_inc(nat_ready, 1)
            unit_done(mm)

        def unit_done(mm):
            mm.then_inc(unit_used, 1)

        COPIED = {0: 0, 1: 1, 2: 2, 3: 3, 4: 4, 5: 5, 6: 6, 8: 7}
        ADDED = {7: 0, 9: 1}
        ADDED.update({c: c - 8 for c in range(10, 20)})

        def nat_free(c, t):
            if c == 0:
                pe.wait_ge(u_copied, UT)
            elif c == 4:
                pe.wait_ge(score_read, 2 * BLOCKS)
                pe.wait_ge(wT_copied, BLOCKS)
                pe.wait_ge(o_gated, BLOCKS)
            elif c - 1 in COPIED:
                pe.wait_ge(nat_copied, TOK * COPIED[c - 1] + t + 1)
            else:
                pe.wait_ge(nat_added, TOK * ADDED[c - 1] + t + 1)

        def turn(g, src, ready, count):
            for k in range(KT):
                if k >= 4:
                    pe.wait_ge(hT_lo_done, KT * g + k - 3)
                elif g == 1:
                    pe.wait_ge(qk_copied, 2 * N_HEADS)
                    pe.wait_ge(y_done, UT)
                elif g == 2:
                    pe.wait_ge(hT_lo_done, 2 * KT)
                pe.wait_ge(ready, count(k))
                for t in range(TOK):
                    mm = nc.tensor.transpose(ps[:, B_T + k % 4, P * t:P * t + P], src[:, t, P * k:P * k + P],
                                             ident[:, :])
                mm.then_inc(turned, 1)

        def drive(i):
            j, ut = i % 4, i // 4
            rows = slice(32 * j, 32 * j + 32)
            pe.wait_ge(BT_ready, 4)
            pe.wait_ge(u_copied, ut + 1)
            if i:
                pe.wait_ge(ssm_step, 14 * (i - 1) + 4)
            for c in range(2):
                for ri in range(2):
                    mm = nc.tensor.matmul(ps[:, B_BU + ri, HALF * c:HALF * c + HALF], BT[rows, c, ri, ut, :],
                                          uT[rows, ut, HALF * c:HALF * c + HALF], start=True, stop=True)
            mm.then_inc(bu_ready, 1)

        def readout(i):
            j, ut = i % 4, i // 4
            pe.wait_ge(ssm_step, 14 * i + 14)
            if j == 0 and ut:
                pe.wait_ge(y_done, ut)
            if i == 0:
                pe.wait_ge(table, 1)
            for c in range(2):
                for ri in range(2):
                    mm = nc.tensor.matmul(ps[32 * j:32 * j + 32, B_Y, HALF * c:HALF * c + HALF],
                                          CT[:, i, c, ri, :], st[:, ri, HALF * c:HALF * c + HALF],
                                          start=(ri == 0), stop=(ri == 1), tile_position=(0, 32 * j))
            mm.then_inc(y_ready, 1)

        pe.wait_ge(ident_set, 2)
        pe.wait_ge(consts_in, 16 * N_CONST)
        nc.tensor.transpose(ps[:, 0, 0:2 * KT + UT], cols_nat[:, :],
                            ident[0:2 * KT + UT, 0:2 * KT + UT]).then_inc(cols_turned, 1)
        turn(0, mixA, x_scaled, lambda k: TOK)
        pe.wait_ge(consts_in, 16 * N_CONST)
        pe.wait_ge(hT_lo_done, 6)
        nc.tensor.matmul(ps[0:N_HEADS, 4, :], rb[:, :], oneh[:, 0:512], start=True, stop=True)
        nc.tensor.matmul(ps[0:N_HEADS, 5, 0:BIAS_W - 512], rb[:, :], oneh[:, 512:BIAS_W], start=True,
                         stop=True).then_inc(frow_mm, 1)

        for u in range(U_SSM, U_V):
            pe.wait_ge(w_lo_done, u + 1)
            if u == 0:
                pe.wait_ge(hT_lo_done, KT)
            mm = col_mm(u, u, range(KT))
            unit_done(mm)
        pe.wait_ge(prm_ready, 1)
        for n, row in enumerate((4, 5, 6, 15, 16)):
            mm = nc.tensor.transpose(ps[:, 7, PAIRS * n:PAIRS * n + PAIRS], prm[:, row, :],
                                     ident[0:PAIRS, 0:PAIRS])
        mm.then_inc(prm_turned, 1)

        def turn_c():
            for ri in range(2):
                if ri == 0:
                    pe.wait_ge(frow_out, 1)
                for ut in range(UT):
                    mm = nc.tensor.transpose(ps[:, 4 + ri, P * ut:P * ut + P],
                                             c_nat[:, ri, ut, :, :].rearrange("p a s -> p (a s)"), ident[:, :])
                mm.then_inc(c_turned, 1)

        def turn_bb(half):
            for ri in range(2):
                pe.wait_ge(bb_ready, 4 * half + 2 * ri + 2)
                if half:
                    pe.wait_ge(BT_ready, ri + 1)
                else:
                    pe.wait_ge(prm_copied, 1)
                for ut in range(UT):
                    mm = nc.tensor.transpose(ps[:, 6 + ri, P * ut:P * ut + P],
                                             bb[:, ri, 4 * ut:4 * ut + 4, :].rearrange("p a h -> p (a h)"),
                                             ident[:, :])
                mm.then_inc(bb_turned, 1)

        for u in range(U_V, U_GA):
            r = (u - U_V) % 4
            row_unit_mm(u, (u - U_V) // 4, r, 4, hT_hi, hT_lo, None, 0)
            if u == U_V + 3:
                turn_c()
                turn_bb(0)
        for u in range(U_GA, U_QK):
            n = u - U_GA
            if n == 0:
                turn_bb(1)
                drive(0)
            row_unit_mm(u, 2 + n // 4, n % 4, 4, hT_hi, hT_lo, None, 0)
            if n % 2 == 0:
                drive(n // 2 + 1)
            else:
                readout(n // 2)

        def qk_part(v, part):
            u = U_QK + v
            if part == 0:
                pe.wait_ge(w_lo_done, u + 1)
                if v:
                    pe.wait_ge(qk_copied, v)
                else:
                    pe.wait_ge(c_packed, 4)
            mm = col_mm(u, B_QK, range(4 * part, 4 * part + 4))
            if part:
                unit_done(mm)

        for v in range(2):
            qk_part(v, 0)
            qk_part(v, 1)

        def scores(n):
            h, i = n // TOK, n % TOK
            L = P * (i + 1)
            pe.wait_ge(qk_copied, 2 * h + 2)
            if n == 0:
                pe.wait_ge(nat_copied, 4 * TOK)
            else:
                pe.wait_ge(score_read, 2 * n)
            for m in range(2):
                rows = slice(HEAD_DIM * m, HEAD_DIM * m + HEAD_DIM)
                mm = nc.tensor.matmul(ps[:, B_SCORE + m, 0:L], qT[rows, h % 2, P * i:P * i + P],
                                      kT[rows, h % 2, 0:L], start=True, stop=True)
            mm.then_inc(score_ready, 1)

        def turn_w(n):
            pe.wait_ge(att_step, 3 * n + 3)
            if n:
                pe.wait_ge(wT_copied, n)
            for j in range(n % TOK + 1):
                mm = nc.tensor.transpose(ps[:, B_WT, P * j:P * j + P], Pm[:, n % 2, 0, P * j:P * j + P],
                                         ident[:, :])
            mm.then_inc(wT_ready, 1)

        def pv(n):
            h, i = n // TOK, n % TOK
            pe.wait_ge(wT_copied, n + 1)
            if i == 0 and h:
                pe.wait_ge(o_gated, TOK * h)
            for j in range(i + 1):
                mm = nc.tensor.matmul(ps[:, B_O, P * i:P * i + P], wT[:, n % 2, P * j:P * j + P],
                                      V[:, j, V_DIM * h:V_DIM * h + V_DIM], start=(j == 0), stop=(j == i))
            mm.then_inc(pv_done, 1)

        for n in range(BLOCKS + 2):
            h, i = n // TOK, n % TOK
            if n >= 2:
                pv(n - 2)
            if n < BLOCKS:
                scores(n)
                if h < N_HEADS - 1:
                    qk_part(2 * (h + 1) + i // 2, i % 2)
                if i == 0 and h:
                    readout(3 + h)
                if i == 1:
                    drive(5 + h)
            if 1 <= n <= BLOCKS:
                turn_w(n - 1)

        for u in range(U_GS, U_GLU):
            n = u - U_GS
            if n == 0:
                readout(11)
            row_unit_mm(u, 4 + n // 4, n % 4, 4, hT_hi, hT_lo, None, 0)
            if n % 2:
                readout(12 + n // 2)
            elif n < 6:
                drive(13 + n // 2)
        for u in range(U_GLU, U_OUT):
            n = u - U_GLU
            row_unit_mm(u, 6 + n // 2, n % 2, 2, gT_hi, gT_lo, gT_lo_done, 0)
        turn(1, mixA, mixed_done, lambda k: 16 * (k // 4) + 16)
        for u in range(U_OUT, U_MLP):
            n = u - U_OUT
            row_unit_mm(u, 10 + n // 4, n % 4, 4, hT_hi, hT_lo, hT_lo_done, KT)
        turn(2, xn2, x_scaled, lambda k: 2 * TOK)

        f = 0
        for step, (kind, quarter) in enumerate(MLP_ORDER):
            for n in range(8):
                u = U_MLP + 8 * step + n
                if kind == "up":
                    pe.wait_ge(w_lo_done, u + 1)
                    if f < 4:
                        pe.wait_ge(hT_lo_done, 3 * KT)
                    else:
                        pe.wait_ge(f_relu, f - 3)
                    mm = col_mm(u, B_T + f % 4, range(KT))
                    unit_done(mm)
                    f += 1
                else:
                    row_unit_mm(u, 12 + 2 * quarter + n // 4, n % 4, 4, fT_hi[:, quarter % 2, :, :],
                                fT_lo[:, quarter % 2, :, :], f_lo_done, 8 * quarter)

    ctx.close()


_INS = ['x', 'g_mix', 'w_in', 'lambda_q1', 'lambda_k1', 'lambda_q2', 'lambda_k2', 'subln_g', 'rel_bias',
        'ssm_a_re', 'ssm_a_im', 'ssm_log_dt', 'ssm_b_re', 'ssm_b_im', 'ssm_c_re', 'ssm_c_im', 'ssm_d',
        'w_glu', 'w_out', 'g_mlp', 'w1', 'w2', 'g_final']


def kernel(**inputs):
    import concourse.bacc as bacc
    from concourse.bass_utils import run_bass_kernel_spmd

    nc = bacc.Bacc("TRN2", target_bir_lowering=False, num_devices=1)
    arrays, args = {}, []
    given = {name: np.ascontiguousarray(inputs[name]) for name in _INS}
    given["onehot"] = bucket_onehot()
    for name, a in given.items():
        arrays[f"in_{name}"] = a
        ap = nc.dram_tensor(f"in_{name}", a.shape, mybir.dt.from_np(a.dtype), kind="ExternalInput").ap()
        args.append(ap[0] if name in ("w_in", "w_glu", "w_out", "w1", "w2") else ap)
    out = nc.dram_tensor("out", (1, SEQ, D_MODEL), F32, kind="ExternalOutput").ap()
    build(nc, *args, out)
    r = run_bass_kernel_spmd(nc, [arrays], core_ids=[0])
    return r.results[0]["out"]
```

```python
import math
from contextlib import ExitStack

import numpy as np

import concourse.bass as bass
from concourse import mybir
from concourse.alu_op_type import AluOpType as ALU

ACT = mybir.ActivationFunctionType
F32 = mybir.dt.float32
F32R = mybir.dt.float32r

P = 128
SEQ, D_MODEL = 512, 1024
N_HEADS, HEAD_DIM, V_DIM = 8, 64, 128
SSM_WIDTH, SSM_GROUP, SSM_GROUPS, SSM_STATE = 512, 16, 32, 64
D_FF = 4096
N_BUCKETS, MAX_DISTANCE = 32, 128
EPS = 1e-6
LAM_INIT = 0.8 - 0.6 * math.exp(-0.3 * 0)
MASKED = -1e30

TOK = SEQ // P
KT = D_MODEL // P
UT = SSM_WIDTH // P
PAIRS = SSM_GROUPS // 2
HALF = SEQ // 2
BIAS_W = 640
BLOCKS = N_HEADS * TOK

RING = 4
U_SSM, U_V, U_GA, U_QK, U_GS, U_GLU, U_OUT, U_MLP = 0, 4, 12, 20, 36, 44, 52, 60
N_UNITS = U_MLP + 64
COL_Q, COL_K, COL_V, COL_U, COL_GA, COL_GS = 0, 1024, 2048, 3072, 3584, 4608

B_SCORE, B_WT, B_O, B_QK, B_Y, B_BU, B_T = 0, 2, 3, 4, 5, 6, 4


def bucket_onehot():
    rel = SEQ - 1 - np.arange(BIAS_W)
    n = np.maximum(rel, 0)
    exact = N_BUCKETS // 2
    large = exact + (np.log(np.maximum(n, 1).astype(np.float32) / np.float32(exact)).astype(np.float32)
                     / np.float32(math.log(MAX_DISTANCE / exact)) * np.float32(N_BUCKETS - exact)).astype(np.int32)
    bucket = np.where(n < exact, n, np.minimum(large, N_BUCKETS - 1))
    return ((bucket[None, :] == np.arange(N_BUCKETS)[:, None]) & (rel >= 0)[None, :]).astype(np.float32)


def build(nc, x, g_mix, w_in, lambda_q1, lambda_k1, lambda_q2, lambda_k2, subln_g, rel_bias,
          ssm_a_re, ssm_a_im, ssm_log_dt, ssm_b_re, ssm_b_im, ssm_c_re, ssm_c_im, ssm_d,
          w_glu, w_out, g_mlp, w1, w2, g_final, onehot, out):
    ctx = ExitStack()
    base = (nc.sbuf_base + 63) // 64 * 64
    at = {"next": base}

    def sb(name, shape, dt=F32, offset=None):
        size = 4 * int(np.prod(shape[1:]))
        if offset is None:
            offset = at["next"]
            at["next"] += (size + 31) // 32 * 32
        at[name] = offset
        return nc.alloc_sbuf_tensor_at(name, list(shape), dt, offset=offset)

    def sem(name):
        return ctx.enter_context(nc.semaphore(name))

    ident = sb("ident", [P, P])
    hT_hi = sb("hT_hi", [P, KT, SEQ], F32R)
    hT_lo = sb("hT_lo", [P, KT, SEQ], F32R)
    raw = sb("raw", [P, RING, 1024])
    w_hi = sb("w_hi", [P, RING, 1024], F32R)
    w_lo = sb("w_lo", [P, RING, 1024], F32R)
    mixA = sb("mixA", [P, TOK, D_MODEL])
    V = sb("V", [P, TOK, D_MODEL])
    uT = sb("uT", [P, UT, SEQ])
    E_re = sb("E_re", [P, PAIRS, HALF])
    BT = sb("BT", [P, 2, 2, UT, P])
    CT = sb("CT", [P, PAIRS, 2, 2, 32])
    E_im = sb("E_im", [P, PAIRS, HALF])
    rt = sb("rt", [P, 4, SEQ])
    st = sb("st", [P, 2, SEQ])
    qT = sb("qT", [P, 2, SEQ])
    kT = sb("kT", [P, 2, SEQ])
    bias = sb("bias", [P, 2, SEQ])
    Pm = sb("Pm", [P, 2, 2, SEQ])
    wT = sb("wT", [P, 2, SEQ])
    mag = sb("mag", [P, 5, PAIRS])
    coef = sb("coef", [P, 2, 2, PAIRS])
    pw = sb("pw", [P, 2, 2, PAIRS])
    pwt = sb("pwt", [P, 4, PAIRS])
    cols = sb("cols", [P, 2 * KT + UT])
    gsub = sb("gsub", [P, V_DIM])
    ssq = sb("ssq", [P, TOK, N_HEADS])
    rsub = sb("rsub", [P, TOK, N_HEADS])
    ms = sb("ms", [P, 3, 2, TOK])
    rstd = sb("rstd", [P, 3, TOK])
    rstd2 = sb("rstd2", [P, TOK])
    mx = sb("mx", [P, 2, 2])
    nmx = sb("nmx", [P, 2, 2])
    sums = sb("sums", [P, 2, 2])
    rinv = sb("rinv", [P, 8, 2])
    cfac = sb("cfac", [P, 2, 1])
    nlam = sb("nlam", [P, 4])
    osq = sb("osq", [P, V_DIM])
    eps_t = sb("eps_t", [P, 1])
    halfpi = sb("halfpi", [P, 1])
    assert at["next"] <= nc.sbuf_usable_end, (at["next"], nc.sbuf_usable_end)
    pt = at["qT"]
    prm = sb("prm", [PAIRS, 20, P], offset=pt)
    b_nat = sb("b_nat", [P, 2, PAIRS, SSM_GROUP], offset=pt + 10240)
    c_nat = sb("c_nat", [P, 2, UT, 2, SSM_STATE], offset=pt + 12288)
    c_pk = sb("c_pk", [P, 2, PAIRS, SSM_GROUP], offset=pt + 16384)
    oneh = sb("oneh", [N_BUCKETS, BIAS_W], offset=pt + 18432)
    frow = sb("frow", [N_HEADS, BIAS_W], offset=pt + 20992)
    lamv = sb("lamv", [P, 2, 2, HEAD_DIM], offset=at["rt"] + 11264)
    cols_nat = sb("cols_nat", [2 * KT + UT, P], offset=pt + 23552)
    bb = sb("bb", [P, 2, PAIRS, 32], offset=at["rt"])
    bt = sb("bt", [P, 4, PAIRS, SSM_GROUP], offset=at["rt"] + 4096)
    rb = sb("rb", [N_BUCKETS, N_HEADS], offset=at["rt"] + 8192)
    dtt = sb("dtt", [PAIRS, 2, 2], offset=at["rt"] + 8256)
    em = sb("em", [P, 2, PAIRS, HALF // 2], offset=at["mixA"])
    mixS = sb("mixS", [P, TOK, D_MODEL], offset=at["V"])
    gT_hi = sb("gT_hi", [P, UT, SEQ], F32R, offset=at["qT"])
    gT_lo = sb("gT_lo", [P, UT, SEQ], F32R, offset=at["bias"])
    zt = sb("zt", [P, 2, SEQ], offset=at["Pm"] + 4096)
    junk = sb("junk", [P, D_MODEL], offset=at["wT"])
    x2 = sb("x2", [P, TOK, D_MODEL], offset=at["E_im"])
    fT_hi = sb("fT_hi", [P, 2, KT, SEQ], F32R, offset=at["mixA"])
    fT_lo = sb("fT_lo", [P, 2, KT, SEQ], F32R, offset=at["mixA"] + 32768)
    fr = sb("fr", [P, 2, SEQ], offset=at["rt"])
    fs = sb("fs", [P, 2, SEQ], offset=at["rt"] + 4096)
    xg = sb("xg", [P, TOK, 512], offset=at["rt"])
    gfin = sb("gfin", [P, D_MODEL], offset=at["st"])
    assert at["fT_lo"] + 32768 <= at["E_im"]
    ps = ctx.enter_context(nc.psum_tensor("ps", [P, 8, 512], F32))
    g1_col, g2_col, d_col = cols[:, 0:KT], cols[:, KT:2 * KT], cols[:, 2 * KT:2 * KT + UT]
    frow_dram = nc.dram_tensor("frow_dram", [N_HEADS, P, BIAS_W], F32, kind="Internal").ap()

    x_in = [sem(f"x_in{t}") for t in range(TOK)]; cols_in = sem("cols_in"); x_again = sem("x_again"); out_stored = sem("out_stored")
    consts_in = sem("consts_in"); prm_in = sem("prm_in"); gfin_in = sem("gfin_in")
    frow_out = sem("frow_out"); frow_done = sem("frow_done"); frow_mm = sem("frow_mm")
    bias_in = [sem(f"bias_in{i}") for i in range(2)]
    raw_in = [sem(f"raw_in{i}") for i in range(RING)]
    w_hi_done = sem("w_hi_done"); w_lo_done = sem("w_lo_done"); unit_used = sem("unit_used")
    ident_set = sem("ident_set"); tiles_set = sem("tiles_set")
    x_squared = [sem(f"x_squared{t}") for t in range(TOK)]; x_sq = sem("x_sq"); ms_sum = sem("ms_sum"); scale_ready = sem("scale_ready"); x_rt = sem("x_rt"); x_rstd = sem("x_rstd"); x_scaled = sem("x_scaled")
    turned = sem("turned"); hT_hi_done = sem("hT_hi_done"); hT_lo_done = sem("hT_lo_done")
    u_copied = sem("u_copied")
    nat_ready = sem("nat_ready"); nat_copied = sem("nat_copied"); nat_added = sem("nat_added")
    gates_done = sem("gates_done"); zt_used = sem("zt_used")
    cols_turned = sem("cols_turned"); cols_copied = sem("cols_copied")
    prep = sem("prep"); lam_dots = sem("lam_dots"); args_ready = sem("args_ready"); prm_ready = sem("prm_ready"); prm_copied = sem("prm_copied"); prep_act = sem("prep_act"); prm_turned = sem("prm_turned")
    table = sem("table"); bb_ready = sem("bb_ready"); bb_turned = sem("bb_turned")
    BT_ready = sem("BT_ready"); c_turned = sem("c_turned"); c_packed = sem("c_packed")
    bu_ready = sem("bu_ready"); bu_read = sem("bu_read"); ssm_step = sem("ssm_step"); states_done = sem("states_done")
    y_ready = sem("y_ready"); y_done = sem("y_done"); gelu_done = sem("gelu_done")
    gT_hi_done = sem("gT_hi_done"); gT_lo_done = sem("gT_lo_done")
    qk_copied = sem("qk_copied")
    score_ready = sem("score_ready"); score_read = sem("score_read"); nmax_ready = sem("nmax_ready")
    exp_done = sem("exp_done"); att_step = sem("att_step"); wT_ready = sem("wT_ready")
    wT_copied = sem("wT_copied"); pv_done = sem("pv_done"); o_squared = sem("o_squared")
    o_gated = sem("o_gated"); rsub_step = sem("rsub_step"); mixed_done = sem("mixed_done")
    f_relu = sem("f_relu"); f_hi_done = sem("f_hi_done")
    f_sq = sem("f_sq"); f_lo_done = sem("f_lo_done"); out_ready = sem("out_ready"); gained = sem("gained"); rows_gained = sem("rows_gained"); last_gained = sem("last_gained"); out_ready_hi = sem("out_ready_hi")

    NAT_OUT, NAT_END = 2 * TOK, 12 * TOK

    block = ctx.enter_context(nc.Block())

    def col_unit(w, c0):
        return w[:, c0:c0 + P].rearrange("(k p) n -> p k n", p=P)

    def row_unit(w, r0, c0):
        return w[r0:r0 + 2 * P, c0:c0 + 512].rearrange("(k p) n -> p k n", p=P)

    def unit_source(u):
        if u < U_V:
            return col_unit(w_in, COL_U + P * u)
        if u < U_GA:
            return row_unit(w_in, 256 * ((u - U_V) % 4), COL_V + 512 * ((u - U_V) // 4))
        if u < U_QK:
            return row_unit(w_in, 256 * ((u - U_GA) % 4), COL_GA + 512 * ((u - U_GA) // 4))
        if u < U_GS:
            return col_unit(w_in, ((u - U_QK) % 2) * COL_K + P * ((u - U_QK) // 2))
        if u < U_GLU:
            return row_unit(w_in, 256 * ((u - U_GS) % 4), COL_GS + 512 * ((u - U_GS) // 4))
        if u < U_OUT:
            c = (u - U_GLU) // 2
            return row_unit(w_glu, 256 * ((u - U_GLU) % 2), (1 - c % 2) * D_MODEL + 512 * (c // 2))
        if u < U_MLP:
            return row_unit(w_out, 256 * ((u - U_OUT) % 4), 512 * ((u - U_OUT) // 4))
        kind, quarter = MLP_ORDER[(u - U_MLP) // 8]
        n = (u - U_MLP) % 8
        if kind == "up":
            return col_unit(w1, 1024 * quarter + P * n)
        return row_unit(w2, 1024 * quarter + 256 * (n % 4), 512 * (n // 4))

    MLP_ORDER = [("up", 0), ("up", 1), ("down", 0), ("up", 2), ("down", 1), ("up", 3), ("down", 2), ("down", 3)]

    def last_unit(c):
        if c < 2:
            return U_V + 4 * c + 3
        if c < 4:
            return U_GA + 4 * (c - 2) + 3
        if c < 6:
            return U_GS + 4 * (c - 4) + 3
        if c < 10:
            return U_GLU + 2 * (c - 6) + 1
        if c < 12:
            return U_OUT + 4 * (c - 10) + 3
        step = MLP_ORDER.index(("down", (c - 12) // 2))
        return U_MLP + 8 * step + 4 * ((c - 12) % 2) + 3

    def gate_bank(c, t):
        return B_QK if c == 4 else t

    def turn_bank(g, k):
        return (B_T + k) % 8 if g == 0 else B_T + k % 4

    def wait_rows(eng, c, t):
        if t < TOK - 1:
            eng.wait_ge(nat_ready, (TOK - 1) * c + t + 1)
        else:
            eng.wait_ge(unit_used, last_unit(c) + 1)

    FIRST_D = 4

    def slot_parts(n):
        total = 3 * (PAIRS - FIRST_D)
        return [(FIRST_D + p // 3, p % 3) for p in range(total * n // BLOCKS, total * (n + 1) // BLOCKS)]

    def slot_units(n):
        h, i = n // TOK, n % TOK
        if i % 2 == 0 and h < N_HEADS - 1:
            return [U_QK + 2 * (h + 1) + i // 2 + 2]
        return {BLOCKS - 5: [U_GS + 2], BLOCKS - 1: [U_GS + 4, U_GS + 5]}.get(n, [])

    @block.sync
    def _(sp):
        for t in range(TOK):
            sp.dma_start(mixA[:, t, :], x[0, P * t:P * t + P, :]).then_inc(x_in[t], 16)

        def load_raw(u):
            if u >= RING:
                sp.wait_ge(w_lo_done, u - RING + 1)
            dst = raw[:, u % RING, :]
            src = unit_source(u)
            sp.dma_start(dst.rearrange("p (k n) -> p k n", k=src.shape[1]), src).then_inc(raw_in[u % RING], 16)

        def load_bias(h):
            if h >= 2:
                sp.wait_ge(score_read, 2 * TOK * (h - 1))
            else:
                sp.wait_ge(BT_ready, 4)
                sp.wait_ge(c_packed, 4)
                sp.wait_ge(table, 1)
                sp.wait_ge(frow_done, 16)
            src = bass.AP(frow_dram.tensor, h * P * BIAS_W + P - 1, [[BIAS_W - 1, P], [1, SEQ]])
            sp.dma_start(bias[:, h % 2, :], src).then_inc(bias_in[h % 2], 16)

        for u in range(RING):
            load_raw(u)
        for src, dst in ((ssm_log_dt[0].rearrange("(i two) -> i two", two=2), dtt[:, 0, :]),
                         (ssm_a_re[0].rearrange("(i two) s -> i (two s)", two=2), prm[:, 0, :]),
                         (ssm_a_im[0].rearrange("(i two) s -> i (two s)", two=2), prm[:, 1, :])):
            sp.dma_start(dst, src).then_inc(prm_in, 16)
        for src, dst in ((bass.AP(subln_g.tensor, 0, [[0, P], [1, V_DIM]]), gsub[:, :]),
                         (bass.AP(lambda_q1.tensor, 0, [[0, P], [1, HEAD_DIM]]), lamv[:, 0, 0, :]),
                         (bass.AP(lambda_k1.tensor, 0, [[0, P], [1, HEAD_DIM]]), lamv[:, 0, 1, :]),
                         (bass.AP(lambda_q2.tensor, 0, [[0, P], [1, HEAD_DIM]]), lamv[:, 1, 0, :]),
                         (bass.AP(lambda_k2.tensor, 0, [[0, P], [1, HEAD_DIM]]), lamv[:, 1, 1, :]),
                         (rel_bias, rb[:, :]), (onehot, oneh[:, :]),
                         (ssm_b_re[0].rearrange("(i two) s h -> (two s) i h", two=2), b_nat[:, 0, :, :]),
                         (ssm_b_im[0].rearrange("(i two) s h -> (two s) i h", two=2), b_nat[:, 1, :, :]),
                         (ssm_c_re[0].rearrange("(t g) h s -> (g h) t s", g=8), c_nat[:, 0, :, 0, :]),
                         (ssm_c_re[0].rearrange("(t g) h s -> (g h) t s", g=8), c_nat[:, 0, :, 1, :]),
                         (ssm_c_im[0].rearrange("(t g) h s -> (g h) t s", g=8), c_nat[:, 1, :, 0, :]),
                         (ssm_c_im[0].rearrange("(t g) h s -> (g h) t s", g=8), c_nat[:, 1, :, 1, :])):
            sp.dma_start(dst, src).then_inc(consts_in, 16)

        for u in range(RING, N_UNITS):
            load_raw(u)
            if u == U_GA + 4:
                load_bias(0)
                load_bias(1)
            if U_QK + 6 <= u < U_QK + 6 + 2 * (N_HEADS - 2) and u % 2 == 0:
                load_bias((u - U_QK - 6) // 2 + 2)
            if u == U_OUT:
                sp.wait_ge(y_done, UT)
                for t in range(TOK):
                    sp.dma_start(x2[:, t, :], x[0, P * t:P * t + P, :]).then_inc(x_again, 16)
                sp.dma_start(gfin[:, :], bass.AP(g_final.tensor, 0, [[0, P], [1, D_MODEL]])).then_inc(gfin_in, 16)
        for t in range(TOK):
            sp.wait_ge(out_ready, t + 1)
            sp.wait_ge(out_ready_hi, t + 1)
            sp.dma_start(out[0, P * t:P * t + P, :], x2[:, t, :]).then_inc(out_stored, 16)
        sp.wait_ge(out_stored, 16 * TOK)

    N_PRM, N_CONST, N_COLS = 3, 13, 3

    STEPS = 12

    def add_states(i, eng, add):
        eng.wait_ge(ssm_step, STEPS * i + 11)
        add(st[:, 0, :], rt[:, 0, :], rt[:, 2, :], ALU.subtract).then_inc(states_done, 1)
        eng.wait_ge(ssm_step, STEPS * i + 12)
        add(st[:, 1, :], st[:, 1, :], rt[:, 3, :], ALU.add).then_inc(states_done, 1)

    def gain_rows(eng, mult, t, done):
        eng.wait_ge(nat_added, NAT_END - TOK + t + 1)
        mult(xg[:, t, :], x2[:, t, 512:1024], gfin[:, 512:1024], ALU.mult).then_inc(done, 1)

    @block.gpsimd
    def _(pool):
        nc.gpsimd.memset(ident[:, :], 0.0).then_inc(ident_set, 1)
        nc.gpsimd.memset(eps_t[:, :], EPS).then_inc(tiles_set, 1)
        nc.gpsimd.memset(halfpi[:, :], math.pi / 2).then_inc(tiles_set, 1)
        pool.wait_ge(ident_set, 1)
        nc.gpsimd.affine_select(out=ident[:, :], in_=ident[:, :], compare_op=ALU.not_equal, fill=1.0,
                                base=0, pattern=[[-1, P]], channel_multiplier=1).then_inc(ident_set, 1)
        nc.gpsimd.memset(bb[:, :, :, :], 0.0).then_inc(tiles_set, 1)
        nc.gpsimd.memset(CT[:, :, :, :, :], 0.0).then_inc(tiles_set, 1)
        nc.gpsimd.memset(E_re[:, :, 0:1], 1.0).then_inc(tiles_set, 1)
        nc.gpsimd.memset(E_im[:, :, 0:1], 0.0).then_inc(tiles_set, 1)
        def split_lo(u):
            pool.wait_ge(w_hi_done, u + 1)
            nc.gpsimd.tensor_tensor(w_lo[:, u % RING, :], raw[:, u % RING, :],
                                    w_hi[:, u % RING, :].bitcast(F32), ALU.subtract).then_inc(w_lo_done, 1)

        for u in range(U_QK + 4):
            split_lo(u)
        for n in range(BLOCKS):
            for u in slot_units(n):
                split_lo(u)
            for i, part in slot_parts(n):
                if part == 2 and i < PAIRS - 1:
                    add_states(i, pool, nc.gpsimd.tensor_tensor)
            if n == BLOCKS - 5:
                split_lo(U_GS + 3)
        for u in range(U_GS + 6, N_UNITS):
            split_lo(u)
        pool.wait_ge(gfin_in, 16)
        for t in range(TOK - 1):
            gain_rows(pool, nc.gpsimd.tensor_tensor, t, rows_gained)

    @block.scalar
    def _(act):
        def col(src):
            return src.rearrange("(k p) -> k p", p=P)

        for src, dst in ((col(g_mix[0]), cols_nat[0:KT, :]), (col(g_mlp[0]), cols_nat[KT:2 * KT, :]),
                         (col(ssm_d[0]), cols_nat[2 * KT:, :])):
            act.dma_start(dst, src).then_inc(cols_in, 16)

        act.wait_ge(tiles_set, 2)
        nc.scalar.activation(osq[:, 0:1], eps_t[:, :], ACT.Sqrt)
        for t in range(TOK):
            if t % 2 == 0:
                act.wait_ge(x_in[t], 16)
                nc.scalar.activation(V[:, t, :], mixA[:, t, :], ACT.Square,
                                     accum_out=ms[:, 0, 0, t:t + 1]).then_inc(x_squared[t], 1)
            if t == 2:
                act.wait_ge(cols_turned, 1)
                nc.scalar.activation(cols[:, :], ps[:, 0, 0:2 * KT + UT], ACT.Identity).then_inc(cols_copied, 1)
            act.wait_ge(x_squared[t], 1)
            nc.scalar.activation(ms[:, 0, 1, t:t + 1], ms[:, 0, 0, t:t + 1], ACT.Sqrt, bias=eps_t[:, :],
                                 scale=1.0 / D_MODEL).then_inc(x_rt, 1)

        def split_hi(u):
            if u >= N_UNITS:
                return
            act.wait_ge(raw_in[u % RING], 16 * (u // RING + 1))
            if u >= RING:
                act.wait_ge(unit_used, u - RING + 1)
            nc.scalar.activation(w_hi[:, u % RING, :], raw[:, u % RING, :], ACT.Identity).then_inc(w_hi_done, 1)

        def turn_hi(g, k, gain):
            act.wait_ge(turned, KT * g + k + 1)
            kw = {} if gain is None else {"scale": gain[:, k:k + 1]}
            nc.scalar.activation(hT_hi[:, k, :], ps[:, turn_bank(g, k), :], ACT.Identity, **kw).then_inc(hT_hi_done, 1)

        split_hi(0)
        act.wait_ge(cols_copied, 1)
        for k in range(KT):
            turn_hi(0, k, g1_col)
            if k == 2:
                split_hi(1)
        for u in range(U_SSM, U_V):
            split_hi(u + 2)
            if u == 0:
                act.wait_ge(prm_in, 16 * N_PRM)
                nc.scalar.activation(dtt[:, 1, :], dtt[:, 0, :], ACT.Exp).then_inc(prep_act, 1)
                act.wait_ge(args_ready, 1)
                nc.scalar.activation(prm[:, 4, :], prm[:, 2, :], ACT.Exp).then_inc(prep_act, 1)
                act.wait_ge(lam_dots, 2)
                nc.scalar.activation(nlam[:, 2:4], nlam[:, 0:2], ACT.Exp).then_inc(prep_act, 1)
            if u == 1:
                act.wait_ge(args_ready, 3)
                nc.scalar.activation(prm[:, 6, :], prm[:, 8, :], ACT.Sin).then_inc(prep_act, 1)
                nc.scalar.activation(prm[:, 5, :], prm[:, 9, :], ACT.Sin, bias=halfpi[0:PAIRS, :],
                                     scale=-1.0).then_inc(prep_act, 1)
            act.wait_ge(unit_used, U_SSM + u + 1)
            nc.scalar.activation(uT[:, u, :], ps[:, 4 + u, :], ACT.Identity).then_inc(u_copied, 1)
        act.wait_ge(frow_out, 2)
        act.dma_start(frow_dram, frow[:, :].unsqueeze(1).to_broadcast([N_HEADS, P, BIAS_W])).then_inc(frow_done, 16)

        def copy_c():
            for ri in range(2):
                act.wait_ge(c_turned, ri + 1)
                for g2 in range(2):
                    rows = slice(64 * g2, 64 * g2 + 64)
                    src = ps[rows, 4 + ri, :].rearrange("p (t j g h) -> p (t j) g h", t=UT, g=2, h=SSM_GROUP)
                    nc.scalar.activation(c_pk[rows, ri, :, :], src[:, :, g2, :], ACT.Identity).then_inc(c_packed, 1)

        def copy_bb(half):
            for n in (2 * half, 2 * half + 1):
                act.wait_ge(bb_turned, n + 1)
                nc.scalar.activation(BT[:, n // 2, n % 2, :, :].rearrange("p t s -> p (t s)"),
                                     ps[:, 6 + n % 2, :], ACT.Identity).then_inc(BT_ready, 1)

        for u in range(U_V, U_QK):
            split_hi(u + 2)
            c, last = (u - U_V) // 4, (u - U_V) % 4 == 3
            if u == U_V + 4:
                copy_c()
                copy_bb(0)
            if u == U_GA:
                copy_bb(1)
            if last:
                for t in range(TOK):
                    wait_rows(act, c, t)
                    if c < 2:
                        nc.scalar.activation(V[:, t, 512 * c:512 * c + 512], ps[:, t, :],
                                             ACT.Identity).then_inc(nat_copied, 1)
                    else:
                        if c == 2:
                            act.wait_ge(table, 1)
                        nc.scalar.activation(mixA[:, t, 512 * (c - 2):512 * (c - 1)], ps[:, t, :], ACT.Tanh,
                                             scale=0.5).then_inc(nat_copied, 1)

        def copy_qk(v):
            act.wait_ge(unit_used, U_QK + v + 1)
            h = v // 2
            if h >= 2:
                act.wait_ge(score_ready, TOK * (h - 1))
            if v == 0:
                act.wait_ge(table, 1)
                act.wait_ge(frow_done, 16)
            dst = (qT, kT)[v % 2][:, h % 2, :]
            nc.scalar.activation(dst, ps[:, B_QK, :], ACT.Identity,
                                 scale=(HEAD_DIM ** -0.5 if v % 2 == 0 else 1.0)).then_inc(qk_copied, 1)

        def exps(n):
            L = P * (n % TOK + 1)
            act.wait_ge(nmax_ready, n + 1)
            for m in range(2):
                nc.scalar.activation(Pm[:, n % 2, m, 0:L], Pm[:, n % 2, m, 0:L], ACT.Exp,
                                     bias=nmx[:, n % 2, m:m + 1],
                                     accum_out=sums[:, n % 2, m:m + 1]).then_inc(exp_done, 1)

        def copy_wT(n):
            L = P * (n % TOK + 1)
            act.wait_ge(wT_ready, n + 1)
            if n >= 2:
                act.wait_ge(pv_done, n - 1)
            nc.scalar.activation(wT[:, n % 2, 0:L], ps[:, B_WT, 0:L], ACT.Identity).then_inc(wT_copied, 1)

        def square_o(h):
            act.wait_ge(pv_done, TOK * (h + 1))
            for i in range(TOK):
                n = TOK * h + i
                if n >= 1:
                    act.wait_ge(o_squared, n)
                nc.scalar.activation(osq[:, :], ps[:, B_O, P * i:P * i + P], ACT.Square,
                                     scale=rinv[:, n % 8, 0:1],
                                     accum_out=ssq[:, i, h:h + 1]).then_inc(o_squared, 1)

        def gate_tanh(c, t):
            wait_rows(act, c, t)
            nc.scalar.activation(mixS[:, t, 512 * (c - 4):512 * (c - 3)], ps[:, gate_bank(c, t), :], ACT.Tanh,
                                 scale=0.5).then_inc(nat_copied, 1)

        for v in range(2):
            split_hi(U_QK + v + 2)
            copy_qk(v)
        for n in range(BLOCKS + 2):
            h, i = n // TOK, n % TOK
            if n < BLOCKS:
                exps(n)
                for u in slot_units(n):
                    split_hi(u)
            if i == 1 and h >= 1:
                square_o(h - 1)
            if 1 <= n <= BLOCKS:
                copy_wT(n - 1)
            if i % 2 == 1 and h < N_HEADS - 1:
                copy_qk(2 * (h + 1) + i // 2)
            if n == BLOCKS - 5:
                split_hi(U_GS + 3)
            if h == N_HEADS - 1:
                gate_tanh(4, i)

        act.wait_ge(o_squared, BLOCKS)
        nc.scalar.activation(ssq[:, :, :], ssq[:, :, :], ACT.Sqrt, bias=eps_t[:, :],
                             scale=1.0 / V_DIM).then_inc(rsub_step, 1)
        for u in range(U_GS + 4, U_GLU):
            split_hi(u + 2)
            if u == U_GS + 4:
                for k in range(UT):
                    act.wait_ge(y_done, k + 1)
                    nc.scalar.activation(uT[:, k, :], uT[:, k, :], ACT.Gelu_apprx_tanh).then_inc(gelu_done, 1)
                for k in range(UT):
                    act.wait_ge(gelu_done, k + 1)
                    nc.scalar.activation(gT_hi[:, k, :], uT[:, k, :], ACT.Identity).then_inc(gT_hi_done, 1)
        for t in range(TOK):
            gate_tanh(5, t)
        for u in range(U_GLU, U_OUT):
            split_hi(u + 2)
            c = 6 + (u - U_GLU) // 2
            if u == U_GLU + 6:
                for k in range(0, 4):
                    turn_hi(1, k, None)
            if (u - U_GLU) % 4 == 1:
                for t in range(TOK):
                    n = TOK * ((c - 6) // 2) + t
                    wait_rows(act, c, t)
                    if n >= 2:
                        act.wait_ge(zt_used, n - 1)
                    nc.scalar.activation(zt[:, n % 2, :], ps[:, t, :], ACT.Tanh, scale=0.5).then_inc(nat_copied, 1)

        for u in range(U_OUT, U_MLP):
            split_hi(u + 2)
            if u == U_OUT + 1:
                for k in range(4, 8):
                    turn_hi(1, k, None)
            if u == U_OUT + 6:
                for k in range(0, 4):
                    turn_hi(2, k, g2_col)
        for k in range(4, 8):
            turn_hi(2, k, g2_col)

        def half_stats(g, half, t, count, before):
            act.wait_ge(nat_added, count)
            if before:
                act.wait_ge(x_sq, before)
            nc.scalar.activation(junk[:, 0:512], x2[:, t, 512 * half:512 * half + 512], ACT.Square,
                                 accum_out=ms[:, g, half, t:t + 1]).then_inc(x_sq, 1)

        f = 0
        for step, (kind, quarter) in enumerate(MLP_ORDER):
            for n in range(8):
                u = U_MLP + 8 * step + n
                split_hi(u + 2)
                if kind == "up":
                    act.wait_ge(unit_used, u + 1)
                    if f >= 2:
                        act.wait_ge(f_sq, f - 1)
                        act.wait_ge(f_hi_done, f - 1)
                    nc.scalar.activation(fr[:, f % 2, :], ps[:, B_T + f % 4, :], ACT.Relu).then_inc(f_relu, 1)
                    act.wait_ge(f_relu, f + 1)
                    if quarter >= 2 and n == 0:
                        act.wait_ge(unit_used, U_MLP + 8 * (MLP_ORDER.index(("down", quarter - 2)) + 1))
                    nc.scalar.activation(fT_hi[:, quarter % 2, n, :], fr[:, f % 2, :],
                                         ACT.Square).then_inc(f_hi_done, 1)
                    f += 1
                    if quarter == 0 and n >= 4:
                        t = n - 4
                        for half in range(2):
                            half_stats(1, half, t, 4 * TOK, 2 * t + half)
                        if t == 3:
                            act.wait_ge(x_sq, 2 * TOK)
                            act.wait_ge(ms_sum, 1)
                            nc.scalar.activation(ms[:, 1, 1, :], ms[:, 1, 1, :], ACT.Identity, bias=eps_t[:, :],
                                                 scale=1.0 / D_MODEL).then_inc(x_rt, 1)
        for t in range(TOK):
            half_stats(2, 0, t, NAT_END - TOK, 2 * TOK + t)
        act.wait_ge(x_sq, 3 * TOK)
        nc.scalar.activation(ms[:, 2, 0, :], ms[:, 2, 0, :], ACT.Identity, bias=eps_t[:, :],
                             scale=1.0 / D_MODEL).then_inc(x_rt, 1)
        nc.scalar.activation(osq[:, 0:1], eps_t[:, :], ACT.Sqrt)
        def scale_out(t):
            act.wait_ge(x_rstd, TOK + t + 1)
            act.wait_ge(gained, t + 1)
            nc.scalar.activation(x2[:, t, 0:512], x2[:, t, 0:512], ACT.Identity,
                                 scale=rstd[:, 2, t:t + 1]).then_inc(out_ready, 1)

        for t in range(TOK):
            half_stats(2, 1, t, NAT_END - TOK + t + 1, 3 * TOK + t)
            if t:
                scale_out(t - 1)
            act.wait_ge(x_sq, 3 * TOK + t + 1)
            act.wait_ge(x_rt, TOK + 2)
            nc.scalar.activation(ms[:, 2, 1, t:t + 1], ms[:, 2, 1, t:t + 1], ACT.Sqrt,
                                 bias=ms[:, 2, 0, t:t + 1], scale=1.0 / D_MODEL).then_inc(x_rt, 1)
        scale_out(TOK - 1)

    @block.vector
    def _(dve):
        steps = [0]

        def link(ins):
            steps[0] += 1
            ins.then_inc(prep, 1)

        def settle():
            dve.wait_ge(prep, steps[0])

        TT, TS, STT = nc.vector.tensor_tensor, nc.vector.tensor_scalar, nc.vector.scalar_tensor_tensor

        def turn_lo(g, k, gain):
            dve.wait_ge(hT_hi_done, KT * g + k + 1)
            src, hi = ps[:, turn_bank(g, k), :], hT_hi[:, k, :].bitcast(F32)
            if gain is None:
                ins = TT(hT_lo[:, k, :], src, hi, ALU.subtract)
            else:
                ins = STT(out=hT_lo[:, k, :], in0=src, scalar=gain[:, k:k + 1], in1=hi,
                          op0=ALU.mult, op1=ALU.subtract)
            ins.then_inc(hT_lo_done, 1)

        def x_square(t):
            dve.wait_ge(x_in[t], 16)
            nc.vector.tensor_tensor_reduce(out=V[:, t, :], in0=mixA[:, t, :], in1=mixA[:, t, :], scale=1.0,
                                           scalar=0.0, op0=ALU.mult, op1=ALU.add,
                                           accum_out=ms[:, 0, 0, t:t + 1]).then_inc(x_squared[t], 1)

        def x_scale(t):
            dve.wait_ge(x_rt, t + 1)
            nc.vector.reciprocal(rstd[:, 0, t:t + 1], ms[:, 0, 1, t:t + 1]).then_inc(x_rstd, 1)
            dve.wait_ge(x_rstd, t + 1)
            TS(mixA[:, t, :], mixA[:, t, :], rstd[:, 0, t:t + 1], None, ALU.mult).then_inc(x_scaled, 1)

        x_square(1)
        x_scale(0)
        x_scale(1)
        x_square(3)
        x_scale(2)
        x_scale(3)
        dve.wait_ge(cols_copied, 1)
        for k in range(KT):
            turn_lo(0, k, g1_col)

        def prow(i):
            return prm[:, i, :]

        A_RE, A_IM, A_DT, TH, MAG, COS, SIN, TURNS, RED, ABS, LR, LI, DEN, T0, T1, CR, CI = range(17)
        dt_b = dtt[:, 1, :].unsqueeze(2).to_broadcast([PAIRS, 2, SSM_STATE])

        def by_group(i):
            return prow(i).rearrange("i (two s) -> i two s", two=2)

        dve.wait_ge(prep_act, 1)
        TT(by_group(A_DT), by_group(A_RE), dt_b, ALU.mult).then_inc(args_ready, 1)
        link(TT(by_group(TH), by_group(A_IM), dt_b, ALU.mult))
        settle()
        dve.wait_ge(consts_in, 16 * N_CONST)
        for j in range(2):
            link(TT(lamv[:, j, 0, :], lamv[:, j, 0, :], lamv[:, j, 1, :], ALU.mult))
        settle()
        for j in range(2):
            nc.vector.tensor_reduce(nlam[:, j:j + 1], lamv[:, j, 0, :], mybir.AxisListType.X,
                                    ALU.add).then_inc(lam_dots, 1)
        link(TS(gsub[:, :], gsub[:, :], (1.0 - LAM_INIT) * 0.5, None, ALU.mult))

        BIG = 1.5 * 2.0 ** 23
        C1 = 6.28125
        C2 = float(np.float32(np.round((2 * math.pi - C1) * 2.0 ** 20) / 2.0 ** 20))
        C3 = float(np.float32(2 * math.pi - C1 - C2))
        link(TS(prow(TURNS), prow(TH), 1.0 / (2 * math.pi), BIG, ALU.mult, ALU.add))
        settle()
        link(TS(prow(TURNS), prow(TURNS), -BIG, None, ALU.add))
        settle()
        link(STT(out=prow(RED), in0=prow(TURNS), scalar=-C1, in1=prow(TH), op0=ALU.mult, op1=ALU.add))
        settle()
        link(STT(out=prow(RED), in0=prow(TURNS), scalar=-C2, in1=prow(RED), op0=ALU.mult, op1=ALU.add))
        settle()
        link(STT(out=prow(RED), in0=prow(TURNS), scalar=-C3, in1=prow(RED), op0=ALU.mult, op1=ALU.add))
        settle()
        TS(prow(RED), prow(RED), 3.1415925, -3.1415925, ALU.min, ALU.max).then_inc(args_ready, 1)
        dve.wait_ge(args_ready, 2)
        STT(out=prow(ABS), in0=prow(RED), scalar=-1.0, in1=prow(RED), op0=ALU.mult,
            op1=ALU.max).then_inc(args_ready, 1)
        link(TT(prow(T0), prow(A_RE), prow(A_RE), ALU.mult))
        link(TT(prow(T1), prow(A_IM), prow(A_IM), ALU.mult))
        settle()
        link(TT(prow(DEN), prow(T0), prow(T1), ALU.add))
        settle()
        link(nc.vector.reciprocal(prow(DEN), prow(DEN)))
        dve.wait_ge(prep_act, 5)
        link(TT(prow(LR), prow(MAG), prow(COS), ALU.mult))
        link(TT(prow(LI), prow(MAG), prow(SIN), ALU.mult))
        settle()
        link(TS(prow(LR), prow(LR), -1.0, None, ALU.add))
        settle()
        link(TT(prow(T0), prow(LR), prow(A_RE), ALU.mult))
        link(TT(prow(T1), prow(LI), prow(A_IM), ALU.mult))
        settle()
        link(TT(prow(CR), prow(T0), prow(T1), ALU.add))
        settle()
        link(TT(prow(T0), prow(LI), prow(A_RE), ALU.mult))
        link(TT(prow(T1), prow(LR), prow(A_IM), ALU.mult))
        settle()
        link(TT(prow(CI), prow(T0), prow(T1), ALU.subtract))
        link(TT(prow(CR), prow(CR), prow(DEN), ALU.mult))
        settle()
        link(TT(prow(CI), prow(CI), prow(DEN), ALU.mult))
        settle()
        nc.vector.sem_inc(prm_ready, 1)
        dve.wait_ge(prm_turned, 1)
        nc.vector.tensor_copy(mag[:, :, :].rearrange("p a i -> p (a i)"), ps[:, 4, 0:5 * PAIRS]).then_inc(prm_copied, 1)
        dve.wait_ge(prm_copied, 1)

        dve.wait_ge(frow_mm, 1)
        TS(frow[:, 0:512], ps[0:N_HEADS, 5, :], 1.0, None, ALU.mult).then_inc(frow_out, 1)
        TS(frow[:, 512:BIAS_W], ps[0:N_HEADS, 6, 0:BIAS_W - 512], 0.0, MASKED, ALU.mult, ALU.add).then_inc(frow_out, 1)

        link(TT(nlam[:, 0:1], nlam[:, 3:4], nlam[:, 2:3], ALU.subtract))
        settle()
        link(TS(nlam[:, 0:1], nlam[:, 0:1], -LAM_INIT, None, ALU.add))

        def coef_b(half):
            cr = coef[:, half, 0, :].unsqueeze(2).to_broadcast([P, PAIRS, SSM_GROUP])
            ci = coef[:, half, 1, :].unsqueeze(2).to_broadcast([P, PAIRS, SSM_GROUP])
            if half:
                dve.wait_ge(bb_turned, 2)
            else:
                dve.wait_ge(tiles_set, 3)
            link(TT(bt[:, 0, :, :], b_nat[:, 0, :, :], cr, ALU.mult))
            link(TT(bt[:, 1, :, :], b_nat[:, 1, :, :], ci, ALU.mult))
            link(TT(bt[:, 2, :, :], b_nat[:, 1, :, :], cr, ALU.mult))
            link(TT(bt[:, 3, :, :], b_nat[:, 0, :, :], ci, ALU.mult))
            settle()
            for ri in range(2):
                for g2 in range(2):
                    rows, cols = slice(64 * g2, 64 * g2 + 64), slice(16 * g2, 16 * g2 + 16)
                    TT(bb[rows, ri, :, cols], bt[rows, 2 * ri, :, :], bt[rows, 2 * ri + 1, :, :],
                       (ALU.subtract, ALU.add)[ri]).then_inc(bb_ready, 1)

        link(nc.vector.tensor_copy(coef[:, 0, :, :], mag[:, 3:5, :]))
        link(nc.vector.tensor_copy(pw[:, 0, :, :], mag[:, 1:3, :]))
        settle()
        coef_b(0)

        dve.wait_ge(tiles_set, 6)
        dve.wait_ge(turned, KT)
        levels = HALF.bit_length() - 1
        for lv in range(levels):
            n = 1 << lv
            p_re, p_im = pw[:, lv % 2, 0, :], pw[:, lv % 2, 1, :]
            q_re, q_im = pw[:, (lv + 1) % 2, 0, :], pw[:, (lv + 1) % 2, 1, :]
            pr = p_re.unsqueeze(2).to_broadcast([P, PAIRS, n])
            pi = p_im.unsqueeze(2).to_broadcast([P, PAIRS, n])
            a, b = em[:, 0, :, 0:n], em[:, 1, :, 0:n]
            link(TT(a, E_re[:, :, 0:n], pr, ALU.mult))
            link(TT(b, E_im[:, :, 0:n], pi, ALU.mult))
            link(TT(pwt[:, 0, :], p_re, p_re, ALU.mult))
            link(TT(pwt[:, 1, :], p_im, p_im, ALU.mult))
            link(STT(out=q_im, in0=p_re, scalar=2.0, in1=p_im, op0=ALU.mult, op1=ALU.mult))
            settle()
            link(TT(E_re[:, :, n:2 * n], a, b, ALU.subtract))
            link(TT(q_re, pwt[:, 0, :], pwt[:, 1, :], ALU.subtract))
            settle()
            link(TT(a, E_re[:, :, 0:n], pi, ALU.mult))
            link(TT(b, E_im[:, :, 0:n], pr, ALU.mult))
            settle()
            link(TT(E_im[:, :, n:2 * n], a, b, ALU.add))
            settle()
        p_re, p_im = pw[:, levels % 2, 0, :], pw[:, levels % 2, 1, :]
        c_re, c_im = coef[:, 0, 0, :], coef[:, 0, 1, :]
        link(TT(pwt[:, 0, :], c_re, p_re, ALU.mult))
        link(TT(pwt[:, 1, :], c_im, p_im, ALU.mult))
        link(TT(pwt[:, 2, :], c_im, p_re, ALU.mult))
        link(TT(pwt[:, 3, :], c_re, p_im, ALU.mult))
        settle()
        link(TT(coef[:, 1, 0, :], pwt[:, 0, :], pwt[:, 1, :], ALU.add))
        link(TT(coef[:, 1, 1, :], pwt[:, 2, :], pwt[:, 3, :], ALU.subtract))
        settle()
        coef_b(1)
        dve.wait_ge(c_packed, 4)
        pr = p_re.unsqueeze(2).to_broadcast([P, PAIRS, SSM_GROUP])
        pi = p_im.unsqueeze(2).to_broadcast([P, PAIRS, SSM_GROUP])
        dve.wait_ge(bb_ready, 8)
        settle()
        link(TT(bt[:, 0, :, :], c_pk[:, 0, :, :], pr, ALU.mult))
        link(TT(bt[:, 1, :, :], c_pk[:, 1, :, :], pi, ALU.mult))
        link(TT(bt[:, 2, :, :], c_pk[:, 0, :, :], pi, ALU.mult))
        link(TT(bt[:, 3, :, :], c_pk[:, 1, :, :], pr, ALU.mult))
        settle()
        for g2 in range(2):
            rows, cols = slice(64 * g2, 64 * g2 + 64), slice(16 * g2, 16 * g2 + 16)
            link(TS(CT[rows, :, 0, 0, cols], c_pk[rows, 0, :, :], 1.0, None, ALU.mult))
            link(TS(CT[rows, :, 0, 1, cols], c_pk[rows, 1, :, :], -1.0, None, ALU.mult))
            link(TT(CT[rows, :, 1, 0, cols], bt[rows, 0, :, :], bt[rows, 1, :, :], ALU.subtract))
            link(STT(out=CT[rows, :, 1, 1, cols], in0=bt[rows, 2, :, :], scalar=-1.0, in1=bt[rows, 3, :, :],
                     op0=ALU.mult, op1=ALU.subtract))
        settle()
        nc.vector.sem_inc(table, 1)

        def halves(ap):
            return ap.rearrange("p (c j) -> p c j", c=2)

        def ssm_part(i, part):
            def done(k):
                dve.wait_ge(ssm_step, STEPS * i + k)

            er = E_re[:, i:i + 1, :].to_broadcast([P, 2, HALF])
            ei = E_im[:, i:i + 1, :].to_broadcast([P, 2, HALF])
            t = [halves(rt[:, k, :]) for k in range(4)]
            s = [halves(st[:, k, :]) for k in range(2)]
            if part == 0:
                dve.wait_ge(bu_ready, i + 1)
                done(0)
                if i:
                    dve.wait_ge(states_done, 2 * i)
                b_re, b_im = halves(ps[:, B_BU, :]), halves(ps[:, B_BU + 1, :])
                TT(t[0], b_re, er, ALU.mult).then_inc(ssm_step, 1)
                TT(t[1], b_im, ei, ALU.mult).then_inc(ssm_step, 1)
                TT(t[2], b_im, er, ALU.mult).then_inc(ssm_step, 1)
                TT(t[3], b_re, ei, ALU.mult).then_inc(ssm_step, 1)
            elif part == 1:
                done(2)
                TT(t[0], t[0], t[1], ALU.add).then_inc(ssm_step, 1)
                done(4)
                TT(t[2], t[2], t[3], ALU.subtract).then_inc(ssm_step, 1)
                decay = mag[:, 0, i:i + 1].to_broadcast([P, SEQ])
                for k in range(2):
                    done(5 + k)
                    nc.vector.tensor_tensor_scan(rt[:, 2 * k + 1, :], decay, rt[:, 2 * k, :], 0.0,
                                                 ALU.mult, ALU.add).then_inc(ssm_step, 1)
            else:
                if i:
                    dve.wait_ge(y_ready, i)
                done(7)
                TT(t[0], t[1], er, ALU.mult).then_inc(ssm_step, 1)
                TT(s[1], t[1], ei, ALU.mult).then_inc(ssm_step, 1)
                done(8)
                TT(t[2], t[3], ei, ALU.mult).then_inc(ssm_step, 1)
                TT(t[3], t[3], er, ALU.mult).then_inc(ssm_step, 1)

        def y_skip(ut):
            dve.wait_ge(y_ready, 4 * ut + 4)
            STT(out=uT[:, ut, :], in0=uT[:, ut, :], scalar=d_col[:, ut:ut + 1], in1=ps[:, B_Y, :],
                op0=ALU.mult, op1=ALU.add).then_inc(y_done, 1)

        def gate_a(c):
            for t in range(TOK):
                dve.wait_ge(nat_copied, TOK * (2 + c) + t + 1)
                g = mixA[:, t, 512 * c:512 * c + 512].rearrange("p (h v) -> p h v", v=V_DIM)
                STT(out=g, in0=g, scalar=1.0, in1=gsub[:, :].unsqueeze(1).to_broadcast([P, 4, V_DIM]),
                    op0=ALU.add, op1=ALU.mult).then_inc(gates_done, 1)

        for i in range(FIRST_D):
            for part in range(3):
                ssm_part(i, part)
            add_states(i, dve, TT)
            if i % 2:
                gate_a(i // 2)

        def pre(n):
            h, i = n // TOK, n % TOK
            L = P * (i + 1)
            dve.wait_ge(score_ready, n + 1)
            dve.wait_ge(bias_in[h % 2], 16 * (h // 2 + 1))
            if n >= 2:
                dve.wait_ge(wT_ready, n - 1)
            for m in range(2):
                nc.vector.tensor_tensor_reduce(
                    out=Pm[:, n % 2, m, 0:L], in0=ps[:, B_SCORE + m, 0:L],
                    in1=bias[:, h % 2, SEQ - L:SEQ], scale=1.0, scalar=-3e38,
                    op0=ALU.add, op1=ALU.max, accum_out=mx[:, n % 2, m:m + 1]).then_inc(score_read, 1)
            dve.wait_ge(score_read, 2 * n + 2)
            TS(nmx[:, n % 2, :], mx[:, n % 2, :], -1.0, None, ALU.mult).then_inc(nmax_ready, 1)

        def post(n):
            L = P * (n % TOK + 1)
            dve.wait_ge(exp_done, 2 * n + 2)
            nc.vector.reciprocal(rinv[:, n % 8, :], sums[:, n % 2, :]).then_inc(att_step, 1)
            dve.wait_ge(att_step, 3 * n + 1)
            STT(out=cfac[:, n % 2, :], in0=rinv[:, n % 8, 1:2], scalar=sums[:, n % 2, 0:1], in1=nlam[:, 0:1],
                op0=ALU.mult, op1=ALU.mult).then_inc(att_step, 1)
            dve.wait_ge(att_step, 3 * n + 2)
            STT(out=Pm[:, n % 2, 0, 0:L], in0=Pm[:, n % 2, 1, 0:L], scalar=cfac[:, n % 2, :],
                in1=Pm[:, n % 2, 0, 0:L], op0=ALU.mult, op1=ALU.add).then_inc(att_step, 1)

        def gate_o(h):
            dve.wait_ge(o_squared, TOK * (h + 1))
            for i in range(TOK):
                n = TOK * h + i
                g = mixA[:, i, V_DIM * h:V_DIM * h + V_DIM]
                STT(out=g, in0=ps[:, B_O, P * i:P * i + P], scalar=rinv[:, n % 8, 0:1], in1=g,
                    op0=ALU.mult, op1=ALU.mult).then_inc(o_gated, 1)

        dve.wait_ge(gates_done, 2 * TOK)
        for n in range(BLOCKS + 2):
            h, i = n // TOK, n % TOK
            if n < BLOCKS:
                pre(n)
                for pair, part in slot_parts(n):
                    ssm_part(pair, part)
                    if part == 2 and pair == PAIRS - 1:
                        add_states(pair, dve, TT)
                    if part == 2 and pair % 4 == 0:
                        y_skip(pair // 4 - 1)
                post(n)
            if i == 1 and h >= 1:
                gate_o(h - 1)

        def gate_s(c):
            for t in range(TOK):
                dve.wait_ge(nat_copied, TOK * (4 + c) + t + 1)
                g = mixS[:, t, 512 * c:512 * c + 512]
                TS(g, g, 0.25, 0.25, ALU.mult, ALU.add).then_inc(gates_done, 1)

        y_skip(UT - 1)
        gate_s(0)
        for k in range(UT):
            dve.wait_ge(gT_hi_done, k + 1)
            TT(gT_lo[:, k, :], uT[:, k, :], gT_hi[:, k, :].bitcast(F32), ALU.subtract).then_inc(gT_lo_done, 1)
        gate_s(1)

        for half in range(2):
            cols = slice(512 * half, 512 * half + 512)
            for t in range(TOK):
                n = TOK * half + t
                dve.wait_ge(nat_copied, TOK * (6 + half) + t + 1)
                dve.wait_ge(gates_done, 4 * TOK)
                STT(out=mixS[:, t, cols], in0=zt[:, n % 2, :], scalar=1.0, in1=mixS[:, t, cols],
                    op0=ALU.add, op1=ALU.mult).then_inc(zt_used, 1)
            if half:
                for k in range(0, 4):
                    turn_lo(1, k, None)
            else:
                dve.wait_ge(rsub_step, 1)
                nc.vector.reciprocal(rsub[:, :, :], ssq[:, :, :]).then_inc(rsub_step, 1)
            for t in range(TOK):
                wait_rows(dve, (7 + 2 * half), t)
                dve.wait_ge(zt_used, TOK * half + t + 1)
                TT(mixS[:, t, cols], ps[:, t, :], mixS[:, t, cols], ALU.mult).then_inc(nat_added, 1)
            dve.wait_ge(rsub_step, 2)
            dve.wait_ge(o_gated, BLOCKS)
            for t in range(TOK):
                dve.wait_ge(nat_added, TOK * half + t + 1)
                for h in range(4 * half, 4 * half + 4):
                    hc = slice(V_DIM * h, V_DIM * h + V_DIM)
                    STT(out=mixA[:, t, hc], in0=mixA[:, t, hc], scalar=rsub[:, t, h:h + 1], in1=mixS[:, t, hc],
                        op0=ALU.mult, op1=ALU.add).then_inc(mixed_done, 1)
        for k in range(4, 8):
            turn_lo(1, k, None)

        dve.wait_ge(x_again, 16 * TOK)

        def add_chunk(c, index):
            for t in range(TOK):
                add_rows(c, index, t)

        def add_rows(c, index, t):
            wait_rows(dve, c, t)
            if index > 3:
                dve.wait_ge(nat_added, TOK * (index - 2) + t + 1)
            cols = slice(512 * (c % 2), 512 * (c % 2) + 512)
            if c < 12:
                ins = TT(x2[:, t, cols], x2[:, t, cols], ps[:, t, :], ALU.add)
            else:
                ins = STT(out=x2[:, t, cols], in0=ps[:, t, :], scalar=rstd2[:, t:t + 1], in1=x2[:, t, cols],
                          op0=ALU.mult, op1=ALU.add)
            ins.then_inc(nat_added, 1)

        add_chunk(10, 2)
        for k in range(0, 4):
            turn_lo(2, k, g2_col)
        add_chunk(11, 3)
        for k in range(4, 8):
            turn_lo(2, k, g2_col)

        f = 0
        for kind, quarter in MLP_ORDER:
            if kind == "up":
                for n in range(8):
                    dve.wait_ge(f_relu, f + 1)
                    if f >= 2:
                        dve.wait_ge(f_lo_done, f - 1)
                    TT(fs[:, f % 2, :], fr[:, f % 2, :], fr[:, f % 2, :], ALU.mult).then_inc(f_sq, 1)
                    dve.wait_ge(f_sq, f + 1)
                    dve.wait_ge(f_hi_done, f + 1)
                    TT(fT_lo[:, quarter % 2, n, :], fs[:, f % 2, :], fT_hi[:, quarter % 2, n, :].bitcast(F32),
                       ALU.subtract).then_inc(f_lo_done, 1)
                    f += 1
                if quarter == 0:
                    dve.wait_ge(x_sq, 2 * TOK)
                    TT(ms[:, 1, 1, :], ms[:, 1, 0, :], ms[:, 1, 1, :], ALU.add).then_inc(ms_sum, 1)
                    dve.wait_ge(x_rt, TOK + 1)
                    nc.vector.reciprocal(rstd2[:, :], ms[:, 1, 1, :]).then_inc(scale_ready, 1)
                    dve.wait_ge(scale_ready, 1)
            else:
                for half in range(2):
                    if (quarter, half) != (3, 1):
                        add_chunk(12 + 2 * quarter + half, 4 + 2 * quarter + half)
        dve.wait_ge(gfin_in, 16)
        dve.wait_ge(x_sq, 3 * TOK)
        for t in range(TOK):
            dve.wait_ge(nat_added, NAT_END - TOK)
            TT(x2[:, t, 0:512], x2[:, t, 0:512], gfin[:, 0:512], ALU.mult).then_inc(gained, 1)

        def norm_out(t):
            dve.wait_ge(x_rt, TOK + 2 + t + 1)
            nc.vector.reciprocal(rstd[:, 2, t:t + 1], ms[:, 2, 1, t:t + 1]).then_inc(x_rstd, 1)
            dve.wait_ge(x_rstd, TOK + t + 1)
            if t < TOK - 1:
                dve.wait_ge(rows_gained, t + 1)
            else:
                dve.wait_ge(last_gained, 1)
            TS(x2[:, t, 512:1024], xg[:, t, :], rstd[:, 2, t:t + 1], None, ALU.mult).then_inc(out_ready_hi, 1)

        for t in range(TOK):
            add_rows(19, 11, t)
            if t == TOK - 1:
                gain_rows(dve, TT, t, last_gained)
            if t:
                norm_out(t - 1)
        norm_out(TOK - 1)

    @block.tensor
    def _(pe):
        def mm3(dst, a_hi, a_lo, b_hi, b_lo, start, stop):
            nc.tensor.matmul(dst, a_hi, b_hi, start=start, stop=False)
            nc.tensor.matmul(dst, a_hi, b_lo, start=False, stop=False)
            return nc.tensor.matmul(dst, a_lo, b_hi, start=False, stop=stop)

        mlp_first = U_MLP

        def col_mm(u, bank, ks):
            for k in ks:
                if u == U_SSM:
                    pe.wait_ge(hT_lo_done, k + 1)
                elif u == mlp_first:
                    pe.wait_ge(hT_lo_done, 2 * KT + k + 1)
                c = slice(P * k, P * k + P)
                mm = mm3(ps[:, bank, :], w_hi[:, u % RING, c], w_lo[:, u % RING, c],
                         hT_hi[:, k, :], hT_lo[:, k, :], k == 0, k == KT - 1)
            return mm

        def row_unit_mm(u, c, r, n_rows, hi, lo, ready, per_row):
            pe.wait_ge(w_lo_done, u + 1)
            for t in range(TOK):
                if r == 0:
                    nat_free(c, t)
                for k2 in range(2):
                    k = 2 * r + k2
                    if t == 0 and ready is not None:
                        pe.wait_ge(ready, per_row + k + 1)
                    wc = slice(512 * k2, 512 * k2 + 512)
                    tc_ = slice(P * t, P * t + P)
                    mm = mm3(ps[:, t, :], hi[:, k, tc_], lo[:, k, tc_], w_hi[:, u % RING, wc],
                             w_lo[:, u % RING, wc], r == 0 and k2 == 0, r == n_rows - 1 and k2 == 1)
                if r == n_rows - 1 and t < TOK - 1:
                    mm.then_inc(nat_ready, 1)
            unit_done(mm)

        def unit_done(mm):
            mm.then_inc(unit_used, 1)

        COPIED = {0: 0, 1: 1, 2: 2, 3: 3, 4: 4, 5: 5, 6: 6, 8: 7}
        ADDED = {7: 0, 9: 1}
        ADDED.update({c: c - 8 for c in range(10, 20)})

        def nat_free(c, t):
            if c == 0:
                pe.wait_ge(hT_lo_done, KT)
            elif c == 4:
                if t == 0:
                    pe.wait_ge(qk_copied, 2 * N_HEADS)
                else:
                    pe.wait_ge(nat_copied, TOK * c + t)
            elif c == 5:
                if t < B_WT:
                    pe.wait_ge(score_read, 2 * BLOCKS)
                elif t == B_WT:
                    pe.wait_ge(wT_copied, BLOCKS)
                else:
                    pe.wait_ge(o_gated, BLOCKS)
            elif c - 1 in COPIED:
                pe.wait_ge(nat_copied, TOK * COPIED[c - 1] + t + 1)
            else:
                pe.wait_ge(nat_added, TOK * ADDED[c - 1] + t + 1)

        def turn(g, ks, src, ready, count):
            pe.wait_ge(ready, count)
            for k in ks:
                if k >= 4:
                    pe.wait_ge(hT_lo_done, KT * g + k - 3)
                elif g == 1:
                    pe.wait_ge(qk_copied, 2 * N_HEADS)
                    pe.wait_ge(nat_copied, 5 * TOK)
                    pe.wait_ge(y_done, UT)
                elif g == 2:
                    pe.wait_ge(hT_lo_done, 2 * KT)
                for t in range(TOK):
                    mm = nc.tensor.transpose(ps[:, turn_bank(g, k), P * t:P * t + P], src[:, t, P * k:P * k + P],
                                             ident[:, :])
                mm.then_inc(turned, 1)

        def drive(i):
            j, ut = i % 4, i // 4
            rows = slice(32 * j, 32 * j + 32)
            pe.wait_ge(BT_ready, 4)
            pe.wait_ge(u_copied, ut + 1)
            if i:
                pe.wait_ge(ssm_step, STEPS * (i - 1) + 4)
            for c in range(2):
                for ri in range(2):
                    mm = nc.tensor.matmul(ps[:, B_BU + ri, HALF * c:HALF * c + HALF], BT[rows, c, ri, ut, :],
                                          uT[rows, ut, HALF * c:HALF * c + HALF], start=True, stop=True)
            mm.then_inc(bu_ready, 1)

        def readout(i):
            j, ut = i % 4, i // 4
            pe.wait_ge(states_done, 2 * i + 2)
            if j == 0 and ut:
                pe.wait_ge(y_done, ut)
            if i == 0:
                pe.wait_ge(table, 1)
            for c in range(2):
                for ri in range(2):
                    mm = nc.tensor.matmul(ps[32 * j:32 * j + 32, B_Y, HALF * c:HALF * c + HALF],
                                          CT[:, i, c, ri, :], st[:, ri, HALF * c:HALF * c + HALF],
                                          start=(ri == 0), stop=(ri == 1), tile_position=(0, 32 * j))
            mm.then_inc(y_ready, 1)

        pe.wait_ge(ident_set, 2)
        pe.wait_ge(cols_in, 16 * N_COLS)
        nc.tensor.transpose(ps[:, 0, 0:2 * KT + UT], cols_nat[:, :],
                            ident[0:2 * KT + UT, 0:2 * KT + UT]).then_inc(cols_turned, 1)
        for t in range(TOK):
            pe.wait_ge(x_scaled, t + 1)
            for k in range(KT):
                if t == 0 and k == 4:
                    pe.wait_ge(cols_copied, 1)
                mm = nc.tensor.transpose(ps[:, turn_bank(0, k), P * t:P * t + P], mixA[:, t, P * k:P * k + P],
                                         ident[:, :])
                if t == TOK - 1:
                    mm.then_inc(turned, 1)

        for u in range(U_SSM, U_V):
            pe.wait_ge(w_lo_done, u + 1)
            unit_done(col_mm(u, 4 + u, range(KT)))
        pe.wait_ge(prm_ready, 1)
        pe.wait_ge(u_copied, 1)
        for n, row in enumerate((4, 5, 6, 15, 16)):
            mm = nc.tensor.transpose(ps[:, 4, PAIRS * n:PAIRS * n + PAIRS], prm[:, row, :],
                                     ident[0:PAIRS, 0:PAIRS])
        mm.then_inc(prm_turned, 1)
        pe.wait_ge(consts_in, 16 * N_CONST)
        pe.wait_ge(u_copied, 3)
        nc.tensor.matmul(ps[0:N_HEADS, 5, :], rb[:, :], oneh[:, 0:512], start=True, stop=True)
        nc.tensor.matmul(ps[0:N_HEADS, 6, 0:BIAS_W - 512], rb[:, :], oneh[:, 512:BIAS_W], start=True,
                         stop=True).then_inc(frow_mm, 1)

        def turn_c():
            for ri in range(2):
                pe.wait_ge((prm_copied, frow_out)[ri], ri + 1)
                for ut in range(UT):
                    mm = nc.tensor.transpose(ps[:, 4 + ri, P * ut:P * ut + P],
                                             c_nat[:, ri, ut, :, :].rearrange("p a s -> p (a s)"), ident[:, :])
                mm.then_inc(c_turned, 1)

        def turn_bb(half):
            for ri in range(2):
                pe.wait_ge(bb_ready, 4 * half + 2 * ri + 2)
                if half:
                    pe.wait_ge(BT_ready, ri + 1)
                else:
                    pe.wait_ge(frow_out, 2)
                    pe.wait_ge(u_copied, UT)
                for ut in range(UT):
                    mm = nc.tensor.transpose(ps[:, 6 + ri, P * ut:P * ut + P],
                                             bb[:, ri, 4 * ut:4 * ut + 4, :].rearrange("p a h -> p (a h)"),
                                             ident[:, :])
                mm.then_inc(bb_turned, 1)

        for u in range(U_V, U_GA):
            r = (u - U_V) % 4
            row_unit_mm(u, (u - U_V) // 4, r, 4, hT_hi, hT_lo, None, 0)
            if u == U_V + 3:
                turn_c()
                turn_bb(0)
        for u in range(U_GA, U_QK):
            n = u - U_GA
            if n == 0:
                turn_bb(1)
                drive(0)
            row_unit_mm(u, 2 + n // 4, n % 4, 4, hT_hi, hT_lo, None, 0)
            if n % 2 == 0:
                drive(n // 2 + 1)
            else:
                readout(n // 2)

        def qk_part(v, part):
            u = U_QK + v
            if part == 0:
                pe.wait_ge(w_lo_done, u + 1)
                if v:
                    pe.wait_ge(qk_copied, v)
                else:
                    pe.wait_ge(c_packed, 4)
            mm = col_mm(u, B_QK, range(4 * part, 4 * part + 4))
            if part:
                unit_done(mm)

        for v in range(2):
            qk_part(v, 0)
            qk_part(v, 1)

        def scores(n):
            h, i = n // TOK, n % TOK
            L = P * (i + 1)
            pe.wait_ge(qk_copied, 2 * h + 2)
            if n == 0:
                pe.wait_ge(nat_copied, 4 * TOK)
            else:
                pe.wait_ge(score_read, 2 * n)
            for m in range(2):
                rows = slice(HEAD_DIM * m, HEAD_DIM * m + HEAD_DIM)
                mm = nc.tensor.matmul(ps[:, B_SCORE + m, 0:L], qT[rows, h % 2, P * i:P * i + P],
                                      kT[rows, h % 2, 0:L], start=True, stop=True)
            mm.then_inc(score_ready, 1)

        def turn_w(n):
            pe.wait_ge(att_step, 3 * n + 3)
            if n:
                pe.wait_ge(wT_copied, n)
            for j in range(n % TOK + 1):
                mm = nc.tensor.transpose(ps[:, B_WT, P * j:P * j + P], Pm[:, n % 2, 0, P * j:P * j + P],
                                         ident[:, :])
            mm.then_inc(wT_ready, 1)

        def pv(n):
            h, i = n // TOK, n % TOK
            pe.wait_ge(wT_copied, n + 1)
            if i == 0 and h:
                pe.wait_ge(o_gated, TOK * h)
            for j in range(i + 1):
                mm = nc.tensor.matmul(ps[:, B_O, P * i:P * i + P], wT[:, n % 2, P * j:P * j + P],
                                      V[:, j, V_DIM * h:V_DIM * h + V_DIM], start=(j == 0), stop=(j == i))
            mm.then_inc(pv_done, 1)

        def gate_tile(t):
            nat_free(4, t)
            for r in range(4):
                u = U_GS + r
                pe.wait_ge(w_lo_done, u + 1)
                for k2 in range(2):
                    k = 2 * r + k2
                    tc_, wc = slice(P * t, P * t + P), slice(512 * k2, 512 * k2 + 512)
                    mm = mm3(ps[:, B_QK, :], hT_hi[:, k, tc_], hT_lo[:, k, tc_], w_hi[:, u % RING, wc],
                             w_lo[:, u % RING, wc], k == 0, k == KT - 1)
                if t == TOK - 1:
                    unit_done(mm)
            if t < TOK - 1:
                mm.then_inc(nat_ready, 1)

        def fill_ssm(n):
            for i, part in slot_parts(n):
                if part == 0 and i + 1 < PAIRS:
                    drive(i + 1)
                if part == 2:
                    readout(i)

        for n in range(BLOCKS + 2):
            h, i = n // TOK, n % TOK
            if n >= 2 and (i == 0 or n >= BLOCKS):
                pv(n - 2)
            if n < BLOCKS:
                scores(n)
                if n >= 2 and i % 2:
                    pv(n - 2)
                if h < N_HEADS - 1:
                    qk_part(2 * (h + 1) + i // 2, i % 2)
                else:
                    gate_tile(i)
                if n >= 2 and i == 2:
                    pv(n - 2)
            if 1 <= n <= BLOCKS:
                turn_w(n - 1)
                fill_ssm(n - 1)

        for u in range(U_GS + 4, U_GLU):
            row_unit_mm(u, 5, u - U_GS - 4, 4, hT_hi, hT_lo, None, 0)
        for u in range(U_GLU, U_OUT):
            n = u - U_GLU
            row_unit_mm(u, 6 + n // 2, n % 2, 2, gT_hi, gT_lo, gT_lo_done, 0)
            if n == 5:
                turn(1, range(0, 4), mixA, mixed_done, 16)
        for u in range(U_OUT, U_MLP):
            n = u - U_OUT
            if n == 1:
                turn(1, range(4, 8), mixA, mixed_done, 32)
            row_unit_mm(u, 10 + n // 4, n % 4, 4, hT_hi, hT_lo, hT_lo_done, KT)
            if n == 6:
                turn(2, range(0, 4), x2, nat_added, 3 * TOK)
        turn(2, range(4, 8), x2, nat_added, 4 * TOK)

        f = 0
        for step, (kind, quarter) in enumerate(MLP_ORDER):
            for n in range(8):
                u = U_MLP + 8 * step + n
                if kind == "up":
                    pe.wait_ge(w_lo_done, u + 1)
                    if f < 4:
                        pe.wait_ge(hT_lo_done, 2 * KT + 4 + f + 1)
                    else:
                        pe.wait_ge(f_relu, f - 3)
                    mm = col_mm(u, B_T + f % 4, range(KT))
                    unit_done(mm)
                    f += 1
                else:
                    row_unit_mm(u, 12 + 2 * quarter + n // 4, n % 4, 4, fT_hi[:, quarter % 2, :, :],
                                fT_lo[:, quarter % 2, :, :], f_lo_done, 8 * quarter)

    ctx.close()


_INS = ['x', 'g_mix', 'w_in', 'lambda_q1', 'lambda_k1', 'lambda_q2', 'lambda_k2', 'subln_g', 'rel_bias',
        'ssm_a_re', 'ssm_a_im', 'ssm_log_dt', 'ssm_b_re', 'ssm_b_im', 'ssm_c_re', 'ssm_c_im', 'ssm_d',
        'w_glu', 'w_out', 'g_mlp', 'w1', 'w2', 'g_final']


def kernel(**inputs):
    import concourse.bacc as bacc
    from concourse.bass_utils import run_bass_kernel_spmd

    nc = bacc.Bacc("TRN2", target_bir_lowering=False, num_devices=1)
    arrays, args = {}, []
    given = {name: np.ascontiguousarray(inputs[name]) for name in _INS}
    given["onehot"] = bucket_onehot()
    for name, a in given.items():
        arrays[f"in_{name}"] = a
        ap = nc.dram_tensor(f"in_{name}", a.shape, mybir.dt.from_np(a.dtype), kind="ExternalInput").ap()
        args.append(ap[0] if name in ("w_in", "w_glu", "w_out", "w1", "w2") else ap)
    out = nc.dram_tensor("out", (1, SEQ, D_MODEL), F32, kind="ExternalOutput").ap()
    build(nc, *args, out)
    r = run_bass_kernel_spmd(nc, [arrays], core_ids=[0])
    return r.results[0]["out"]
```

```python
import math
from contextlib import ExitStack

import numpy as np

import concourse.bass as bass
from concourse import mybir
from concourse.alu_op_type import AluOpType as ALU

ACT = mybir.ActivationFunctionType
F32 = mybir.dt.float32
F32R = mybir.dt.float32r

P = 128
SEQ, D_MODEL = 512, 1024
N_HEADS, HEAD_DIM, V_DIM = 8, 64, 128
SSM_WIDTH, SSM_GROUP, SSM_GROUPS, SSM_STATE = 512, 16, 32, 64
D_FF = 4096
N_BUCKETS, MAX_DISTANCE = 32, 128
EPS = 1e-6
LAM_INIT = 0.8 - 0.6 * math.exp(-0.3 * 0)
MASKED = -1e30

TOK = SEQ // P
KT = D_MODEL // P
UT = SSM_WIDTH // P
PAIRS = SSM_GROUPS // 2
HALF = SEQ // 2
BIAS_W = 640
BLOCKS = N_HEADS * TOK

RING = 4
U_SSM, U_V, U_GA, U_QK, U_GS, U_GLU, U_OUT, U_MLP = 0, 4, 12, 20, 36, 44, 52, 60
N_UNITS = U_MLP + 64
COL_Q, COL_K, COL_V, COL_U, COL_GA, COL_GS = 0, 1024, 2048, 3072, 3584, 4608

B_SCORE, B_WT, B_O, B_QK, B_Y, B_BU, B_T = 0, 2, 3, 4, 5, 6, 4


def bucket_onehot():
    rel = SEQ - 1 - np.arange(BIAS_W)
    n = np.maximum(rel, 0)
    exact = N_BUCKETS // 2
    large = exact + (np.log(np.maximum(n, 1).astype(np.float32) / np.float32(exact)).astype(np.float32)
                     / np.float32(math.log(MAX_DISTANCE / exact)) * np.float32(N_BUCKETS - exact)).astype(np.int32)
    bucket = np.where(n < exact, n, np.minimum(large, N_BUCKETS - 1))
    return ((bucket[None, :] == np.arange(N_BUCKETS)[:, None]) & (rel >= 0)[None, :]).astype(np.float32)


def build(nc, x, g_mix, w_in, lambda_q1, lambda_k1, lambda_q2, lambda_k2, subln_g, rel_bias,
          ssm_a_re, ssm_a_im, ssm_log_dt, ssm_b_re, ssm_b_im, ssm_c_re, ssm_c_im, ssm_d,
          w_glu, w_out, g_mlp, w1, w2, g_final, onehot, out):
    ctx = ExitStack()
    base = (nc.sbuf_base + 63) // 64 * 64
    at = {"next": base}

    def sb(name, shape, dt=F32, offset=None):
        size = 4 * int(np.prod(shape[1:]))
        if offset is None:
            offset = at["next"]
            at["next"] += (size + 31) // 32 * 32
        at[name] = offset
        return nc.alloc_sbuf_tensor_at(name, list(shape), dt, offset=offset)

    def sem(name):
        return ctx.enter_context(nc.semaphore(name))

    ident = sb("ident", [P, P])
    hT_hi = sb("hT_hi", [P, KT, SEQ], F32R)
    hT_lo = sb("hT_lo", [P, KT, SEQ], F32R)
    raw = sb("raw", [P, RING, 1024])
    w_hi = sb("w_hi", [P, RING, 1024], F32R)
    w_lo = sb("w_lo", [P, RING, 1024], F32R)
    mixA = sb("mixA", [P, TOK, D_MODEL])
    V = sb("V", [P, TOK, D_MODEL])
    uT = sb("uT", [P, UT, SEQ])
    E_re = sb("E_re", [P, PAIRS, HALF])
    BT = sb("BT", [P, 2, 2, UT, P])
    CT = sb("CT", [P, PAIRS, 2, 2, 32])
    E_im = sb("E_im", [P, PAIRS, HALF])
    rt = sb("rt", [P, 4, SEQ])
    st = sb("st", [P, 2, SEQ])
    qT = sb("qT", [P, 2, SEQ])
    kT = sb("kT", [P, 2, SEQ])
    bias = sb("bias", [P, 2, SEQ])
    Pm = sb("Pm", [P, 2, 2, SEQ])
    wT = sb("wT", [P, 2, SEQ])
    mag = sb("mag", [P, 5, PAIRS])
    coef = sb("coef", [P, 2, 2, PAIRS])
    pw = sb("pw", [P, 2, 2, PAIRS])
    pwt = sb("pwt", [P, 4, PAIRS])
    cols = sb("cols", [P, 2 * KT + UT])
    gsub = sb("gsub", [P, V_DIM])
    ssq = sb("ssq", [P, TOK, N_HEADS])
    rsub = sb("rsub", [P, TOK, N_HEADS])
    ms = sb("ms", [P, 3, 2, TOK])
    rstd = sb("rstd", [P, 3, TOK])
    rstd2 = sb("rstd2", [P, TOK])
    mx = sb("mx", [P, 2, 2])
    nmx = sb("nmx", [P, 2, 2])
    sums = sb("sums", [P, 2, 2])
    rinv = sb("rinv", [P, 8, 2])
    cfac = sb("cfac", [P, 2, 1])
    nlam = sb("nlam", [P, 4])
    osq = sb("osq", [P, V_DIM])
    eps_t = sb("eps_t", [P, 1])
    halfpi = sb("halfpi", [P, 1])
    assert at["next"] <= nc.sbuf_usable_end, (at["next"], nc.sbuf_usable_end)
    pt = at["qT"]
    prm = sb("prm", [PAIRS, 20, P], offset=pt)
    b_nat = sb("b_nat", [P, 2, PAIRS, SSM_GROUP], offset=pt + 10240)
    c_nat = sb("c_nat", [P, 2, UT, 2, SSM_STATE], offset=pt + 12288)
    c_pk = sb("c_pk", [P, 2, PAIRS, SSM_GROUP], offset=pt + 16384)
    oneh = sb("oneh", [N_BUCKETS, BIAS_W], offset=pt + 18432)
    frow = sb("frow", [N_HEADS, BIAS_W], offset=pt + 20992)
    lamv = sb("lamv", [P, 2, 2, HEAD_DIM], offset=at["rt"] + 11264)
    cols_nat = sb("cols_nat", [2 * KT + UT, P], offset=pt + 23552)
    bb = sb("bb", [P, 2, PAIRS, 32], offset=at["rt"])
    bt = sb("bt", [P, 4, PAIRS, SSM_GROUP], offset=at["rt"] + 4096)
    rb = sb("rb", [N_BUCKETS, N_HEADS], offset=at["rt"] + 8192)
    dtt = sb("dtt", [PAIRS, 2, 2], offset=at["rt"] + 8256)
    em = sb("em", [P, 2, PAIRS, HALF // 2], offset=at["mixA"])
    mixS = sb("mixS", [P, TOK, D_MODEL], offset=at["V"])
    gT_hi = sb("gT_hi", [P, UT, SEQ], F32R, offset=at["qT"])
    gT_lo = sb("gT_lo", [P, UT, SEQ], F32R, offset=at["bias"])
    zt = sb("zt", [P, 2, SEQ], offset=at["Pm"] + 4096)
    junk = sb("junk", [P, D_MODEL], offset=at["wT"])
    x2 = sb("x2", [P, TOK, D_MODEL], offset=at["E_im"])
    fT_hi = sb("fT_hi", [P, 2, 4, SEQ], F32R, offset=at["mixA"])
    fT_lo = sb("fT_lo", [P, 2, 4, SEQ], F32R, offset=at["mixA"] + 16384)
    fr = sb("fr", [P, 2, SEQ], offset=at["rt"])
    fs = sb("fs", [P, 2, SEQ], offset=at["rt"] + 4096)
    xg = sb("xg", [P, TOK, 512], offset=at["rt"])
    gfin = sb("gfin", [P, D_MODEL], offset=at["st"])
    assert at["fT_lo"] + 16384 <= at["E_im"]
    ps = ctx.enter_context(nc.psum_tensor("ps", [P, 8, 512], F32))
    g1_col, g2_col, d_col = cols[:, 0:KT], cols[:, KT:2 * KT], cols[:, 2 * KT:2 * KT + UT]
    frow_dram = nc.dram_tensor("frow_dram", [N_HEADS, P, BIAS_W], F32, kind="Internal").ap()

    x_in = [sem(f"x_in{t}") for t in range(TOK)]; cols_in = sem("cols_in"); x_again = sem("x_again")
    out_stored = sem("out_stored")
    consts_in = sem("consts_in"); prm_in = sem("prm_in"); gfin_in = sem("gfin_in")
    frow_out = sem("frow_out"); frow_done = sem("frow_done"); frow_mm = sem("frow_mm")
    bias_in = [sem(f"bias_in{i}") for i in range(2)]
    raw_in = [sem(f"raw_in{i}") for i in range(RING)]
    w_hi_done = sem("w_hi_done"); w_lo_done = sem("w_lo_done"); unit_used = sem("unit_used")
    ident_set = sem("ident_set"); tiles_set = sem("tiles_set")
    x_squared = sem("x_squared"); x_sq = sem("x_sq"); ms_sum = sem("ms_sum")
    scale_ready = sem("scale_ready"); x_rt = sem("x_rt"); x_rstd = sem("x_rstd"); x_scaled = sem("x_scaled")
    turned = sem("turned"); hT_hi_done = sem("hT_hi_done"); hT_lo_done = sem("hT_lo_done")
    u_copied = sem("u_copied")
    nat_ready = sem("nat_ready"); nat_copied = sem("nat_copied"); nat_added = sem("nat_added")
    gates_done = sem("gates_done"); zt_used = sem("zt_used")
    cols_turned = sem("cols_turned"); cols_copied = sem("cols_copied")
    prep = sem("prep"); lam_dots = sem("lam_dots"); args_ready = sem("args_ready")
    prm_ready = sem("prm_ready"); prm_copied = sem("prm_copied"); prep_act = sem("prep_act")
    prm_turned = sem("prm_turned")
    table = sem("table"); bb_ready = sem("bb_ready"); bb_turned = sem("bb_turned")
    BT_ready = sem("BT_ready"); c_turned = sem("c_turned"); c_packed = sem("c_packed")
    bu_ready = sem("bu_ready"); ssm_step = sem("ssm_step"); states_done = sem("states_done")
    y_ready = sem("y_ready"); y_done = sem("y_done"); gelu_done = sem("gelu_done")
    gT_hi_done = sem("gT_hi_done"); gT_lo_done = sem("gT_lo_done")
    qk_copied = sem("qk_copied")
    score_ready = sem("score_ready"); score_read = sem("score_read"); nmax_ready = sem("nmax_ready")
    exp_done = sem("exp_done"); att_step = sem("att_step"); wT_ready = sem("wT_ready")
    wT_copied = sem("wT_copied"); pv_done = sem("pv_done"); o_squared = sem("o_squared")
    o_gated = sem("o_gated"); rsub_step = sem("rsub_step"); mixed_done = sem("mixed_done")
    f_relu = sem("f_relu"); f_hi_done = sem("f_hi_done")
    f_sq = sem("f_sq"); f_lo_done = sem("f_lo_done"); out_ready = sem("out_ready"); gained = sem("gained")
    rows_gained = sem("rows_gained"); last_gained = sem("last_gained"); out_ready_hi = sem("out_ready_hi")

    block = ctx.enter_context(nc.Block())

    def col_unit(w, c0):
        return w[:, c0:c0 + P].rearrange("(k p) n -> p k n", p=P)

    def row_unit(w, r0, c0):
        return w[r0:r0 + 2 * P, c0:c0 + 512].rearrange("(k p) n -> p k n", p=P)

    def unit_source(u):
        if u < U_V:
            return col_unit(w_in, COL_U + P * u)
        if u < U_GA:
            return row_unit(w_in, 256 * ((u - U_V) % 4), COL_V + 512 * ((u - U_V) // 4))
        if u < U_QK:
            return row_unit(w_in, 256 * ((u - U_GA) % 4), COL_GA + 512 * ((u - U_GA) // 4))
        if u < U_GS:
            return col_unit(w_in, ((u - U_QK) % 2) * COL_K + P * ((u - U_QK) // 2))
        if u < U_GLU:
            return row_unit(w_in, 256 * ((u - U_GS) % 4), COL_GS + 512 * ((u - U_GS) // 4))
        if u < U_OUT:
            c = (u - U_GLU) // 2
            return row_unit(w_glu, 256 * ((u - U_GLU) % 2), (1 - c % 2) * D_MODEL + 512 * (c // 2))
        if u < U_MLP:
            return row_unit(w_out, 256 * ((u - U_OUT) % 4), 512 * ((u - U_OUT) // 4))

    EIGHTHS = 8
    FT = D_FF // EIGHTHS // P
    U_LOOP, PER_LOOP, LOOPS = U_MLP + 4, 16, (EIGHTHS - 2) // 2
    U_TAIL = U_LOOP + PER_LOOP * LOOPS

    def mlp_steps(e, u):
        return (("up", e + 1, 1, u), ("down", e, 0, u + 4), ("up", e + 2, 0, u + 8), ("down", e + 1, 1, u + 12))

    MLP_TAIL = (("up", EIGHTHS - 1, 1, U_TAIL), ("down", EIGHTHS - 2, 0, U_TAIL + 4),
                ("down", EIGHTHS - 1, 1, U_TAIL + 8))

    NAT_END = TOK * (4 + 2 * EIGHTHS)

    def mlp_source(kind, e, n):
        if kind == "up":
            c0 = 512 * e + P * n
            return w1[:, bass.ds(c0, P)].rearrange("(k p) n -> p k n", p=P)
        r0 = 512 * e + 256 * (n % 2)
        return w2[bass.ds(r0, 2 * P), 512 * (n // 2):512 * (n // 2) + 512].rearrange("(k p) n -> p k n", p=P)

    def last_unit(c):
        if c < 2:
            return U_V + 4 * c + 3
        if c < 4:
            return U_GA + 4 * (c - 2) + 3
        if c < 6:
            return U_GS + 4 * (c - 4) + 3
        if c < 10:
            return U_GLU + 2 * (c - 6) + 1
        return U_OUT + 4 * (c - 10) + 3

    def qk_bank(v):
        return B_SCORE if v == 1 else B_QK

    def gate_bank(c, t):
        return B_QK if c == 4 else t

    def turn_bank(g, k):
        if g == 2 and k >= 4:
            return k - 4
        return (B_T + k) % 8 if g == 0 else B_T + k % 4

    def wait_rows(eng, c, t):
        if t < TOK - 1:
            eng.wait_ge(nat_ready, (TOK - 1) * c + t + 1)
        else:
            eng.wait_ge(unit_used, last_unit(c) + 1)

    FIRST_D = 4

    def slot_parts(n):
        total = 3 * (PAIRS - FIRST_D)
        return [(FIRST_D + p // 3, p % 3) for p in range(total * n // BLOCKS, total * (n + 1) // BLOCKS)]

    def slot_units(n):
        h, i = n // TOK, n % TOK
        if i % 2 == 0 and h < N_HEADS - 1:
            return [U_QK + 2 * (h + 1) + i // 2 + 2]
        return {BLOCKS - 5: [U_GS + 2], BLOCKS - 1: [U_GS + 4, U_GS + 5]}.get(n, [])

    def wait_mlp_rows(eng, e, half, u, t):
        if t < TOK - 1:
            eng.wait_ge(nat_ready, e * (2 * (TOK - 1)) + (TOK - 1) * (12 + half) + t + 1)
        else:
            eng.wait_ge(unit_used, u + 2 * half + 2)

    @block.sync
    def _(sp):
        for t in range(TOK):
            sp.dma_start(mixA[:, t, :], x[0, P * t:P * t + P, :]).then_inc(x_in[t], 16)

        def load_raw(u):
            if u >= RING:
                sp.wait_ge(w_lo_done, u - RING + 1)
            dst = raw[:, u % RING, :]
            src = unit_source(u)
            sp.dma_start(dst.rearrange("p (k n) -> p k n", k=src.shape[1]), src).then_inc(raw_in[u % RING], 16)

        def load_bias(h):
            if h >= 2:
                sp.wait_ge(score_read, 2 * TOK * (h - 1))
            else:
                sp.wait_ge(BT_ready, 4)
                sp.wait_ge(c_packed, 4)
                sp.wait_ge(table, 1)
                sp.wait_ge(frow_done, 16)
            src = bass.AP(frow_dram.tensor, h * P * BIAS_W + P - 1, [[BIAS_W - 1, P], [1, SEQ]])
            sp.dma_start(bias[:, h % 2, :], src).then_inc(bias_in[h % 2], 16)

        for u in range(RING):
            load_raw(u)
        for src, dst in ((ssm_log_dt[0].rearrange("(i two) -> i two", two=2), dtt[:, 0, :]),
                         (ssm_a_re[0].rearrange("(i two) s -> i (two s)", two=2), prm[:, 0, :]),
                         (ssm_a_im[0].rearrange("(i two) s -> i (two s)", two=2), prm[:, 1, :])):
            sp.dma_start(dst, src).then_inc(prm_in, 16)
        for src, dst in ((bass.AP(subln_g.tensor, 0, [[0, P], [1, V_DIM]]), gsub[:, :]),
                         (bass.AP(lambda_q1.tensor, 0, [[0, P], [1, HEAD_DIM]]), lamv[:, 0, 0, :]),
                         (bass.AP(lambda_k1.tensor, 0, [[0, P], [1, HEAD_DIM]]), lamv[:, 0, 1, :]),
                         (bass.AP(lambda_q2.tensor, 0, [[0, P], [1, HEAD_DIM]]), lamv[:, 1, 0, :]),
                         (bass.AP(lambda_k2.tensor, 0, [[0, P], [1, HEAD_DIM]]), lamv[:, 1, 1, :]),
                         (rel_bias, rb[:, :]), (onehot, oneh[:, :]),
                         (ssm_b_re[0].rearrange("(i two) s h -> (two s) i h", two=2), b_nat[:, 0, :, :]),
                         (ssm_b_im[0].rearrange("(i two) s h -> (two s) i h", two=2), b_nat[:, 1, :, :]),
                         (ssm_c_re[0].rearrange("(t g) h s -> (g h) t s", g=8), c_nat[:, 0, :, 0, :]),
                         (ssm_c_re[0].rearrange("(t g) h s -> (g h) t s", g=8), c_nat[:, 0, :, 1, :]),
                         (ssm_c_im[0].rearrange("(t g) h s -> (g h) t s", g=8), c_nat[:, 1, :, 0, :]),
                         (ssm_c_im[0].rearrange("(t g) h s -> (g h) t s", g=8), c_nat[:, 1, :, 1, :])):
            sp.dma_start(dst, src).then_inc(consts_in, 16)

        for u in range(RING, U_MLP):
            load_raw(u)
            if u == U_GA + 4:
                load_bias(0)
                load_bias(1)
            if U_QK + 6 <= u < U_QK + 6 + 2 * (N_HEADS - 2) and u % 2 == 0:
                load_bias((u - U_QK - 6) // 2 + 2)
            if u == U_OUT:
                sp.wait_ge(y_done, UT)
                for t in range(TOK):
                    sp.dma_start(x2[:, t, :], x[0, P * t:P * t + P, :]).then_inc(x_again, 16)
                sp.dma_start(gfin[:, :], bass.AP(g_final.tensor, 0, [[0, P], [1, D_MODEL]])).then_inc(gfin_in, 16)

        def load_mlp(kind, e, u):
            for n in range(4):
                sp.wait_ge(w_lo_done, u + n - RING + 1)
                src = mlp_source(kind, e, n)
                sp.dma_start(raw[:, n, :].rearrange("p (k n) -> p k n", k=src.shape[1]), src).then_inc(raw_in[n], 16)

        load_mlp("up", 0, U_MLP)
        with sp.Fori(0, LOOPS) as j:
            for kind, e, odd, u in mlp_steps(2 * j, U_LOOP + PER_LOOP * j):
                load_mlp(kind, e, u)
        for kind, e, odd, u in MLP_TAIL:
            load_mlp(kind, e, u)
        for t in range(TOK):
            sp.wait_ge(out_ready, t + 1)
            sp.wait_ge(out_ready_hi, t + 1)
            sp.dma_start(out[0, P * t:P * t + P, :], x2[:, t, :]).then_inc(out_stored, 16)
        sp.wait_ge(out_stored, 16 * TOK)

    N_PRM, N_CONST, N_COLS = 3, 13, 3

    STEPS = 12

    def add_states(i, eng, add):
        eng.wait_ge(ssm_step, STEPS * i + 11)
        add(st[:, 0, :], rt[:, 0, :], rt[:, 2, :], ALU.subtract).then_inc(states_done, 1)
        eng.wait_ge(ssm_step, STEPS * i + 12)
        add(st[:, 1, :], st[:, 1, :], rt[:, 3, :], ALU.add).then_inc(states_done, 1)

    def gain_rows(eng, mult, t, done):
        eng.wait_ge(nat_added, NAT_END - TOK + t + 1)
        mult(xg[:, t, :], x2[:, t, 512:1024], gfin[:, 512:1024], ALU.mult).then_inc(done, 1)

    @block.gpsimd
    def _(pool):
        nc.gpsimd.memset(ident[:, :], 0.0).then_inc(ident_set, 1)
        nc.gpsimd.memset(eps_t[:, :], EPS).then_inc(tiles_set, 1)
        nc.gpsimd.memset(halfpi[:, :], math.pi / 2).then_inc(tiles_set, 1)
        pool.wait_ge(ident_set, 1)
        nc.gpsimd.affine_select(out=ident[:, :], in_=ident[:, :], compare_op=ALU.not_equal, fill=1.0,
                                base=0, pattern=[[-1, P]], channel_multiplier=1).then_inc(ident_set, 1)
        nc.gpsimd.memset(bb[:, :, :, :], 0.0).then_inc(tiles_set, 1)
        nc.gpsimd.memset(CT[:, :, :, :, :], 0.0).then_inc(tiles_set, 1)
        nc.gpsimd.memset(E_re[:, :, 0:1], 1.0).then_inc(tiles_set, 1)
        nc.gpsimd.memset(E_im[:, :, 0:1], 0.0).then_inc(tiles_set, 1)
        def split_lo(u):
            pool.wait_ge(w_hi_done, u + 1)
            nc.gpsimd.tensor_tensor(w_lo[:, u % RING, :], raw[:, u % RING, :],
                                    w_hi[:, u % RING, :].bitcast(F32), ALU.subtract).then_inc(w_lo_done, 1)

        def split_lo_turn(u):
            for s in range(RING):
                pool.wait_ge(w_hi_done, u + s + 1)
                nc.gpsimd.tensor_tensor(w_lo[:, s, :], raw[:, s, :], w_hi[:, s, :].bitcast(F32),
                                        ALU.subtract).then_inc(w_lo_done, 1)

        with pool.Fori(0, (U_QK + 4) // RING) as turn:
            split_lo_turn(RING * turn)
        for n in range(BLOCKS):
            for u in slot_units(n):
                split_lo(u)
            for i, part in slot_parts(n):
                if part == 2 and i < PAIRS - 1:
                    add_states(i, pool, nc.gpsimd.tensor_tensor)
            if n == BLOCKS - 5:
                split_lo(U_GS + 3)
        for u in range(U_GS + 6, U_GLU):
            split_lo(u)
        with pool.Fori(0, (N_UNITS - U_GLU) // RING) as turn:
            split_lo_turn(RING * turn + U_GLU)
        pool.wait_ge(gfin_in, 16)
        for t in range(TOK - 1):
            gain_rows(pool, nc.gpsimd.tensor_tensor, t, rows_gained)

    @block.scalar
    def _(act):
        def col(src):
            return src.rearrange("(k p) -> k p", p=P)

        act.wait_ge(tiles_set, 2)
        nc.scalar.activation(osq[:, 0:1], eps_t[:, :], ACT.Sqrt)
        for src, dst in ((col(g_mix[0]), cols_nat[0:KT, :]), (col(g_mlp[0]), cols_nat[KT:2 * KT, :]),
                         (col(ssm_d[0]), cols_nat[2 * KT:, :])):
            act.dma_start(dst, src).then_inc(cols_in, 16)
        for t in range(TOK):
            act.wait_ge(x_in[t], 16)
            nc.scalar.activation(V[:, t, :], mixA[:, t, :], ACT.Square,
                                 accum_out=ms[:, 0, 0, t:t + 1]).then_inc(x_squared, 1)
            act.wait_ge(x_squared, t + 1)
            nc.scalar.activation(ms[:, 0, 1, t:t + 1], ms[:, 0, 0, t:t + 1], ACT.Sqrt, bias=eps_t[:, :],
                                 scale=1.0 / D_MODEL).then_inc(x_rt, 1)
        act.wait_ge(cols_turned, 1)
        nc.scalar.activation(cols[:, :], ps[:, turn_bank(0, KT - 1), 0:2 * KT + UT],
                             ACT.Identity).then_inc(cols_copied, 1)

        def split_hi(u):
            if u >= N_UNITS:
                return
            act.wait_ge(raw_in[u % RING], 16 * (u // RING + 1))
            if u >= RING:
                act.wait_ge(unit_used, u - RING + 1)
            nc.scalar.activation(w_hi[:, u % RING, :], raw[:, u % RING, :], ACT.Identity).then_inc(w_hi_done, 1)

        def turn_hi(g, k, gain):
            act.wait_ge(turned, KT * g + k + 1)
            kw = {} if gain is None else {"scale": gain[:, k:k + 1]}
            nc.scalar.activation(hT_hi[:, k, :], ps[:, turn_bank(g, k), :], ACT.Identity, **kw).then_inc(hT_hi_done, 1)

        split_hi(0)
        act.wait_ge(cols_copied, 1)
        for k in range(KT):
            turn_hi(0, k, g1_col)
            if k == 2:
                split_hi(1)
        for u in range(U_SSM, U_V):
            split_hi(u + 2)
            if u == 0:
                act.wait_ge(prm_in, 16 * N_PRM)
                nc.scalar.activation(dtt[:, 1, :], dtt[:, 0, :], ACT.Exp).then_inc(prep_act, 1)
                act.wait_ge(args_ready, 1)
                nc.scalar.activation(prm[:, 4, :], prm[:, 2, :], ACT.Exp).then_inc(prep_act, 1)
                act.wait_ge(lam_dots, 2)
                nc.scalar.activation(nlam[:, 2:4], nlam[:, 0:2], ACT.Exp).then_inc(prep_act, 1)
            if u == 1:
                act.wait_ge(args_ready, 3)
                nc.scalar.activation(prm[:, 6, :], prm[:, 8, :], ACT.Sin).then_inc(prep_act, 1)
                nc.scalar.activation(prm[:, 5, :], prm[:, 9, :], ACT.Sin, bias=halfpi[0:PAIRS, :],
                                     scale=-1.0).then_inc(prep_act, 1)
            act.wait_ge(unit_used, U_SSM + u + 1)
            nc.scalar.activation(uT[:, u, :], ps[:, 4 + u, :], ACT.Identity).then_inc(u_copied, 1)
        act.wait_ge(frow_out, 2)
        act.dma_start(frow_dram, frow[:, :].unsqueeze(1).to_broadcast([N_HEADS, P, BIAS_W])).then_inc(frow_done, 16)

        def copy_c():
            for ri in range(2):
                act.wait_ge(c_turned, ri + 1)
                for g2 in range(2):
                    rows = slice(64 * g2, 64 * g2 + 64)
                    src = ps[rows, 4 + ri, :].rearrange("p (t j g h) -> p (t j) g h", t=UT, g=2, h=SSM_GROUP)
                    nc.scalar.activation(c_pk[rows, ri, :, :], src[:, :, g2, :], ACT.Identity).then_inc(c_packed, 1)

        def copy_bb(half):
            for n in (2 * half, 2 * half + 1):
                act.wait_ge(bb_turned, n + 1)
                nc.scalar.activation(BT[:, n // 2, n % 2, :, :].rearrange("p t s -> p (t s)"),
                                     ps[:, 6 + n % 2, :], ACT.Identity).then_inc(BT_ready, 1)

        for u in range(U_V, U_QK):
            split_hi(u + 2)
            c, last = (u - U_V) // 4, (u - U_V) % 4 == 3
            if u == U_V + 4:
                copy_c()
                copy_bb(0)
            if u == U_GA:
                copy_bb(1)
            if last:
                for t in range(TOK):
                    wait_rows(act, c, t)
                    if c < 2:
                        nc.scalar.activation(V[:, t, 512 * c:512 * c + 512], ps[:, t, :],
                                             ACT.Identity).then_inc(nat_copied, 1)
                    else:
                        if c == 2:
                            act.wait_ge(table, 1)
                        nc.scalar.activation(mixA[:, t, 512 * (c - 2):512 * (c - 1)], ps[:, t, :], ACT.Tanh,
                                             scale=0.5).then_inc(nat_copied, 1)

        def copy_qk(v):
            act.wait_ge(unit_used, U_QK + v + 1)
            h = v // 2
            if h >= 2:
                act.wait_ge(score_ready, TOK * (h - 1))
            if v == 0:
                act.wait_ge(table, 1)
                act.wait_ge(frow_done, 16)
            dst = (qT, kT)[v % 2][:, h % 2, :]
            nc.scalar.activation(dst, ps[:, qk_bank(v), :], ACT.Identity,
                                 scale=(HEAD_DIM ** -0.5 if v % 2 == 0 else 1.0)).then_inc(qk_copied, 1)

        def exps(n):
            L = P * (n % TOK + 1)
            act.wait_ge(nmax_ready, n + 1)
            for m in range(2):
                nc.scalar.activation(Pm[:, n % 2, m, 0:L], Pm[:, n % 2, m, 0:L], ACT.Exp,
                                     bias=nmx[:, n % 2, m:m + 1],
                                     accum_out=sums[:, n % 2, m:m + 1]).then_inc(exp_done, 1)

        def copy_wT(n):
            L = P * (n % TOK + 1)
            act.wait_ge(wT_ready, n + 1)
            if n >= 2:
                act.wait_ge(pv_done, n - 1)
            nc.scalar.activation(wT[:, n % 2, 0:L], ps[:, B_WT, 0:L], ACT.Identity).then_inc(wT_copied, 1)

        def square_o(h):
            act.wait_ge(pv_done, TOK * (h + 1))
            for i in range(TOK):
                n = TOK * h + i
                if n >= 1:
                    act.wait_ge(o_squared, n)
                nc.scalar.activation(osq[:, :], ps[:, B_O, P * i:P * i + P], ACT.Square,
                                     scale=rinv[:, n % 8, 0:1],
                                     accum_out=ssq[:, i, h:h + 1]).then_inc(o_squared, 1)

        def gate_tanh(c, t):
            wait_rows(act, c, t)
            nc.scalar.activation(mixS[:, t, 512 * (c - 4):512 * (c - 3)], ps[:, gate_bank(c, t), :], ACT.Tanh,
                                 scale=0.5).then_inc(nat_copied, 1)

        for v in range(2):
            split_hi(U_QK + v + 2)
            copy_qk(v)
        for n in range(BLOCKS + 2):
            h, i = n // TOK, n % TOK
            if n < BLOCKS:
                exps(n)
                for u in slot_units(n):
                    split_hi(u)
            if i == 1 and h >= 1:
                square_o(h - 1)
            if 1 <= n <= BLOCKS:
                copy_wT(n - 1)
            if i % 2 == 1 and h < N_HEADS - 1:
                copy_qk(2 * (h + 1) + i // 2)
            if n == BLOCKS - 5:
                split_hi(U_GS + 3)
            if h == N_HEADS - 1:
                gate_tanh(4, i)

        act.wait_ge(o_squared, BLOCKS)
        nc.scalar.activation(ssq[:, :, :], ssq[:, :, :], ACT.Sqrt, bias=eps_t[:, :],
                             scale=1.0 / V_DIM).then_inc(rsub_step, 1)
        for u in range(U_GS + 4, U_GLU):
            split_hi(u + 2)
            if u == U_GS + 4:
                for k in range(UT):
                    act.wait_ge(y_done, k + 1)
                    nc.scalar.activation(uT[:, k, :], uT[:, k, :], ACT.Gelu_apprx_tanh).then_inc(gelu_done, 1)
                for k in range(UT):
                    act.wait_ge(gelu_done, k + 1)
                    nc.scalar.activation(gT_hi[:, k, :], uT[:, k, :], ACT.Identity).then_inc(gT_hi_done, 1)
        for t in range(TOK):
            gate_tanh(5, t)
        for u in range(U_GLU, U_OUT):
            split_hi(u + 2)
            c = 6 + (u - U_GLU) // 2
            if u == U_GLU + 6:
                for k in range(0, 4):
                    turn_hi(1, k, None)
            if (u - U_GLU) % 4 == 1:
                for t in range(TOK):
                    n = TOK * ((c - 6) // 2) + t
                    wait_rows(act, c, t)
                    if n >= 2:
                        act.wait_ge(zt_used, n - 1)
                    nc.scalar.activation(zt[:, n % 2, :], ps[:, t, :], ACT.Tanh, scale=0.5).then_inc(nat_copied, 1)

        for u in range(U_OUT, U_MLP):
            split_hi(u + 2)
            if u == U_OUT + 1:
                for k in range(4, 8):
                    turn_hi(1, k, None)
            if u == U_OUT + 6:
                for k in range(0, 4):
                    turn_hi(2, k, g2_col)
        for k in range(4, 8):
            turn_hi(2, k, g2_col)

        def half_stats(g, half, t, count, before):
            act.wait_ge(nat_added, count)
            if before:
                act.wait_ge(x_sq, before)
            nc.scalar.activation(junk[:, 0:512], x2[:, t, 512 * half:512 * half + 512], ACT.Square,
                                 accum_out=ms[:, g, half, t:t + 1]).then_inc(x_sq, 1)

        def mlp_split_hi(u, n):
            slot = (n + 2) % RING
            act.wait_ge(raw_in[slot], 4 * (u + n - (n + 2) % 4 + 2) + 16)
            act.wait_ge(unit_used, u + n + 2 - RING + 1)
            nc.scalar.activation(w_hi[:, slot, :], raw[:, slot, :], ACT.Identity).then_inc(w_hi_done, 1)

        def relu_up(e, odd, u, n):
            act.wait_ge(unit_used, u + n + 1)
            if not (isinstance(e, int) and e == 0 and n < 2):
                act.wait_ge(f_sq, FT * e + n - 1)
                act.wait_ge(f_hi_done, FT * e + n - 1)
            nc.scalar.activation(fr[:, n % 2, :], ps[:, B_T + n, :], ACT.Relu).then_inc(f_relu, 1)
            act.wait_ge(f_relu, FT * e + n + 1)
            nc.scalar.activation(fT_hi[:, odd, n, :], fr[:, n % 2, :], ACT.Square).then_inc(f_hi_done, 1)

        for n in range(4):
            mlp_split_hi(U_MLP, n)
            relu_up(0, 0, U_MLP, n)
            for half in range(2):
                half_stats(1, half, n, 4 * TOK, 2 * n + half)
        act.wait_ge(x_sq, 2 * TOK)
        act.wait_ge(ms_sum, 1)
        nc.scalar.activation(ms[:, 1, 1, :], ms[:, 1, 1, :], ACT.Identity, bias=eps_t[:, :],
                             scale=1.0 / D_MODEL).then_inc(x_rt, 1)
        with act.Fori(0, LOOPS) as j:
            for kind, e, odd, u in mlp_steps(2 * j, U_LOOP + PER_LOOP * j):
                for n in range(4):
                    mlp_split_hi(u, n)
                    if kind == "up":
                        relu_up(e, odd, u, n)
        for kind, e, odd, u in MLP_TAIL:
            for n in range(4):
                if u + n + 2 < N_UNITS:
                    mlp_split_hi(u, n)
                if kind == "up":
                    relu_up(e, odd, u, n)
        for t in range(TOK):
            half_stats(2, 0, t, NAT_END - TOK, 2 * TOK + t)
        act.wait_ge(x_sq, 3 * TOK)
        nc.scalar.activation(ms[:, 2, 0, :], ms[:, 2, 0, :], ACT.Identity, bias=eps_t[:, :],
                             scale=1.0 / D_MODEL).then_inc(x_rt, 1)
        nc.scalar.activation(osq[:, 0:1], eps_t[:, :], ACT.Sqrt)

        def scale_out(t):
            act.wait_ge(x_rstd, TOK + t + 1)
            act.wait_ge(gained, t + 1)
            nc.scalar.activation(x2[:, t, 0:512], x2[:, t, 0:512], ACT.Identity,
                                 scale=rstd[:, 2, t:t + 1]).then_inc(out_ready, 1)

        for t in range(TOK):
            half_stats(2, 1, t, NAT_END - TOK + t + 1, 3 * TOK + t)
            if t:
                scale_out(t - 1)
            act.wait_ge(x_sq, 3 * TOK + t + 1)
            act.wait_ge(x_rt, TOK + 2)
            nc.scalar.activation(ms[:, 2, 1, t:t + 1], ms[:, 2, 1, t:t + 1], ACT.Sqrt,
                                 bias=ms[:, 2, 0, t:t + 1], scale=1.0 / D_MODEL).then_inc(x_rt, 1)
        scale_out(TOK - 1)

    @block.vector
    def _(dve):
        steps = [0]

        def link(ins):
            steps[0] += 1
            ins.then_inc(prep, 1)

        def settle():
            dve.wait_ge(prep, steps[0])

        TT, TS, STT = nc.vector.tensor_tensor, nc.vector.tensor_scalar, nc.vector.scalar_tensor_tensor

        def turn_lo(g, k, gain):
            dve.wait_ge(hT_hi_done, KT * g + k + 1)
            src, hi = ps[:, turn_bank(g, k), :], hT_hi[:, k, :].bitcast(F32)
            if gain is None:
                ins = TT(hT_lo[:, k, :], src, hi, ALU.subtract)
            else:
                ins = STT(out=hT_lo[:, k, :], in0=src, scalar=gain[:, k:k + 1], in1=hi,
                          op0=ALU.mult, op1=ALU.subtract)
            ins.then_inc(hT_lo_done, 1)

        for t in range(TOK):
            dve.wait_ge(x_rt, t + 1)
            nc.vector.reciprocal(rstd[:, 0, t:t + 1], ms[:, 0, 1, t:t + 1]).then_inc(x_rstd, 1)
            dve.wait_ge(x_rstd, t + 1)
            TS(mixA[:, t, :], mixA[:, t, :], rstd[:, 0, t:t + 1], None, ALU.mult).then_inc(x_scaled, 1)
        dve.wait_ge(cols_copied, 1)
        for k in range(KT):
            turn_lo(0, k, g1_col)

        def prow(i):
            return prm[:, i, :]

        A_RE, A_IM, A_DT, TH, MAG, COS, SIN, TURNS, RED, ABS, LR, LI, DEN, T0, T1, CR, CI = range(17)
        dt_b = dtt[:, 1, :].unsqueeze(2).to_broadcast([PAIRS, 2, SSM_STATE])

        def by_group(i):
            return prow(i).rearrange("i (two s) -> i two s", two=2)

        dve.wait_ge(prep_act, 1)
        TT(by_group(A_DT), by_group(A_RE), dt_b, ALU.mult).then_inc(args_ready, 1)
        link(TT(by_group(TH), by_group(A_IM), dt_b, ALU.mult))
        settle()
        dve.wait_ge(consts_in, 16 * N_CONST)
        for j in range(2):
            link(TT(lamv[:, j, 0, :], lamv[:, j, 0, :], lamv[:, j, 1, :], ALU.mult))
        settle()
        for j in range(2):
            nc.vector.tensor_reduce(nlam[:, j:j + 1], lamv[:, j, 0, :], mybir.AxisListType.X,
                                    ALU.add).then_inc(lam_dots, 1)
        link(TS(gsub[:, :], gsub[:, :], (1.0 - LAM_INIT) * 0.5, None, ALU.mult))

        BIG = 1.5 * 2.0 ** 23
        C1 = 6.28125
        C2 = float(np.float32(np.round((2 * math.pi - C1) * 2.0 ** 20) / 2.0 ** 20))
        C3 = float(np.float32(2 * math.pi - C1 - C2))
        link(TS(prow(TURNS), prow(TH), 1.0 / (2 * math.pi), BIG, ALU.mult, ALU.add))
        settle()
        link(TS(prow(TURNS), prow(TURNS), -BIG, None, ALU.add))
        settle()
        link(STT(out=prow(RED), in0=prow(TURNS), scalar=-C1, in1=prow(TH), op0=ALU.mult, op1=ALU.add))
        settle()
        link(STT(out=prow(RED), in0=prow(TURNS), scalar=-C2, in1=prow(RED), op0=ALU.mult, op1=ALU.add))
        settle()
        link(STT(out=prow(RED), in0=prow(TURNS), scalar=-C3, in1=prow(RED), op0=ALU.mult, op1=ALU.add))
        settle()
        TS(prow(RED), prow(RED), 3.1415925, -3.1415925, ALU.min, ALU.max).then_inc(args_ready, 1)
        dve.wait_ge(args_ready, 2)
        STT(out=prow(ABS), in0=prow(RED), scalar=-1.0, in1=prow(RED), op0=ALU.mult,
            op1=ALU.max).then_inc(args_ready, 1)
        link(TT(prow(T0), prow(A_RE), prow(A_RE), ALU.mult))
        link(TT(prow(T1), prow(A_IM), prow(A_IM), ALU.mult))
        settle()
        link(TT(prow(DEN), prow(T0), prow(T1), ALU.add))
        settle()
        link(nc.vector.reciprocal(prow(DEN), prow(DEN)))
        dve.wait_ge(prep_act, 5)
        link(TT(prow(LR), prow(MAG), prow(COS), ALU.mult))
        link(TT(prow(LI), prow(MAG), prow(SIN), ALU.mult))
        settle()
        link(TS(prow(LR), prow(LR), -1.0, None, ALU.add))
        settle()
        link(TT(prow(T0), prow(LR), prow(A_RE), ALU.mult))
        link(TT(prow(T1), prow(LI), prow(A_IM), ALU.mult))
        settle()
        link(TT(prow(CR), prow(T0), prow(T1), ALU.add))
        settle()
        link(TT(prow(T0), prow(LI), prow(A_RE), ALU.mult))
        link(TT(prow(T1), prow(LR), prow(A_IM), ALU.mult))
        settle()
        link(TT(prow(CI), prow(T0), prow(T1), ALU.subtract))
        link(TT(prow(CR), prow(CR), prow(DEN), ALU.mult))
        settle()
        link(TT(prow(CI), prow(CI), prow(DEN), ALU.mult))
        settle()
        nc.vector.sem_inc(prm_ready, 1)
        dve.wait_ge(prm_turned, 1)
        nc.vector.tensor_copy(mag[:, :, :].rearrange("p a i -> p (a i)"), ps[:, 4, 0:5 * PAIRS]).then_inc(prm_copied, 1)
        dve.wait_ge(prm_copied, 1)

        dve.wait_ge(frow_mm, 1)
        TS(frow[:, 0:512], ps[0:N_HEADS, 5, :], 1.0, None, ALU.mult).then_inc(frow_out, 1)
        TS(frow[:, 512:BIAS_W], ps[0:N_HEADS, 6, 0:BIAS_W - 512], 0.0, MASKED, ALU.mult, ALU.add).then_inc(frow_out, 1)

        link(TT(nlam[:, 0:1], nlam[:, 3:4], nlam[:, 2:3], ALU.subtract))
        settle()
        link(TS(nlam[:, 0:1], nlam[:, 0:1], -LAM_INIT, None, ALU.add))

        def coef_b(half):
            cr = coef[:, half, 0, :].unsqueeze(2).to_broadcast([P, PAIRS, SSM_GROUP])
            ci = coef[:, half, 1, :].unsqueeze(2).to_broadcast([P, PAIRS, SSM_GROUP])
            if half:
                dve.wait_ge(bb_turned, 2)
            else:
                dve.wait_ge(tiles_set, 3)
            link(TT(bt[:, 0, :, :], b_nat[:, 0, :, :], cr, ALU.mult))
            link(TT(bt[:, 1, :, :], b_nat[:, 1, :, :], ci, ALU.mult))
            link(TT(bt[:, 2, :, :], b_nat[:, 1, :, :], cr, ALU.mult))
            link(TT(bt[:, 3, :, :], b_nat[:, 0, :, :], ci, ALU.mult))
            settle()
            for ri in range(2):
                for g2 in range(2):
                    rows, cols = slice(64 * g2, 64 * g2 + 64), slice(16 * g2, 16 * g2 + 16)
                    TT(bb[rows, ri, :, cols], bt[rows, 2 * ri, :, :], bt[rows, 2 * ri + 1, :, :],
                       (ALU.subtract, ALU.add)[ri]).then_inc(bb_ready, 1)

        link(nc.vector.tensor_copy(coef[:, 0, :, :], mag[:, 3:5, :]))
        link(nc.vector.tensor_copy(pw[:, 0, :, :], mag[:, 1:3, :]))
        settle()
        coef_b(0)

        dve.wait_ge(tiles_set, 6)
        dve.wait_ge(turned, KT)
        levels = HALF.bit_length() - 1
        for lv in range(levels):
            n = 1 << lv
            p_re, p_im = pw[:, lv % 2, 0, :], pw[:, lv % 2, 1, :]
            q_re, q_im = pw[:, (lv + 1) % 2, 0, :], pw[:, (lv + 1) % 2, 1, :]
            pr = p_re.unsqueeze(2).to_broadcast([P, PAIRS, n])
            pi = p_im.unsqueeze(2).to_broadcast([P, PAIRS, n])
            a, b = em[:, 0, :, 0:n], em[:, 1, :, 0:n]
            link(TT(a, E_re[:, :, 0:n], pr, ALU.mult))
            link(TT(b, E_im[:, :, 0:n], pi, ALU.mult))
            link(TT(pwt[:, 0, :], p_re, p_re, ALU.mult))
            link(TT(pwt[:, 1, :], p_im, p_im, ALU.mult))
            link(STT(out=q_im, in0=p_re, scalar=2.0, in1=p_im, op0=ALU.mult, op1=ALU.mult))
            settle()
            link(TT(E_re[:, :, n:2 * n], a, b, ALU.subtract))
            link(TT(q_re, pwt[:, 0, :], pwt[:, 1, :], ALU.subtract))
            settle()
            link(TT(a, E_re[:, :, 0:n], pi, ALU.mult))
            link(TT(b, E_im[:, :, 0:n], pr, ALU.mult))
            settle()
            link(TT(E_im[:, :, n:2 * n], a, b, ALU.add))
            settle()
        p_re, p_im = pw[:, levels % 2, 0, :], pw[:, levels % 2, 1, :]
        c_re, c_im = coef[:, 0, 0, :], coef[:, 0, 1, :]
        link(TT(pwt[:, 0, :], c_re, p_re, ALU.mult))
        link(TT(pwt[:, 1, :], c_im, p_im, ALU.mult))
        link(TT(pwt[:, 2, :], c_im, p_re, ALU.mult))
        link(TT(pwt[:, 3, :], c_re, p_im, ALU.mult))
        settle()
        link(TT(coef[:, 1, 0, :], pwt[:, 0, :], pwt[:, 1, :], ALU.add))
        link(TT(coef[:, 1, 1, :], pwt[:, 2, :], pwt[:, 3, :], ALU.subtract))
        settle()
        coef_b(1)
        dve.wait_ge(c_packed, 4)
        pr = p_re.unsqueeze(2).to_broadcast([P, PAIRS, SSM_GROUP])
        pi = p_im.unsqueeze(2).to_broadcast([P, PAIRS, SSM_GROUP])
        dve.wait_ge(bb_ready, 8)
        settle()
        link(TT(bt[:, 0, :, :], c_pk[:, 0, :, :], pr, ALU.mult))
        link(TT(bt[:, 1, :, :], c_pk[:, 1, :, :], pi, ALU.mult))
        link(TT(bt[:, 2, :, :], c_pk[:, 0, :, :], pi, ALU.mult))
        link(TT(bt[:, 3, :, :], c_pk[:, 1, :, :], pr, ALU.mult))
        settle()
        for g2 in range(2):
            rows, cols = slice(64 * g2, 64 * g2 + 64), slice(16 * g2, 16 * g2 + 16)
            link(TS(CT[rows, :, 0, 0, cols], c_pk[rows, 0, :, :], 1.0, None, ALU.mult))
            link(TS(CT[rows, :, 0, 1, cols], c_pk[rows, 1, :, :], -1.0, None, ALU.mult))
            link(TT(CT[rows, :, 1, 0, cols], bt[rows, 0, :, :], bt[rows, 1, :, :], ALU.subtract))
            link(STT(out=CT[rows, :, 1, 1, cols], in0=bt[rows, 2, :, :], scalar=-1.0, in1=bt[rows, 3, :, :],
                     op0=ALU.mult, op1=ALU.subtract))
        settle()
        nc.vector.sem_inc(table, 1)

        def halves(ap):
            return ap.rearrange("p (c j) -> p c j", c=2)

        def ssm_part(i, part):
            def done(k):
                dve.wait_ge(ssm_step, STEPS * i + k)

            er = E_re[:, i:i + 1, :].to_broadcast([P, 2, HALF])
            ei = E_im[:, i:i + 1, :].to_broadcast([P, 2, HALF])
            t = [halves(rt[:, k, :]) for k in range(4)]
            s = [halves(st[:, k, :]) for k in range(2)]
            if part == 0:
                dve.wait_ge(bu_ready, i + 1)
                done(0)
                if i:
                    dve.wait_ge(states_done, 2 * i)
                b_re, b_im = halves(ps[:, B_BU, :]), halves(ps[:, B_BU + 1, :])
                TT(t[0], b_re, er, ALU.mult).then_inc(ssm_step, 1)
                TT(t[1], b_im, ei, ALU.mult).then_inc(ssm_step, 1)
                TT(t[2], b_im, er, ALU.mult).then_inc(ssm_step, 1)
                TT(t[3], b_re, ei, ALU.mult).then_inc(ssm_step, 1)
            elif part == 1:
                done(2)
                TT(t[0], t[0], t[1], ALU.add).then_inc(ssm_step, 1)
                done(4)
                TT(t[2], t[2], t[3], ALU.subtract).then_inc(ssm_step, 1)
                decay = mag[:, 0, i:i + 1].to_broadcast([P, SEQ])
                for k in range(2):
                    done(5 + k)
                    nc.vector.tensor_tensor_scan(rt[:, 2 * k + 1, :], decay, rt[:, 2 * k, :], 0.0,
                                                 ALU.mult, ALU.add).then_inc(ssm_step, 1)
            else:
                if i:
                    dve.wait_ge(y_ready, i)
                done(7)
                TT(t[0], t[1], er, ALU.mult).then_inc(ssm_step, 1)
                TT(s[1], t[1], ei, ALU.mult).then_inc(ssm_step, 1)
                done(8)
                TT(t[2], t[3], ei, ALU.mult).then_inc(ssm_step, 1)
                TT(t[3], t[3], er, ALU.mult).then_inc(ssm_step, 1)

        def y_skip(ut):
            dve.wait_ge(y_ready, 4 * ut + 4)
            STT(out=uT[:, ut, :], in0=uT[:, ut, :], scalar=d_col[:, ut:ut + 1], in1=ps[:, B_Y, :],
                op0=ALU.mult, op1=ALU.add).then_inc(y_done, 1)

        def gate_a(c):
            for t in range(TOK):
                dve.wait_ge(nat_copied, TOK * (2 + c) + t + 1)
                g = mixA[:, t, 512 * c:512 * c + 512].rearrange("p (h v) -> p h v", v=V_DIM)
                STT(out=g, in0=g, scalar=1.0, in1=gsub[:, :].unsqueeze(1).to_broadcast([P, 4, V_DIM]),
                    op0=ALU.add, op1=ALU.mult).then_inc(gates_done, 1)

        for i in range(FIRST_D):
            for part in range(3):
                ssm_part(i, part)
            add_states(i, dve, TT)
            if i % 2:
                gate_a(i // 2)

        def pre(n):
            h, i = n // TOK, n % TOK
            L = P * (i + 1)
            dve.wait_ge(score_ready, n + 1)
            dve.wait_ge(bias_in[h % 2], 16 * (h // 2 + 1))
            if n >= 2:
                dve.wait_ge(wT_ready, n - 1)
            for m in range(2):
                nc.vector.tensor_tensor_reduce(
                    out=Pm[:, n % 2, m, 0:L], in0=ps[:, B_SCORE + m, 0:L],
                    in1=bias[:, h % 2, SEQ - L:SEQ], scale=1.0, scalar=-3e38,
                    op0=ALU.add, op1=ALU.max, accum_out=mx[:, n % 2, m:m + 1]).then_inc(score_read, 1)
            dve.wait_ge(score_read, 2 * n + 2)
            TS(nmx[:, n % 2, :], mx[:, n % 2, :], -1.0, None, ALU.mult).then_inc(nmax_ready, 1)

        def post(n):
            L = P * (n % TOK + 1)
            dve.wait_ge(exp_done, 2 * n + 2)
            nc.vector.reciprocal(rinv[:, n % 8, :], sums[:, n % 2, :]).then_inc(att_step, 1)
            dve.wait_ge(att_step, 3 * n + 1)
            STT(out=cfac[:, n % 2, :], in0=rinv[:, n % 8, 1:2], scalar=sums[:, n % 2, 0:1], in1=nlam[:, 0:1],
                op0=ALU.mult, op1=ALU.mult).then_inc(att_step, 1)
            dve.wait_ge(att_step, 3 * n + 2)
            STT(out=Pm[:, n % 2, 0, 0:L], in0=Pm[:, n % 2, 1, 0:L], scalar=cfac[:, n % 2, :],
                in1=Pm[:, n % 2, 0, 0:L], op0=ALU.mult, op1=ALU.add).then_inc(att_step, 1)

        def gate_o(h):
            dve.wait_ge(o_squared, TOK * (h + 1))
            for i in range(TOK):
                n = TOK * h + i
                g = mixA[:, i, V_DIM * h:V_DIM * h + V_DIM]
                STT(out=g, in0=ps[:, B_O, P * i:P * i + P], scalar=rinv[:, n % 8, 0:1], in1=g,
                    op0=ALU.mult, op1=ALU.mult).then_inc(o_gated, 1)

        dve.wait_ge(gates_done, 2 * TOK)
        for n in range(BLOCKS + 2):
            h, i = n // TOK, n % TOK
            if n < BLOCKS:
                pre(n)
                for pair, part in slot_parts(n):
                    ssm_part(pair, part)
                    if part == 2 and pair == PAIRS - 1:
                        add_states(pair, dve, TT)
                    if part == 2 and pair % 4 == 0:
                        y_skip(pair // 4 - 1)
                post(n)
            if i == 1 and h >= 1:
                gate_o(h - 1)

        def gate_s(c):
            for t in range(TOK):
                dve.wait_ge(nat_copied, TOK * (4 + c) + t + 1)
                g = mixS[:, t, 512 * c:512 * c + 512]
                TS(g, g, 0.25, 0.25, ALU.mult, ALU.add).then_inc(gates_done, 1)

        y_skip(UT - 1)
        gate_s(0)
        for k in range(UT):
            dve.wait_ge(gT_hi_done, k + 1)
            TT(gT_lo[:, k, :], uT[:, k, :], gT_hi[:, k, :].bitcast(F32), ALU.subtract).then_inc(gT_lo_done, 1)
        gate_s(1)

        for half in range(2):
            cols = slice(512 * half, 512 * half + 512)
            for t in range(TOK):
                n = TOK * half + t
                dve.wait_ge(nat_copied, TOK * (6 + half) + t + 1)
                dve.wait_ge(gates_done, 4 * TOK)
                STT(out=mixS[:, t, cols], in0=zt[:, n % 2, :], scalar=1.0, in1=mixS[:, t, cols],
                    op0=ALU.add, op1=ALU.mult).then_inc(zt_used, 1)
            if half:
                for k in range(0, 4):
                    turn_lo(1, k, None)
            else:
                dve.wait_ge(rsub_step, 1)
                nc.vector.reciprocal(rsub[:, :, :], ssq[:, :, :]).then_inc(rsub_step, 1)
            for t in range(TOK):
                wait_rows(dve, 7 + 2 * half, t)
                dve.wait_ge(zt_used, TOK * half + t + 1)
                TT(mixS[:, t, cols], ps[:, t, :], mixS[:, t, cols], ALU.mult).then_inc(nat_added, 1)
            dve.wait_ge(rsub_step, 2)
            dve.wait_ge(o_gated, BLOCKS)
            for t in range(TOK):
                dve.wait_ge(nat_added, TOK * half + t + 1)
                for h in range(4 * half, 4 * half + 4):
                    hc = slice(V_DIM * h, V_DIM * h + V_DIM)
                    STT(out=mixA[:, t, hc], in0=mixA[:, t, hc], scalar=rsub[:, t, h:h + 1], in1=mixS[:, t, hc],
                        op0=ALU.mult, op1=ALU.add).then_inc(mixed_done, 1)
        for k in range(4, 8):
            turn_lo(1, k, None)

        dve.wait_ge(x_again, 16 * TOK)

        def add_chunk(c, index):
            for t in range(TOK):
                wait_rows(dve, c, t)
                cols = slice(512 * (c % 2), 512 * (c % 2) + 512)
                TT(x2[:, t, cols], x2[:, t, cols], ps[:, t, :], ALU.add).then_inc(nat_added, 1)

        add_chunk(10, 2)
        for k in range(0, 4):
            turn_lo(2, k, g2_col)
        add_chunk(11, 3)
        for k in range(4, 8):
            turn_lo(2, k, g2_col)

        def square_up(e, odd):
            for n in range(FT):
                dve.wait_ge(f_relu, FT * e + n + 1)
                if not (isinstance(e, int) and e == 0 and n < 2):
                    dve.wait_ge(f_lo_done, FT * e + n - 1)
                TT(fs[:, n % 2, :], fr[:, n % 2, :], fr[:, n % 2, :], ALU.mult).then_inc(f_sq, 1)
                dve.wait_ge(f_sq, FT * e + n + 1)
                dve.wait_ge(f_hi_done, FT * e + n + 1)
                TT(fT_lo[:, odd, n, :], fs[:, n % 2, :], fT_hi[:, odd, n, :].bitcast(F32),
                   ALU.subtract).then_inc(f_lo_done, 1)

        def add_down(e, half, u, t):
            wait_mlp_rows(dve, e, half, u, t)
            dve.wait_ge(nat_added, 2 * TOK * e + TOK * (2 + half) + t + 1)
            cols = slice(512 * half, 512 * half + 512)
            STT(out=x2[:, t, cols], in0=ps[:, t, :], scalar=rstd2[:, t:t + 1], in1=x2[:, t, cols],
                op0=ALU.mult, op1=ALU.add).then_inc(nat_added, 1)

        square_up(0, 0)
        dve.wait_ge(x_sq, 2 * TOK)
        TT(ms[:, 1, 1, :], ms[:, 1, 0, :], ms[:, 1, 1, :], ALU.add).then_inc(ms_sum, 1)
        dve.wait_ge(x_rt, TOK + 1)
        nc.vector.reciprocal(rstd2[:, :], ms[:, 1, 1, :]).then_inc(scale_ready, 1)
        dve.wait_ge(scale_ready, 1)
        with dve.Fori(0, LOOPS) as j:
            for kind, e, odd, u in mlp_steps(2 * j, U_LOOP + PER_LOOP * j):
                if kind == "up":
                    square_up(e, odd)
                else:
                    for half in range(2):
                        for t in range(TOK):
                            add_down(e, half, u, t)
        for kind, e, odd, u in MLP_TAIL:
            if kind == "up":
                square_up(e, odd)
            elif e < EIGHTHS - 1:
                for half in range(2):
                    for t in range(TOK):
                        add_down(e, half, u, t)
        for t in range(TOK):
            add_down(EIGHTHS - 1, 0, U_TAIL + 8, t)
        dve.wait_ge(gfin_in, 16)
        dve.wait_ge(x_sq, 3 * TOK)
        for t in range(TOK):
            dve.wait_ge(nat_added, NAT_END - TOK)
            TT(x2[:, t, 0:512], x2[:, t, 0:512], gfin[:, 0:512], ALU.mult).then_inc(gained, 1)

        def norm_out(t):
            dve.wait_ge(x_rt, TOK + 2 + t + 1)
            nc.vector.reciprocal(rstd[:, 2, t:t + 1], ms[:, 2, 1, t:t + 1]).then_inc(x_rstd, 1)
            dve.wait_ge(x_rstd, TOK + t + 1)
            if t < TOK - 1:
                dve.wait_ge(rows_gained, t + 1)
            else:
                dve.wait_ge(last_gained, 1)
            TS(x2[:, t, 512:1024], xg[:, t, :], rstd[:, 2, t:t + 1], None, ALU.mult).then_inc(out_ready_hi, 1)

        for t in range(TOK):
            add_down(EIGHTHS - 1, 1, U_TAIL + 8, t)
            if t == TOK - 1:
                gain_rows(dve, TT, t, last_gained)
            if t:
                norm_out(t - 1)
        norm_out(TOK - 1)

    @block.tensor
    def _(pe):
        def mm3(dst, a_hi, a_lo, b_hi, b_lo, start, stop):
            nc.tensor.matmul(dst, a_hi, b_hi, start=start, stop=False)
            nc.tensor.matmul(dst, a_hi, b_lo, start=False, stop=False)
            return nc.tensor.matmul(dst, a_lo, b_hi, start=False, stop=stop)

        def col_mm(u, bank, ks):
            for k in ks:
                if u == U_SSM:
                    pe.wait_ge(hT_lo_done, k + 1)
                c = slice(P * k, P * k + P)
                mm = mm3(ps[:, bank, :], w_hi[:, u % RING, c], w_lo[:, u % RING, c],
                         hT_hi[:, k, :], hT_lo[:, k, :], k == 0, k == KT - 1)
            return mm

        def row_unit_mm(u, c, r, n_rows, hi, lo, ready, per_row, tiles=range(TOK)):
            if 0 in tiles:
                pe.wait_ge(w_lo_done, u + 1)
            for t in tiles:
                if r == 0:
                    nat_free(c, t)
                for k2 in range(2):
                    k = 2 * r + k2
                    if t == 0 and ready is not None:
                        pe.wait_ge(ready, per_row + k + 1)
                    wc = slice(512 * k2, 512 * k2 + 512)
                    tc_ = slice(P * t, P * t + P)
                    mm = mm3(ps[:, t, :], hi[:, k, tc_], lo[:, k, tc_], w_hi[:, u % RING, wc],
                             w_lo[:, u % RING, wc], r == 0 and k2 == 0, r == n_rows - 1 and k2 == 1)
                if r == n_rows - 1 and t < TOK - 1:
                    mm.then_inc(nat_ready, 1)
            if TOK - 1 in tiles:
                unit_done(mm)

        def unit_done(mm):
            mm.then_inc(unit_used, 1)

        COPIED = {0: 0, 1: 1, 2: 2, 3: 3, 4: 4, 5: 5, 6: 6, 8: 7}
        ADDED = {7: 0, 9: 1, 10: 2, 11: 3}

        def nat_free(c, t):
            if c == 0:
                pe.wait_ge(hT_lo_done, KT)
            elif c == 4:
                if t == 0:
                    pe.wait_ge(qk_copied, 2 * N_HEADS)
                else:
                    pe.wait_ge(nat_copied, TOK * c + t)
            elif c == 5:
                if t < B_WT:
                    pe.wait_ge(score_read, 2 * BLOCKS)
                elif t == B_WT:
                    pe.wait_ge(wT_copied, BLOCKS)
                else:
                    pe.wait_ge(o_gated, BLOCKS)
            elif c - 1 in COPIED:
                pe.wait_ge(nat_copied, TOK * COPIED[c - 1] + t + 1)
            else:
                pe.wait_ge(nat_added, TOK * ADDED[c - 1] + t + 1)

        def turn(g, ks, src, ready, count):
            pe.wait_ge(ready, count)
            for k in ks:
                if k >= 4:
                    pe.wait_ge(hT_lo_done, KT * g + k - 3)
                elif g == 1:
                    pe.wait_ge(qk_copied, 2 * N_HEADS)
                    pe.wait_ge(nat_copied, 5 * TOK)
                    pe.wait_ge(y_done, UT)
                elif g == 2:
                    pe.wait_ge(hT_lo_done, 2 * KT)
                for t in range(TOK):
                    mm = nc.tensor.transpose(ps[:, turn_bank(g, k), P * t:P * t + P], src[:, t, P * k:P * k + P],
                                             ident[:, :])
                mm.then_inc(turned, 1)

        def drive(i):
            j, ut = i % 4, i // 4
            rows = slice(32 * j, 32 * j + 32)
            pe.wait_ge(BT_ready, 4)
            pe.wait_ge(u_copied, ut + 1)
            if i:
                pe.wait_ge(ssm_step, STEPS * (i - 1) + 4)
            for c in range(2):
                for ri in range(2):
                    mm = nc.tensor.matmul(ps[:, B_BU + ri, HALF * c:HALF * c + HALF], BT[rows, c, ri, ut, :],
                                          uT[rows, ut, HALF * c:HALF * c + HALF], start=True, stop=True)
            mm.then_inc(bu_ready, 1)

        def readout(i):
            j, ut = i % 4, i // 4
            pe.wait_ge(states_done, 2 * i + 2)
            if j == 0 and ut:
                pe.wait_ge(y_done, ut)
            if i == 0:
                pe.wait_ge(table, 1)
            for c in range(2):
                for ri in range(2):
                    mm = nc.tensor.matmul(ps[32 * j:32 * j + 32, B_Y, HALF * c:HALF * c + HALF],
                                          CT[:, i, c, ri, :], st[:, ri, HALF * c:HALF * c + HALF],
                                          start=(ri == 0), stop=(ri == 1), tile_position=(0, 32 * j))
            mm.then_inc(y_ready, 1)

        def turn_x(t, k):
            return nc.tensor.transpose(ps[:, turn_bank(0, k), P * t:P * t + P], mixA[:, t, P * k:P * k + P],
                                       ident[:, :])

        pe.wait_ge(ident_set, 2)
        for t in range(TOK):
            pe.wait_ge(x_scaled, t + 1)
            for k in range(KT - 1):
                mm = turn_x(t, k)
                if t == TOK - 1:
                    mm.then_inc(turned, 1)
            if t == 0:
                pe.wait_ge(cols_in, 16 * N_COLS)
                nc.tensor.transpose(ps[:, turn_bank(0, KT - 1), 0:2 * KT + UT], cols_nat[:, :],
                                    ident[0:2 * KT + UT, 0:2 * KT + UT]).then_inc(cols_turned, 1)
        pe.wait_ge(cols_copied, 1)
        for t in range(TOK):
            mm = turn_x(t, KT - 1)
        mm.then_inc(turned, 1)

        for u in range(U_SSM, U_V):
            pe.wait_ge(w_lo_done, u + 1)
            unit_done(col_mm(u, 4 + u, range(KT)))
        pe.wait_ge(prm_ready, 1)
        pe.wait_ge(u_copied, 1)
        for n, row in enumerate((4, 5, 6, 15, 16)):
            mm = nc.tensor.transpose(ps[:, 4, PAIRS * n:PAIRS * n + PAIRS], prm[:, row, :],
                                     ident[0:PAIRS, 0:PAIRS])
        mm.then_inc(prm_turned, 1)
        pe.wait_ge(consts_in, 16 * N_CONST)
        pe.wait_ge(u_copied, 3)
        nc.tensor.matmul(ps[0:N_HEADS, 5, :], rb[:, :], oneh[:, 0:512], start=True, stop=True)
        nc.tensor.matmul(ps[0:N_HEADS, 6, 0:BIAS_W - 512], rb[:, :], oneh[:, 512:BIAS_W], start=True,
                         stop=True).then_inc(frow_mm, 1)

        def turn_c():
            for ri in range(2):
                if ri == 0:
                    pe.wait_ge(prm_copied, 1)
                else:
                    pe.wait_ge(frow_out, 2)
                for ut in range(UT):
                    mm = nc.tensor.transpose(ps[:, 4 + ri, P * ut:P * ut + P],
                                             c_nat[:, ri, ut, :, :].rearrange("p a s -> p (a s)"), ident[:, :])
                mm.then_inc(c_turned, 1)

        def turn_bb(half):
            for ri in range(2):
                pe.wait_ge(bb_ready, 4 * half + 2 * ri + 2)
                if half:
                    pe.wait_ge(BT_ready, ri + 1)
                else:
                    pe.wait_ge(frow_out, 2)
                    pe.wait_ge(u_copied, UT)
                for ut in range(UT):
                    mm = nc.tensor.transpose(ps[:, 6 + ri, P * ut:P * ut + P],
                                             bb[:, ri, 4 * ut:4 * ut + 4, :].rearrange("p a h -> p (a h)"),
                                             ident[:, :])
                mm.then_inc(bb_turned, 1)

        for u in range(U_V, U_GA):
            r = (u - U_V) % 4
            row_unit_mm(u, (u - U_V) // 4, r, 4, hT_hi, hT_lo, None, 0)
            if u == U_V + 3:
                turn_c()
                turn_bb(0)
        for u in range(U_GA, U_QK):
            n = u - U_GA
            if n == 0:
                turn_bb(1)
                drive(0)
            row_unit_mm(u, 2 + n // 4, n % 4, 4, hT_hi, hT_lo, None, 0)
            if n % 2 == 0:
                drive(n // 2 + 1)
            else:
                readout(n // 2)

        def qk_part(v, part):
            u = U_QK + v
            if part == 0:
                pe.wait_ge(w_lo_done, u + 1)
                if v == 1:
                    pe.wait_ge(nat_copied, 3 * TOK + 1)
                elif v:
                    pe.wait_ge(qk_copied, 1 if v == 2 else v)
                else:
                    pe.wait_ge(c_packed, 4)
            mm = col_mm(u, qk_bank(v), range(4 * part, 4 * part + 4))
            if part:
                unit_done(mm)

        for v in range(2):
            qk_part(v, 0)
            qk_part(v, 1)

        def scores(n):
            h, i = n // TOK, n % TOK
            L = P * (i + 1)
            pe.wait_ge(qk_copied, 2 * h + 2)
            if n == 0:
                pe.wait_ge(nat_copied, 4 * TOK)
            else:
                pe.wait_ge(score_read, 2 * n)
            for m in range(2):
                rows = slice(HEAD_DIM * m, HEAD_DIM * m + HEAD_DIM)
                mm = nc.tensor.matmul(ps[:, B_SCORE + m, 0:L], qT[rows, h % 2, P * i:P * i + P],
                                      kT[rows, h % 2, 0:L], start=True, stop=True)
            mm.then_inc(score_ready, 1)

        def turn_w(n):
            pe.wait_ge(att_step, 3 * n + 3)
            if n:
                pe.wait_ge(wT_copied, n)
            for j in range(n % TOK + 1):
                mm = nc.tensor.transpose(ps[:, B_WT, P * j:P * j + P], Pm[:, n % 2, 0, P * j:P * j + P],
                                         ident[:, :])
            mm.then_inc(wT_ready, 1)

        def pv(n):
            h, i = n // TOK, n % TOK
            pe.wait_ge(wT_copied, n + 1)
            if i == 0 and h:
                pe.wait_ge(o_gated, TOK * h)
            for j in range(i + 1):
                mm = nc.tensor.matmul(ps[:, B_O, P * i:P * i + P], wT[:, n % 2, P * j:P * j + P],
                                      V[:, j, V_DIM * h:V_DIM * h + V_DIM], start=(j == 0), stop=(j == i))
            mm.then_inc(pv_done, 1)

        def gate_tile(t):
            nat_free(4, t)
            for r in range(4):
                u = U_GS + r
                pe.wait_ge(w_lo_done, u + 1)
                for k2 in range(2):
                    k = 2 * r + k2
                    tc_, wc = slice(P * t, P * t + P), slice(512 * k2, 512 * k2 + 512)
                    mm = mm3(ps[:, B_QK, :], hT_hi[:, k, tc_], hT_lo[:, k, tc_], w_hi[:, u % RING, wc],
                             w_lo[:, u % RING, wc], k == 0, k == KT - 1)
                if t == TOK - 1:
                    unit_done(mm)
            if t < TOK - 1:
                mm.then_inc(nat_ready, 1)

        def fill_ssm(n):
            for i, part in slot_parts(n):
                if part == 0 and i + 1 < PAIRS:
                    drive(i + 1)
                if part == 2:
                    readout(i)

        for n in range(BLOCKS + 2):
            h, i = n // TOK, n % TOK
            if n >= BLOCKS:
                row_unit_mm(U_GS + 4, 5, 0, 4, hT_hi, hT_lo, None, 0, range(n - BLOCKS, n - BLOCKS + 1))
            if n >= 2 and (i == 0 or n >= BLOCKS):
                pv(n - 2)
            if n < BLOCKS:
                scores(n)
                if n >= 2 and i % 2:
                    pv(n - 2)
                if h < N_HEADS - 1:
                    qk_part(2 * (h + 1) + i // 2, i % 2)
                else:
                    gate_tile(i)
                if n >= 2 and i == 2:
                    pv(n - 2)
            if 1 <= n <= BLOCKS:
                turn_w(n - 1)
                fill_ssm(n - 1)

        for u in range(U_GS + 4, U_GLU):
            row_unit_mm(u, 5, u - U_GS - 4, 4, hT_hi, hT_lo, None, 0, range(2, TOK) if u == U_GS + 4 else range(TOK))
        for u in range(U_GLU, U_OUT):
            n = u - U_GLU
            row_unit_mm(u, 6 + n // 2, n % 2, 2, gT_hi, gT_lo, gT_lo_done, 0)
            if n == 5:
                turn(1, range(0, 4), mixA, mixed_done, 16)
        for u in range(U_OUT, U_MLP):
            n = u - U_OUT
            if n == 1:
                turn(1, range(4, 8), mixA, mixed_done, 32)
            row_unit_mm(u, 10 + n // 4, n % 4, 4, hT_hi, hT_lo, hT_lo_done, KT)
            if n == 6:
                turn(2, range(0, 4), x2, nat_added, 3 * TOK)
        def up(e, u):
            first = isinstance(e, int) and e == 0
            for n in range(FT):
                pe.wait_ge(w_lo_done, u + n + 1)
                if first:
                    pe.wait_ge(hT_lo_done, 2 * KT + n + 1)
                else:
                    pe.wait_ge(f_relu, FT * e + n - 3)
                for k in range(KT):
                    if first and n == 0:
                        if k == 4:
                            turn(2, range(4, 8), x2, nat_added, 4 * TOK)
                        pe.wait_ge(hT_lo_done, 2 * KT + k + 1)
                    c = slice(P * k, P * k + P)
                    mm = mm3(ps[:, B_T + n, :], w_hi[:, n, c], w_lo[:, n, c], hT_hi[:, k, :], hT_lo[:, k, :],
                             k == 0, k == KT - 1)
                unit_done(mm)

        def down(e, odd, u):
            for n in range(4):
                half, r = n // 2, n % 2
                pe.wait_ge(w_lo_done, u + n + 1)
                for t in range(TOK):
                    if r == 0:
                        pe.wait_ge(nat_added, 2 * TOK * e + TOK * (3 + half) + t + 1)
                    for k in (2 * r, 2 * r + 1):
                        if t == 0:
                            pe.wait_ge(f_lo_done, FT * e + k + 1)
                        wc, tc_ = slice(512 * (k % 2), 512 * (k % 2) + 512), slice(P * t, P * t + P)
                        mm = mm3(ps[:, t, :], fT_hi[:, odd, k, tc_], fT_lo[:, odd, k, tc_], w_hi[:, n, wc],
                                 w_lo[:, n, wc], k == 0, k == FT - 1)
                    if r == 1 and t < TOK - 1:
                        mm.then_inc(nat_ready, 1)
                unit_done(mm)

        up(0, U_MLP)
        with pe.Fori(0, LOOPS) as j:
            for kind, e, odd, u in mlp_steps(2 * j, U_LOOP + PER_LOOP * j):
                if kind == "up":
                    up(e, u)
                else:
                    down(e, odd, u)
        for kind, e, odd, u in MLP_TAIL:
            if kind == "up":
                up(e, u)
            else:
                down(e, odd, u)

    ctx.close()


_INS = ['x', 'g_mix', 'w_in', 'lambda_q1', 'lambda_k1', 'lambda_q2', 'lambda_k2', 'subln_g', 'rel_bias',
        'ssm_a_re', 'ssm_a_im', 'ssm_log_dt', 'ssm_b_re', 'ssm_b_im', 'ssm_c_re', 'ssm_c_im', 'ssm_d',
        'w_glu', 'w_out', 'g_mlp', 'w1', 'w2', 'g_final']


def kernel(**inputs):
    import concourse.bacc as bacc
    from concourse.bass_utils import run_bass_kernel_spmd

    nc = bacc.Bacc("TRN2", target_bir_lowering=False, num_devices=1)
    arrays, args = {}, []
    given = {name: np.ascontiguousarray(inputs[name]) for name in _INS}
    given["onehot"] = bucket_onehot()
    for name, a in given.items():
        arrays[f"in_{name}"] = a
        ap = nc.dram_tensor(f"in_{name}", a.shape, mybir.dt.from_np(a.dtype), kind="ExternalInput").ap()
        args.append(ap[0] if name in ("w_in", "w_glu", "w_out", "w1", "w2") else ap)
    out = nc.dram_tensor("out", (1, SEQ, D_MODEL), F32, kind="ExternalOutput").ap()
    build(nc, *args, out)
    r = run_bass_kernel_spmd(nc, [arrays], core_ids=[0])
    return r.results[0]["out"]
```
